# Optimizing a Trainium2 kernel written in Bass

```python
import math, functools
import jax, jax.numpy as jnp
from jax import lax
import numpy as np

D_MODEL = 1024
BATCH = 1
SEQ = 128
DEPTH = 2
DEC_BATCH = 1
DEC_SEQ = 512
PAST_LEN = 128

GRID_W = 64
POOL_WINDOWS = (2, 4, 8, 16)
POOL_GROUPS = 4
POOL_GC = 128
POOL_WIDTH = POOL_GROUPS * POOL_GC
NA_HEADS = 8
NA_HEAD_DIM = 64
NA_WIDTH = NA_HEADS * NA_HEAD_DIM
NA_WIN_ROWS = 8
NA_WIN_COLS = 16
MLA_HEADS = 8
MLA_NOPE_DIM = 64
MLA_ROPE_DIM = 32
MLA_V_DIM = 64
MLA_QK_DIM = MLA_NOPE_DIM + MLA_ROPE_DIM
MLA_Q_LORA = 384
MLA_KV_LORA = 256
MLA_WIDTH = MLA_HEADS * MLA_V_DIM
N_BRANCHES = 3
BRANCH_WIDTH = 512
IN_SPLIT_SIZES = (POOL_WIDTH, NA_WIDTH, NA_WIDTH, NA_WIDTH, MLA_Q_LORA, MLA_KV_LORA, MLA_ROPE_DIM, N_BRANCHES * D_MODEL)
IN_COLS = POOL_WIDTH + 3 * NA_WIDTH + MLA_Q_LORA + MLA_KV_LORA + MLA_ROPE_DIM + N_BRANCHES * D_MODEL
N_GROUPS = 4
EXPERTS_PER_GROUP = 4
N_EXPERTS = N_GROUPS * EXPERTS_PER_GROUP
TOP_K = 2
EXPERT_FF = 256
ROPE_BASE = 10000.0
EPS = 1e-6
Q_BLOCK = 128
NEG_INF = -1e30

kernel_name = 'hybrid_diffusion_prefix_step'

def rmsnorm(x, g):
    xf = x.astype(jnp.float32)
    y = xf * lax.rsqrt(jnp.mean(xf * xf, axis=-1, keepdims=True) + EPS)
    return y.astype(x.dtype) * g

def modulation(cvec, w_mod, b_mod):
    m = (jax.nn.silu(cvec) @ w_mod + b_mod)[..., None, :]
    return jnp.split(m, 6, axis=-1)

def ada_norm(x, g, shift, scale):
    return rmsnorm(x, g) * (1.0 + scale) + shift

def heads(t, n, d):
    return t.reshape(t.shape[:-1] + (n, d))

def split_inputs(h, w_in):
    z = h @ w_in
    idx = np.cumsum(IN_SPLIT_SIZES)[:-1].tolist()
    return jnp.split(z, idx, axis=-1)

def axial_rope_tables(T, dtype):
    t = jnp.arange(T)
    n_freq = MLA_ROPE_DIM // 4
    inv = ROPE_BASE ** (-jnp.arange(n_freq, dtype=jnp.float32) / n_freq)
    ang_r = (t // GRID_W).astype(jnp.float32)[:, None] * inv
    ang_c = (t % GRID_W).astype(jnp.float32)[:, None] * inv
    ang = jnp.stack([ang_r, ang_c], axis=1)
    return jnp.cos(ang).astype(dtype), jnp.sin(ang).astype(dtype)

def apply_axial_rope(x, cos, sin):
    B, T, H, _ = x.shape
    xa = x.reshape(B, T, H, 2, 2, MLA_ROPE_DIM // 4)
    x1, x2 = xa[..., 0, :], xa[..., 1, :]
    c = cos[None, :, None]
    s = sin[None, :, None]
    out = jnp.stack([x1 * c - x2 * s, x1 * s + x2 * c], axis=-2)
    return out.reshape(B, T, H, MLA_ROPE_DIM)

def blocked_attention(q, k, v, scale):
    B, T, H, dk = q.shape
    nb = T // Q_BLOCK
    qb = jnp.moveaxis(q.reshape(B, nb, Q_BLOCK, H, dk), 1, 0)

    def one_block(qi):
        s = jnp.einsum('bqhd,bshd->bhqs', qi, k, preferred_element_type=jnp.float32) * scale
        p = jax.nn.softmax(s, axis=-1).astype(v.dtype)
        return jnp.einsum('bhqs,bshd->bqhd', p, v)

    out = lax.map(one_block, qb)
    return jnp.moveaxis(out, 0, 1).reshape(B, T, H, v.shape[-1])

def pool_mixer(u, w_pool, pool_scale):
    B, T, _ = u.shape
    uf = u.astype(jnp.float32)
    cs = jnp.concatenate([jnp.zeros((B, 1, POOL_WIDTH), jnp.float32), jnp.cumsum(uf, axis=1)], axis=1)
    t = jnp.arange(T)
    outs = []
    for g, w in enumerate(POOL_WINDOWS):
        lo = jnp.clip(t - w // 2, 0, T)
        hi = jnp.clip(t + (w - w // 2), 0, T)
        csg = cs[..., g * POOL_GC:(g + 1) * POOL_GC]
        cnt = (hi - lo).astype(jnp.float32)[None, :, None]
        outs.append((csg[:, hi] - csg[:, lo]) / cnt)
    pooled = jnp.stack(outs, axis=2)
    d = (pooled - uf.reshape(B, T, POOL_GROUPS, POOL_GC)).astype(u.dtype)
    y = jnp.einsum('btgc,gcd->btgd', d, w_pool).reshape(B, T, POOL_WIDTH)
    return y * pool_scale

def neighbourhood_attention(q, k, v, k_ctx, v_ctx, rpb):
    B, T, H, d = q.shape
    R = T // GRID_W
    WR = min(NA_WIN_ROWS, R)
    K = WR * GRID_W
    scale = d ** -0.5
    rows = jnp.arange(R)
    r0 = jnp.clip(rows - NA_WIN_ROWS // 2, 0, R - WR)
    krow = r0[:, None] + jnp.arange(WR)[None, :]
    kg = k.reshape(B, R, GRID_W, H, d)[:, krow].reshape(B, R, K, H, d)
    vg = v.reshape(B, R, GRID_W, H, d)[:, krow].reshape(B, R, K, H, d)
    qg = q.reshape(B, R, GRID_W, H, d)
    s_win = jnp.einsum('brqhd,brkhd->brhqk', qg, kg, preferred_element_type=jnp.float32) * scale
    cols = jnp.arange(GRID_W)
    c0 = jnp.clip(cols - NA_WIN_COLS // 2, 0, GRID_W - NA_WIN_COLS)
    kcol = jnp.arange(K) % GRID_W
    kloc = jnp.arange(K) // GRID_W
    in_win = (kcol[None, :] >= c0[:, None]) & (kcol[None, :] < c0[:, None] + NA_WIN_COLS)
    dr_idx = (krow - rows[:, None])[:, kloc] + NA_WIN_ROWS - 1
    dc_idx = jnp.clip(kcol[None, :] - cols[:, None], -(NA_WIN_COLS - 1), NA_WIN_COLS - 1) + NA_WIN_COLS - 1
    bias = jnp.moveaxis(rpb[:, dr_idx[:, None, :], dc_idx[None, :, :]], 0, 1)
    s_win = jnp.where(in_win[None, None, None], s_win + bias[None].astype(jnp.float32), NEG_INF)
    s_ctx = jnp.einsum('brqhd,bshd->brhqs', qg, k_ctx, preferred_element_type=jnp.float32) * scale
    p = jax.nn.softmax(jnp.concatenate([s_win, s_ctx], axis=-1), axis=-1).astype(v.dtype)
    out = (jnp.einsum('brhqk,brkhd->brqhd', p[..., :K], vg)
           + jnp.einsum('brhqs,bshd->brqhd', p[..., K:], v_ctx))
    return out.reshape(B, T, H, d)

def mla_queries(cq, q_norm, w_uq):
    return heads(rmsnorm(cq, q_norm) @ w_uq, MLA_HEADS, MLA_QK_DIM)

def mla_keys_values(ckv, kpe, w_ukv):
    kv = heads(ckv @ w_ukv, MLA_HEADS, MLA_NOPE_DIM + MLA_V_DIM)
    k_nope, v = kv[..., :MLA_NOPE_DIM], kv[..., MLA_NOPE_DIM:]
    kpe_b = jnp.broadcast_to(kpe[:, :, None, :], k_nope.shape[:-1] + (MLA_ROPE_DIM,))
    return jnp.concatenate([k_nope, kpe_b], axis=-1), v

def merge_branches(y_pool, y_na, y_mla, g_logits, w_branch, w_out):
    B, T, _ = y_pool.shape
    ys = jnp.stack([y_pool, y_na.reshape(B, T, NA_WIDTH), y_mla.reshape(B, T, MLA_WIDTH)], axis=2)
    proj = jnp.einsum('btnc,ncd->btnd', ys, w_branch)
    gates = jax.nn.sigmoid(g_logits.reshape(B, T, N_BRANCHES, D_MODEL))
    return jnp.sum(gates * proj, axis=2) @ w_out

def context_mixer(h, w_in, w_pool, pool_scale, q_norm, w_uq, kv_norm, w_ukv, w_branch, w_out):
    u, nq, nk, nv, cq, ckv, kpe, g_logits = split_inputs(h, w_in)
    y_pool = pool_mixer(u, w_pool, pool_scale)
    nq = heads(nq, NA_HEADS, NA_HEAD_DIM)
    nk = heads(nk, NA_HEADS, NA_HEAD_DIM)
    nv = heads(nv, NA_HEADS, NA_HEAD_DIM)
    y_na = blocked_attention(nq, nk, nv, NA_HEAD_DIM ** -0.5)
    ckv = rmsnorm(ckv, kv_norm)
    q = mla_queries(cq, q_norm, w_uq)
    k, v = mla_keys_values(ckv, kpe, w_ukv)
    y_mla = blocked_attention(q, k, v, MLA_QK_DIM ** -0.5)
    y = merge_branches(y_pool, y_na, y_mla, g_logits, w_branch, w_out)
    return y, nk, nv, ckv, kpe

def latent_mixer(h, ctx_na_k, ctx_na_v, ctx_ckv, ctx_kpe, w_in, w_pool, pool_scale, na_rpb,
                 q_norm, w_uq, kv_norm, w_ukv, w_branch, w_out):
    T = h.shape[1]
    u, nq, nk, nv, cq, ckv, kpe, g_logits = split_inputs(h, w_in)
    y_pool = pool_mixer(u, w_pool, pool_scale)
    y_na = neighbourhood_attention(heads(nq, NA_HEADS, NA_HEAD_DIM), heads(nk, NA_HEADS, NA_HEAD_DIM),
                                   heads(nv, NA_HEADS, NA_HEAD_DIM), ctx_na_k, ctx_na_v, na_rpb)
    cos, sin = axial_rope_tables(T, h.dtype)
    q = mla_queries(cq, q_norm, w_uq)
    q = jnp.concatenate([q[..., :MLA_NOPE_DIM], apply_axial_rope(q[..., MLA_NOPE_DIM:], cos, sin)], axis=-1)
    kpe = apply_axial_rope(kpe[:, :, None, :], cos, sin)[:, :, 0]
    k_lat, v_lat = mla_keys_values(rmsnorm(ckv, kv_norm), kpe, w_ukv)
    k_ctx, v_ctx = mla_keys_values(ctx_ckv, ctx_kpe, w_ukv)
    k = jnp.concatenate([k_lat, k_ctx], axis=1)
    v = jnp.concatenate([v_lat, v_ctx], axis=1)
    y_mla = blocked_attention(q, k, v, MLA_QK_DIM ** -0.5)
    return merge_branches(y_pool, y_na, y_mla, g_logits, w_branch, w_out)

def hier_moe(h, w_group_router, w_expert_router, w1, w3, w2):
    B, T, D = h.shape
    x = h.reshape(-1, D)
    N = x.shape[0]
    gp = jax.nn.softmax((x @ w_group_router).astype(jnp.float32), axis=-1)
    g_w, g_idx = lax.top_k(gp, 1)
    el = (x @ w_expert_router).astype(jnp.float32).reshape(N, N_GROUPS, EXPERTS_PER_GROUP)
    el_g = jnp.take_along_axis(el, g_idx[:, :, None], axis=1)[:, 0]
    top_w, top_i = lax.top_k(jax.nn.softmax(el_g, axis=-1), TOP_K)
    top_w = top_w / jnp.sum(top_w, axis=-1, keepdims=True)
    expert_id = g_idx * EXPERTS_PER_GROUP + top_i
    gates = jnp.einsum('nk,nke->ne', g_w * top_w, jax.nn.one_hot(expert_id, N_EXPERTS, dtype=jnp.float32))
    hid = jax.nn.silu(jnp.einsum('nd,edf->nef', x, w1)) * jnp.einsum('nd,edf->nef', x, w3)
    out = jnp.einsum('nef,efd->nd', hid * gates[:, :, None].astype(hid.dtype), w2)
    return out.reshape(B, T, D)

def setup_inputs(seed: int = 0) -> dict:
    key = jax.random.key(seed)
    ks = jax.random.split(key, 32)

    def nrm(k, shape, scale):
        return jax.random.normal(k, shape, jnp.float32) * scale

    def gain(k, shape):
        return 1.0 + 0.05 * jax.random.normal(k, shape, jnp.float32)

    return {
        'x_prompt': nrm(ks[0], (BATCH, SEQ, D_MODEL), 1.0),
        'x_sample': nrm(ks[1], (DEC_BATCH, DEC_SEQ, D_MODEL), 1.0),
        'cache_na_k': nrm(ks[2], (DEC_BATCH, DEPTH, PAST_LEN, NA_HEADS, NA_HEAD_DIM), 1.0),
        'cache_na_v': nrm(ks[3], (DEC_BATCH, DEPTH, PAST_LEN, NA_HEADS, NA_HEAD_DIM), 1.0),
        'cache_mla_ckv': nrm(ks[4], (DEC_BATCH, DEPTH, PAST_LEN, MLA_KV_LORA), 1.0),
        'cache_mla_kpe': nrm(ks[5], (DEC_BATCH, DEPTH, PAST_LEN, MLA_ROPE_DIM), 1.0),
        'c': nrm(ks[6], (DEC_BATCH, D_MODEL), 1.0),
        'c_ctx': nrm(ks[7], (D_MODEL,), 1.0),
        'w_mod': nrm(ks[8], (DEPTH, D_MODEL, 6 * D_MODEL), 0.5 * D_MODEL ** -0.5),
        'b_mod': nrm(ks[9], (DEPTH, 6 * D_MODEL), 0.02),
        'g_pre_mix': gain(ks[10], (DEPTH, D_MODEL)),
        'g_post_mix': gain(ks[11], (DEPTH, D_MODEL)),
        'g_pre_ffn': gain(ks[12], (DEPTH, D_MODEL)),
        'g_post_ffn': gain(ks[13], (DEPTH, D_MODEL)),
        'w_in': nrm(ks[14], (DEPTH, D_MODEL, IN_COLS), D_MODEL ** -0.5),
        'w_pool': nrm(ks[15], (DEPTH, POOL_GROUPS, POOL_GC, POOL_GC), POOL_GC ** -0.5),
        'pool_scale': gain(ks[16], (DEPTH, POOL_WIDTH)),
        'na_rpb': nrm(ks[17], (DEPTH, NA_HEADS, 2 * NA_WIN_ROWS - 1, 2 * NA_WIN_COLS - 1), 0.1),
        'mla_q_norm': gain(ks[18], (DEPTH, MLA_Q_LORA)),
        'mla_w_uq': nrm(ks[19], (DEPTH, MLA_Q_LORA, MLA_HEADS * MLA_QK_DIM), MLA_Q_LORA ** -0.5),
        'mla_kv_norm': gain(ks[20], (DEPTH, MLA_KV_LORA)),
        'mla_w_ukv': nrm(ks[21], (DEPTH, MLA_KV_LORA, MLA_HEADS * (MLA_NOPE_DIM + MLA_V_DIM)), MLA_KV_LORA ** -0.5),
        'w_branch': nrm(ks[22], (DEPTH, N_BRANCHES, BRANCH_WIDTH, D_MODEL), BRANCH_WIDTH ** -0.5),
        'w_out': nrm(ks[23], (DEPTH, D_MODEL, D_MODEL), D_MODEL ** -0.5),
        'w_group_router': nrm(ks[24], (DEPTH, D_MODEL, N_GROUPS), D_MODEL ** -0.5),
        'w_expert_router': nrm(ks[25], (DEPTH, D_MODEL, N_EXPERTS), D_MODEL ** -0.5),
        'w_exp_gate': nrm(ks[26], (DEPTH, N_EXPERTS, D_MODEL, EXPERT_FF), D_MODEL ** -0.5),
        'w_exp_up': nrm(ks[27], (DEPTH, N_EXPERTS, D_MODEL, EXPERT_FF), D_MODEL ** -0.5),
        'w_exp_down': nrm(ks[28], (DEPTH, N_EXPERTS, EXPERT_FF, D_MODEL), EXPERT_FF ** -0.5),
    }

def reference(x_prompt, x_sample, cache_na_k, cache_na_v, cache_mla_ckv, cache_mla_kpe, c, c_ctx,
              w_mod, b_mod, g_pre_mix, g_post_mix, g_pre_ffn, g_post_ffn, w_in, w_pool, pool_scale, na_rpb,
              mla_q_norm, mla_w_uq, mla_kv_norm, mla_w_ukv, w_branch, w_out, w_group_router, w_expert_router,
              w_exp_gate, w_exp_up, w_exp_down):
    xp = x_prompt
    na_k_l, na_v_l, ckv_l, kpe_l = [], [], [], []
    for l in range(DEPTH):
        sh1, sc1, gt1, sh2, sc2, gt2 = modulation(c_ctx, w_mod[l], b_mod[l])
        h = ada_norm(xp, g_pre_mix[l], sh1, sc1)
        y, nk, nv, ckv, kpe = context_mixer(h, w_in[l], w_pool[l], pool_scale[l], mla_q_norm[l], mla_w_uq[l],
                                            mla_kv_norm[l], mla_w_ukv[l], w_branch[l], w_out[l])
        na_k_l.append(nk)
        na_v_l.append(nv)
        ckv_l.append(ckv)
        kpe_l.append(kpe)
        xp = xp + gt1 * rmsnorm(y, g_post_mix[l])
        h = ada_norm(xp, g_pre_ffn[l], sh2, sc2)
        y = hier_moe(h, w_group_router[l], w_expert_router[l], w_exp_gate[l], w_exp_up[l], w_exp_down[l])
        xp = xp + gt2 * rmsnorm(y, g_post_ffn[l])

    xs = x_sample
    for l in range(DEPTH):
        sh1, sc1, gt1, sh2, sc2, gt2 = modulation(c, w_mod[l], b_mod[l])
        h = ada_norm(xs, g_pre_mix[l], sh1, sc1)
        y = latent_mixer(h, cache_na_k[:, l], cache_na_v[:, l], cache_mla_ckv[:, l], cache_mla_kpe[:, l],
                         w_in[l], w_pool[l], pool_scale[l], na_rpb[l], mla_q_norm[l], mla_w_uq[l],
                         mla_kv_norm[l], mla_w_ukv[l], w_branch[l], w_out[l])
        xs = xs + gt1 * rmsnorm(y, g_post_mix[l])
        h = ada_norm(xs, g_pre_ffn[l], sh2, sc2)
        y = hier_moe(h, w_group_router[l], w_expert_router[l], w_exp_gate[l], w_exp_up[l], w_exp_down[l])
        xs = xs + gt2 * rmsnorm(y, g_post_ffn[l])

    return (xp, xs, jnp.stack(na_k_l, axis=1), jnp.stack(na_v_l, axis=1), jnp.stack(ckv_l, axis=1), jnp.stack(kpe_l, axis=1))


_drawn_inputs = setup_inputs


def setup_inputs(seed=0):
    import zlib

    import numpy as np

    out = dict(_drawn_inputs(seed))
    spreads = {}
    factors = {'na_rpb': 2.847, 'cache_mla_kpe': 3.341}
    for name, (base, spread) in spreads.items():
        noise = np.random.default_rng([zlib.crc32(name.encode()), seed]).standard_normal(out[name].shape)
        drawn = base * np.exp(spread * noise) if base else spread * noise
        out[name] = __import__('jax').numpy.asarray(drawn.astype(out[name].dtype))
    for name, factor in factors.items():
        out[name] = (out[name] * factor).astype(out[name].dtype)
    return out
```

```python
import concourse.bass as bass
from concourse import mybir
from contextlib import ExitStack

F32 = mybir.dt.float32
U32 = mybir.dt.uint32
ALU = mybir.AluOpType
ACT = mybir.ActivationFunctionType
AX_X = mybir.AxisListType.X
ds = bass.ds

P = 128
D = 1024
KD = D // P
N_CTX, N_LAT = 128, 512
T = N_CTX + N_LAT
TT = T // P
N_CACHE = 128
KEYS = T + N_CACHE
KT = KEYS // P
DEPTH = 2
GW = 64
ROWS = N_LAT // GW
WIN = 16
NH, HD = 8, 64
NM = NH * HD // P
RD = 32
QKD = HD + RD
QL, KVL = 384, 256
QT, KVT = QL // P, KVL // P
LOW = QL + KVL + RD
MOD = 6 * D
NMOD = MOD // 512
EPS = 1e-6
NG, EG = 4, 4
NE = NG * EG
FF = 256
FT = FF // P
DR = 14
POOL_W = (2, 4, 8, 16)
PADT = 8 + N_CTX + 16 + N_LAT + 8
C_AT, L_AT = 8, 8 + N_CTX + 16
BLOCK = P
NB = (2 * T + NE * (BLOCK - 1)) // BLOCK
NB += NB % 2
NEG = -1e30
LEAST = -3e38

U_AT, NQ_AT, NK_AT, NV_AT, LOW_AT, G_AT = 0, 512, 1024, 1536, 2048, 2048 + LOW

NPAIR = 3
NSLOT = 3
SLOT = 4096
LAG_PT, LAG_PV = 2, 3


def attention_steps():
    return [(h, t) for h in range(NH) for t in range(TT)]


MERGE = [(m, n) for c in range(2) for n in range(3) for m in range(4 * c, 4 * c + 4)]

CONST_COLS = [("ident", P), ("tri", P), ("ones", P), ("mask", GW), ("rope", N_LAT), ("cos", 4 * RD), ("sin", 4 * RD),
              ("rev", TT * EG), ("tok", TT), ("blk", NB), ("edge", 4 * 16)]


def plan_jobs():
    jobs = [("mod", j) for j in range(NMOD)]
    jobs += [("xt", t) for t in range(TT)]
    jobs += [("nk", m) for m in range(NM)] + [("nv", t) for t in range(TT)]
    jobs += [("nq", m) for m in range(NM)] + [("u", m) for m in range(NM)]
    for t in range(TT):
        jobs.append(("low", t))
        if t:
            jobs.append(("lowt", t - 1))
    jobs.append(("lowt", TT - 1))

    def attention(kind):
        units = attention_steps()
        for i in range(len(units) + LAG_PV):
            if i < len(units):
                jobs.append((kind + "s", i))
            if 0 <= i - LAG_PT < len(units):
                jobs.append((kind + "t", i - LAG_PT))

    attention("na")
    jobs += [("vm", t) for t in range(KT)] + [("kn", h) for h in range(NH)] + [("qm", h) for h in range(NH)]
    attention("ml")
    jobs += [("pool", g) for g in range(NM)]
    for m, n in MERGE:
        jobs += [("gate", m, n), ("branch", m, n)]
    jobs += [("y", t) for t in range(TT)]
    for t in range(TT):
        jobs += [("ht", t), ("lg", t)]
    jobs.append(("cnt", 0))
    return jobs


def plan_chunks():
    chunks = [(("mod", j), ("mod", j)) for j in range(NMOD)]
    chunks += [(("nk",), ("nk", NM - 1)), (("nv",), ("nv", TT - 1)), (("nq",), ("nq", NM - 1)), (("u",), ("u", NM - 1))]
    chunks += [(("low", 0), ("low", TT - 1)), (("low", 1), ("low", TT - 1))]
    chunks += [(("ukv",), ("kn", NH - 1)), (("uq",), ("qm", NH - 1))]
    for c in range(2):
        for n in range(3):
            chunks += [(("gate", c, n), ("gate", 4 * c + 3, n)), (("branch", c, n), ("branch", 4 * c + 3, n))]
    chunks += [(("out", 0), ("y", TT - 1)), (("out", 1), ("y", TT - 1))]
    return chunks


def bass_hybrid_step(nc, x0, k_cache_t, v_cache, ckv_cache_t, kpe_cache_t, c_t, mod_aux, w_mod, w_in, w_pool,
                     pool_scale, rpb_rows, q_norm, kv_norm, w_uq, w_ukv, w_branch, w_out, w_router,
                     w_gate, w_up, w_down, consts,
                     x_res, o_nk_t, o_nv, o_ckv_t, o_kpe):
    jobs, chunks = plan_jobs(), plan_chunks()
    PAIR_OF = {key: i % NPAIR for i, key in enumerate(jobs)}
    USE_OF = {key: i // NPAIR + 1 for i, key in enumerate(jobs)}
    SLOT_OF = {key: i % NSLOT for i, (key, _) in enumerate(chunks)}
    FILL_OF = {key: i // NSLOT + 1 for i, (key, _) in enumerate(chunks)}

    with ExitStack() as ctx:
        sems = []

        def sem(name):
            s = ctx.enter_context(nc.semaphore(name))
            sems.append(s)
            return s

        def sb(name, shape, dt=F32):
            return ctx.enter_context(nc.sbuf_tensor(name, shape, dt))

        ring = sb("ring", [P, NSLOT * SLOT])
        hT = sb("hT", [P, KD * T])
        ysT = sb("ysT", [P, 2 * NM * T])
        NQ_W, T_W, NK_W, NV_W = NM * T, NH * DR * GW, NM * KEYS, KT * 512
        R1_W = NQ_W + T_W + NK_W + NV_W
        r1 = sb("r1", [P, R1_W])
        pp = sb("pp", [P, 4 * T])
        low_t = sb("low_t", [P, QT * T + KVT * KEYS])
        low_tm = sb("low_tm", [P, 2 * LOW])
        u_sb = sb("u_sb", [P, NM * PADT])
        kpeT = sb("kpeT", [P, KEYS])
        cst = sb("cst", [P, consts.shape[1]])
        small = sb("small", [P, 1000])
        wpool_sb = sb("wpool_sb", [P, NM * P])
        router_sb = sb("router_sb", [P, KD * (NG + NE)])
        cols = sb("cols", [P, 2 * KD + NM + QT + KVT + 4])
        ids = sb("ids", [P, 64], U32)

        def view(buf, at, n, **kw):
            v = buf[:, at:at + n]
            if kw:
                (name, size), = kw.items()
                v = v.rearrange(f"p ({name} z) -> p {name} z", **{name: size})
            return v

        xt = view(ysT, 0, TT * D, t=TT)
        bc1 = [view(u_sb, 0, 2 * D, a=2),
               view(r1, NQ_W + T_W + NK_W, 2 * D, a=2)]
        hb = view(pp, 0, 2 * D, a=2)
        h_t = view(hT, 0, KD * T, k=KD)
        aux = view(r1, 0, 2 * 1024, a=2)
        modst = view(low_t, 0, 2 * 512, a=2)
        nqT = view(r1, 0, NQ_W, m=NM)
        tb = view(r1, NQ_W, T_W, h=NH)
        nkT = view(r1, NQ_W + T_W, NK_W, m=NM)
        nv = view(r1, NQ_W + T_W + NK_W, NV_W, t=KT)
        qT = view(r1, 0, NH * T, h=NH)
        kT = view(r1, NH * T, NH * KEYS, h=NH)
        vm = view(r1, NH * T + NH * KEYS, KT * 512, t=KT)
        assert NH * T + NH * KEYS + KT * 512 <= R1_W
        cqT = view(low_t, 0, QT * T, k=QT)
        ckvT = view(low_t, QT * T, KVT * KEYS, k=KVT)
        ltm = view(low_tm, 0, 2 * LOW, a=2)
        probs = [view(pp, 0, T), view(pp, T, T), view(low_tm, 0, T)]
        probT = [view(pp, 2 * T, T), view(pp, 3 * T, T)]
        yT = [None, view(ysT, 0, NM * T, m=NM), view(ysT, NM * T, NM * T, m=NM)]
        u_pad = view(u_sb, 0, NM * PADT, m=NM)
        sum_a = view(ysT, NM * T, PADT)
        sum_b = view(ysT, NM * T + PADT, PADT)
        mergedT = view(r1, 0, KD * T, k=KD)
        yT[0] = view(r1, KD * T, NM * T, m=NM)
        sig = view(r1, (KD + NM) * T, 2 * T, a=2)
        prod = view(r1, (KD + NM + 2) * T, 2 * T, a=2)
        x2 = view(r1, (KD + NM + 4) * T, TT * D, t=TT)
        assert (KD + NM + 4) * T + TT * D <= R1_W
        gb1 = view(u_sb, 0, 2 * D, a=2)
        bc2 = view(hT, 0, 4 * D, a=4)
        yb = view(pp, 0, 2 * D, a=2)
        h2 = view(ysT, 0, TT * D, t=TT)
        h2T = view(low_t, 0, 2 * D, a=2)
        w13 = [view(ring, s * 6144, 4096) for s in range(2)]
        w2s = [view(ring, s * 6144 + 4096, 2048) for s in range(2)]
        xg = view(r1, 0, 2 * D, a=2)
        xgT = view(r1, 2 * D, 2 * D, a=2)
        yo = view(r1, 4 * D, 2 * D, a=2)
        sil = view(r1, 6 * D, 2 * FF, a=2)
        hid = view(r1, 6 * D + 2 * FF, 2 * FF, a=2)
        gb2 = view(u_sb, 0, 2 * D, a=2)
        picks = view(ysT, 0, 4 * D, a=4)
        assert 6 * D + 4 * FF <= (KD + NM + 4) * T

        at = 0
        where = {}
        for name, n in CONST_COLS:
            where[name] = (at, at + n)
            at += n

        def const(name):
            a, b = where[name]
            return cst[:, a:b]

        ident, tri, ones = const("ident"), const("tri"), const("ones")
        cvec = view(cols, 0, 2 * KD, k=KD)
        psc = cols[:, 2 * KD:2 * KD + NM]
        lown = cols[:, 2 * KD + NM:2 * KD + NM + QT + KVT]

        sm_at = [0]

        def sm(n):
            a = sm_at[0]
            sm_at[0] += n
            assert sm_at[0] <= 1000
            return small[:, a:a + n]

        ss, rs, rstd = sm(8), sm(8), sm(8)
        ss2, rs2, rstd2 = sm(12), sm(12), sm(12)
        mx, negm, rsum, rinv = sm(2), sm(1), sm(3), sm(2)
        mxs = [mx, sm(2)]
        negms = [negm] + [sm(1) for _ in range(2)]
        rsums = [rsum[:, i:i + 1] for i in range(3)]
        cvraw = sm(2 * KD)
        LG = NG + NE
        lg = sm(TT * LG).rearrange("p (t n) -> p t n", t=TT)

        def smt(n):
            return sm(TT * n).rearrange("p (t n) -> p t n", t=TT)

        gmax, gsum, gate1, gate2, m1, m2 = smt(1), smt(1), smt(1), smt(1), smt(1), smt(1)
        e4, oh_g, el, oh1, oh2, w4 = smt(4), smt(4), smt(4), smt(4), smt(4), smt(4)
        ch1, ch2, chs = smt(NE), smt(NE), smt(NE)
        slots = smt(NE)
        slot1, slot2 = smt(1), smt(1)
        elm, big = smt(4), smt(1)
        rot = sm(RD)
        swapped = view(low_tm, T, N_LAT)
        n_e, blocks, blk_end, blk_start = sm(NE), sm(NE), sm(NE), sm(NE)
        bexp = sm(NB)
        bcmp = view(pp, 0, NB * NE, a=NB)
        slot_ids = ids[:, 0:2 * TT]
        tok_ids = ids[:, 2 * TT:3 * TT]
        blk_ids = ids[:, 16:16 + NB]
        src_ids = sb("src_ids", [P, NB], U32)[:, :]

        pair = [ctx.enter_context(nc.psum_tensor(f"pair{i}", [P, 1024], F32)) for i in range(NPAIR)]
        opair = ctx.enter_context(nc.psum_tensor("opair", [P, 1024], F32))
        MID = 512 - T // 2
        KMID = 512 - KEYS // 2
        LMID = 512 - LOW // 2

        mod_rows = nc.dram_tensor("mod_rows", [2, MOD], F32).ap()
        h2_rows = nc.dram_tensor("h2_rows", [T, D], F32).ap()
        slot_token = nc.dram_tensor("slot_token", [NB * BLOCK, 1], U32).ap()
        expert_out = nc.dram_tensor("expert_out", [NB * BLOCK, D], F32).ap()

        consts_in, x_copied, ids_zeroed, list_zeroed, cv_in, cv_ready = (
            ctx.enter_context(nc.semaphore(n)) for n in ("consts_in", "x_copied", "ids_zeroed", "list_zeroed", "cv_in", "cv_ready"))
        layer_done = ctx.enter_context(nc.semaphore("layer_done"))
        go = {e: ctx.enter_context(nc.semaphore("go_" + e)) for e in ("pe", "act", "dve", "pool")}
        filled = [sem(f"filled{i}") for i in range(NPAIR)]
        freed = [sem(f"freed{i}") for i in range(NPAIR)]
        landed = [sem(f"landed{i}") for i in range(NSLOT)]
        aux_in = [sem(f"aux_in{i}") for i in range(2)]
        mod_row, bc_in, x_in = sem("mod_row"), sem("bc_in"), sem("x_in")
        mod_stored = [sem(f"mod_stored{i}") for i in range(2)]
        bias_in, bias_masked, caches_in, small_in, kpe_in = (sem(n) for n in ("bias_in", "bias_masked", "caches_in", "small_in", "kpe_in"))
        pooled, pool_step, kpe_copied = (sem(n) for n in ("pooled", "pool_step", "kpe_copied"))
        dve_step, act_step = sem("dve_step"), sem("act_step")
        ms_ready, root_ready = sem("ms_ready"), sem("root_ready")
        sq_ready, h_ready = sem("sq_ready"), sem("h_ready")
        low_sq, low_ms, low_root, low_scaled = sem("low_sq"), sem("low_ms"), sem("low_root"), sem("low_scaled")
        caches_out, kpe_out = sem("caches_out"), sem("kpe_out")
        q_ready = sem("q_ready")
        biased, exped, scaled, pv_done, o_freed = (sem(n) for n in ("biased", "exped", "scaled", "pv_done", "o_freed"))
        merged, x2_in, gb_in, bc2_in = sem("merged"), sem("x2_in"), sem("gb_in"), sem("bc2_in")
        x2_new, h2_ready, h2_stored = sem("x2_new"), sem("h2_ready"), sem("h2_stored")
        routed_a, routed_b, chosen, slots_ready, list_in, blocks_ready = (
            sem(n) for n in ("routed_a", "routed_b", "chosen", "slots_ready", "list_in", "blocks_ready"))
        scattered = ctx.enter_context(nc.semaphore("scattered"))
        xg_in = [ctx.enter_context(nc.semaphore(f"xg_in{i}")) for i in range(2)]
        picked = [ctx.enter_context(nc.semaphore(f"picked{i}")) for i in range(2)]
        PICKS = (32 * 3, 32 * 2)
        up_in = [sem(f"up_in{i}") for i in range(2)]
        down_in = [sem(f"down_in{i}") for i in range(2)]
        t_filled, t_freed, h_filled, sil_ready, hid_ready, y_filled, y_read = (
            sem(n) for n in ("t_filled", "t_freed", "h_filled", "sil_ready", "hid_ready", "y_filled", "y_read"))
        yo_stored = [sem(f"yo_stored{i}") for i in range(2)]
        mixed, x_stored, sq3, ms3, root3 = (sem(n) for n in ("mixed", "x_stored", "sq3", "ms3", "root3"))

        def pair_for(eng, key):
            if USE_OF[key] > 1:
                eng.wait_ge(freed[PAIR_OF[key]], USE_OF[key] - 1)
            return pair[PAIR_OF[key]]

        def await_job(eng, key):
            eng.wait_ge(filled[PAIR_OF[key]], USE_OF[key])
            return pair[PAIR_OF[key]]

        def await_read(eng, key):
            eng.wait_ge(freed[PAIR_OF[key]], USE_OF[key])

        block = ctx.enter_context(nc.Block())

        @block.sync
        def _(sp):
            sp.dma_start(cst[:, :], consts).then_inc(consts_in, 16)
            sp.dma_start(cvraw, c_t).then_inc(cv_in, 16)
            sp.dma_start(x_res, x0).then_inc(x_copied, 16)
            with sp.Fori(0, DEPTH) as L:
                def src(key):
                    kind = key[0]
                    wl = w_in[ds(L, 1)].rearrange("a (k p) n -> p (a k) n", p=P)
                    if kind == "mod":
                        w = w_mod[ds(L, 1)].rearrange("a (k p) n -> p (a k) n", p=P)
                        return w[:, :, key[1] * 512:(key[1] + 1) * 512]
                    if kind in ("u", "nq", "nk", "nv"):
                        c0 = {"u": U_AT, "nq": NQ_AT, "nk": NK_AT, "nv": NV_AT}[kind]
                        return wl[:, :, c0:c0 + 512]
                    if kind == "low":
                        c0 = LOW_AT + key[1] * (LOW // 2)
                        return wl[:, :, c0:c0 + LOW // 2]
                    if kind == "ukv":
                        return w_ukv[ds(L, 1)].rearrange("a (k p) n -> p (a k) n", p=P)
                    if kind == "uq":
                        return w_uq[ds(L, 1)].rearrange("a (k p) n -> p (a k) n", p=P)
                    if kind == "gate":
                        c0 = G_AT + key[2] * D + key[1] * 512
                        return wl[:, :, c0:c0 + 512]
                    if kind == "branch":
                        w = w_branch[ds(L, 1)].rearrange("a n (k p) d -> p (a n k) d", p=P)
                        return w[:, 4 * key[2]:4 * key[2] + 4, key[1] * 512:(key[1] + 1) * 512]
                    w = w_out[ds(L, 1)].rearrange("a (k p) n -> p (a k) n", p=P)
                    return w[:, :, key[1] * 512:(key[1] + 1) * 512]

                for i, (key, _) in enumerate(chunks):
                    if i >= NSLOT:
                        last_reader = chunks[i - NSLOT][1]
                        await_job(sp, last_reader)
                    s = src(key)
                    k, n = s.shape[1], s.shape[2]
                    dst = view(ring, SLOT_OF[key] * SLOT, k * n, k=k)
                    sp.dma_start(dst, s).then_inc(landed[SLOT_OF[key]], 16)

                h2_out = h2_rows.rearrange("(t p) d -> p t d", p=P)
                for t in range(TT):
                    sp.wait_ge(h2_ready, t + 1)
                    sp.dma_start(h2_out[:, t, :], h2[:, t, :]).then_inc(h2_stored, 16)
                sp.wait_ge(scattered, L * (32 * TT) + 32 * TT)
                with nc.allow_non_contiguous_dma(reason="four-byte rows"):
                    sp.dma_start(src_ids, slot_token.rearrange("(b p) o -> p (b o)", p=P)).then_inc(list_in, 16)
                sp.wait_ge(blocks_ready, 1)
                with sp.Fori(0, NB // 2) as it:
                    for s in range(2):
                        e = sp.value_load(blk_ids[0:1, ds(it * 2 + s, 1)], min_val=0, max_val=NE - 1)
                        sp.wait_ge(h_filled, it * 2 + (s + 1))
                        for w, at_ in ((w_gate, 0), (w_up, 2048)):
                            sp.dma_start(w13[s][:, at_:at_ + 2048].rearrange("p (k f) -> p k f", k=KD),
                                         w[ds(L * NE + e, 1)].rearrange("a (k p) f -> p (a k) f", p=P)).then_inc(up_in[s], 16)
                        sp.wait_ge(y_filled, it * 2 + (s + 1))
                        sp.dma_start(w2s[s].rearrange("p (k f) -> p k f", k=FT),
                                     w_down[ds(L * NE + e, 1)].rearrange("a (k p) f -> p (a k) f", p=P)).then_inc(down_in[s], 16)

                sp.wait_ge(layer_done, 4)
                for s in sems:
                    sp.sem_clear(s)
                sp.sem_clear(layer_done)
                for e in ("pe", "act", "dve", "pool"):
                    sp.sem_inc(go[e], 1)

        @block.scalar
        def _(act):
            act.wait_ge(cv_in, 16)
            nc.scalar.activation(cols[:, 0:2 * KD], cvraw, ACT.Silu).then_inc(cv_ready, 1)
            act.wait_ge(x_copied, 16)
            with act.Fori(0, DEPTH) as L:
                def layer(t):
                    return t[ds(L, 1)]

                steps = [0]

                def chain(ins):
                    ins.then_inc(act_step, 1)
                    steps[0] += 1
                    act.wait_ge(act_step, steps[0])

                act.dma_start(xt, x_res.rearrange("(t p) d -> p t d", p=P)).then_inc(x_in, 16)
                act.dma_start(cols[:, 2 * KD:2 * KD + NM], layer(pool_scale).rearrange("a p n -> p (a n)")).then_inc(small_in, 16)
                act.dma_start(lown[:, 0:QT], layer(q_norm).rearrange("a p n -> p (a n)")).then_inc(small_in, 16)
                act.dma_start(lown[:, QT:QT + KVT], layer(kv_norm).rearrange("a p n -> p (a n)")).then_inc(small_in, 16)
                act.dma_start(view(wpool_sb, 0, NM * P, g=NM), layer(w_pool).rearrange("a g c d -> c (a g) d")).then_inc(small_in, 16)
                act.dma_start(view(router_sb, 0, KD * LG, k=KD), layer(w_router).rearrange("a (k p) n -> p (a k) n", p=P)).then_inc(small_in, 16)
                act.dma_start(nkT[:, :, T:KEYS], layer(k_cache_t).rearrange("a (m p) t -> p (a m) t", p=P)).then_inc(caches_in, 16)
                act.dma_start(nv[:, KT - 1, :], layer(v_cache).rearrange("a p n -> p (a n)")).then_inc(caches_in, 16)
                act.dma_start(ckvT[:, :, T:KEYS], layer(ckv_cache_t).rearrange("a (k p) t -> p (a k) t", p=P)).then_inc(caches_in, 16)
                act.dma_start(kpeT[HD:QKD, T:KEYS], layer(kpe_cache_t).rearrange("a p t -> p (a t)")).then_inc(caches_in, 16)
                tr = layer(rpb_rows).rearrange("a q h r c -> q (a h) r c")
                tb4 = tb.rearrange("p h (r c) -> p h r c", c=GW)
                act.dma_start(tb4[0:GW], tr[:, :, 1:1 + DR, :]).then_inc(bias_in, 16)
                act.dma_start(tb4[GW:P], tr[:, :, 0:DR, :]).then_inc(bias_in, 16)

                act.wait_ge(x_in, 16)
                for t in range(TT):
                    nc.scalar.activation(hT[:, 0:D], xt[:, t, :],
                                         ACT.Square, accum_out=ss[:, t:t + 1]).then_inc(sq_ready, 1)
                    act.wait_ge(sq_ready, t + 1)
                def load_aux(j):
                    if j >= 2:
                        act.wait_ge(mod_row, j - 1)
                    act.dma_start(aux[0:2, j % 2, :], mod_aux[ds(L, 1)][:, j:j + 1].rearrange("a b r n -> (a b r) n"))\
                        .then_inc(aux_in[j % 2], 16)

                load_aux(0)
                load_aux(1)
                for j in range(NMOD):
                    act.wait_ge(mod_row, j + 1)
                    act.dma_start(mod_rows[:, j * 512:(j + 1) * 512], modst[0:2, j % 2, :]).then_inc(mod_stored[j % 2], 16)
                    if j + 2 < NMOD:
                        load_aux(j + 2)
                    if j == 3:
                        for s in range(2):
                            act.wait_ge(mod_stored[s], 32)
                        for g in range(2):
                            for i, c0 in enumerate((D, 0)):
                                act.dma_start(bc1[g][:, i, :], mod_rows[g:g + 1, c0:c0 + D].partition_broadcast(P))\
                                    .then_inc(bc_in, 16)
                act.wait_ge(ms_ready, 1)
                nc.scalar.activation(rs[:, 0:TT], rs[:, 0:TT], ACT.Sqrt).then_inc(root_ready, 1)
                for t in range(TT):
                    ps = await_job(act, ("xt", t))
                    nc.scalar.copy(h_t[:, :, t * P:(t + 1) * P], ps[:, :].rearrange("p (k c) -> p k c", k=KD))\
                        .then_inc(freed[PAIR_OF[("xt", t)]], 1)
                for m in range(NM):
                    ps = await_job(act, ("nk", m))
                    nc.scalar.copy(nkT[:, m, 0:T], ps[:, MID:MID + T]).then_inc(freed[PAIR_OF[("nk", m)]], 1)
                await_read(act, ("nk", NM - 1))
                act.dma_start(layer(o_nk_t).rearrange("a (m p) t -> p (a m) t", p=P), nkT[:, :, 0:N_CTX]).then_inc(caches_out, 16)
                await_read(act, ("nv", 0))
                act.dma_start(layer(o_nv).rearrange("a p n -> p (a n)"), nv[:, 0, :]).then_inc(caches_out, 16)
                for m in range(NM):
                    ps = await_job(act, ("nq", m))
                    nc.scalar.mul(nqT[:, m, :], ps[:, MID:MID + T], HD ** -0.5).then_inc(freed[PAIR_OF[("nq", m)]], 1)

                for t in range(TT):
                    ps = await_job(act, ("low", t))
                    nc.scalar.activation(pp[:, 0:QL], ps[:, LMID:LMID + QL], ACT.Square,
                                         accum_out=ss2[:, 2 * t:2 * t + 1])
                    nc.scalar.activation(pp[:, QL:QL + KVL], ps[:, LMID + QL:LMID + QL + KVL], ACT.Square,
                                         accum_out=ss2[:, 2 * t + 1:2 * t + 2]).then_inc(low_sq, 1)
                    if t >= 2:
                        await_job(act, ("lowt", t - 2))
                        if t == 2:
                            act.wait_ge(kpe_out, 16)
                    nc.scalar.copy(ltm[:, t % 2, :], ps[:, LMID:LMID + LOW]).then_inc(freed[PAIR_OF[("low", t)]], 1)
                    if t == 0:
                        await_read(act, ("low", 0))
                        act.dma_start(layer(o_kpe).rearrange("a p n -> p (a n)"), ltm[:, 0, QL + KVL:LOW]).then_inc(kpe_out, 16)
                    act.wait_ge(low_ms, t + 1)
                    nc.scalar.activation(rs2[:, 2 * t:2 * t + 2], rs2[:, 2 * t:2 * t + 2], ACT.Sqrt).then_inc(low_root, 1)
                await_read(act, ("lowt", 0))
                act.dma_start(layer(o_ckv_t).rearrange("a (k p) t -> p (a k) t", p=P), ckvT[:, :, 0:N_CTX]).then_inc(caches_out, 16)

                units = attention_steps()

                def attention(kind, base):
                    for i in range(len(units) + LAG_PV):
                        if i < len(units):
                            t = units[i][1]
                            n = T if t else P
                            act.wait_ge(biased, base + i + 1)
                            if kind == "na" and t:
                                nc.scalar.activation(probs[i % 3][:, 0:n], probs[i % 3][:, 0:n], ACT.Exp,
                                                     bias=negms[i % 3], accum_out=rsums[i % 3]).then_inc(exped, 1)
                            else:
                                ps = pair[PAIR_OF[(kind + "s", i)]]
                                if i >= 3:
                                    await_job(act, (kind + "t", i - 3))
                                nc.scalar.activation(probs[i % 3][:, 0:n], ps[:, MID:MID + n], ACT.Exp,
                                                     bias=negms[i % 3], scale=1.0 if kind == "na" else QKD ** -0.5,
                                                     accum_out=rsums[i % 3])\
                                    .then_inc(freed[PAIR_OF[(kind + "s", i)]], 1)
                        j = i - LAG_PT
                        if 0 <= j < len(units):
                            n = T if units[j][1] else P
                            ps = await_job(act, (kind + "t", j))
                            if j >= 2:
                                act.wait_ge(pv_done, base + j - 1)
                            nc.scalar.copy(probT[j % 2][:, 0:n], ps[:, 0:n]).then_inc(freed[PAIR_OF[(kind + "t", j)]], 1)

                attention("na", 0)
                act.wait_ge(caches_out, 48)
                for t in range(KT):
                    ps = await_job(act, ("vm", t))
                    nc.scalar.copy(vm[:, t, :], ps[:, 0:512]).then_inc(freed[PAIR_OF[("vm", t)]], 1)
                for h in range(NH):
                    ps = await_job(act, ("kn", h))
                    nc.scalar.copy(kT[0:HD, h, :], ps[0:HD, KMID:KMID + KEYS]).then_inc(freed[PAIR_OF[("kn", h)]], 1)
                attention("ml", len(units))

                for g in range(NM):
                    ps = await_job(act, ("pool", g))
                    nc.scalar.mul(yT[0][:, g, :], ps[:, 1024 - T:1024], psc[:, g:g + 1]).then_inc(freed[PAIR_OF[("pool", g)]], 1)
                for s in range(2):
                    act.wait_ge(mod_stored[s], 16 * NMOD // 2)
                act.dma_start(x2, x_res.rearrange("(t p) d -> p t d", p=P)).then_inc(x2_in, 16)
                for g in range(2):
                    act.dma_start(gb1[:, g, :], mod_rows[g:g + 1, 2 * D:3 * D].partition_broadcast(P)).then_inc(gb_in, 16)
                for i, (m, n) in enumerate(MERGE):
                    ps = await_job(act, ("gate", m, n))
                    if i >= 2:
                        await_read(act, ("branch", *MERGE[i - 2]))
                    nc.scalar.activation(sig[:, i % 2, :], ps[:, MID:MID + T], ACT.Sigmoid)\
                        .then_inc(freed[PAIR_OF[("gate", m, n)]], 1)
                await_job(act, ("gate", KD - 1, 2))
                for g in range(2):
                    act.dma_start(bc2[:, 2 * g, :], mod_rows[g:g + 1, 4 * D:5 * D].partition_broadcast(P)).then_inc(bc2_in, 16)
                    act.dma_start(bc2[:, 2 * g + 1, :], mod_rows[g:g + 1, 3 * D:4 * D].partition_broadcast(P)).then_inc(bc2_in, 16)
                for t in range(TT):
                    ps = await_job(act, ("y", t))
                    if t >= 2:
                        act.wait_ge(x2_new, t - 1)
                    nc.scalar.activation(yb[:, t % 2, :], ps[:, :], ACT.Square, accum_out=ss[:, t:t + 1]).then_inc(sq3, 1)
                    act.wait_ge(ms3, t + 1)
                    nc.scalar.activation(rs[:, t:t + 1], rs[:, t:t + 1], ACT.Sqrt).then_inc(root3, 1)
                for t in range(TT):
                    act.wait_ge(x2_new, t + 1)
                    nc.scalar.activation(hT[:, 4 * D:5 * D], x2[:, t, :], ACT.Square,
                                         accum_out=ss[:, t:t + 1]).then_inc(sq3, 1)
                    act.wait_ge(sq3, TT + t + 1)
                    act.wait_ge(ms3, TT + t + 1)
                    nc.scalar.activation(rs[:, t:t + 1], rs[:, t:t + 1], ACT.Sqrt).then_inc(root3, 1)
                for t in range(TT):
                    ps = await_job(act, ("ht", t))
                    if t >= 2:
                        await_job(act, ("lg", t - 2))
                    nc.scalar.copy(h2T[:, t % 2, :], ps[:, :]).then_inc(freed[PAIR_OF[("ht", t)]], 1)
                act.wait_ge(routed_a, 1)
                nc.scalar.activation(e4, e4, ACT.Exp).then_inc(routed_b, 1)
                act.wait_ge(routed_a, 2)
                nc.scalar.activation(m2, m2, ACT.Exp).then_inc(routed_b, 1)

                for g in range(2):
                    if g == 0:
                        act.wait_ge(x2_new, TT)
                    act.dma_start(gb2[:, g, :], mod_rows[g:g + 1, 5 * D:6 * D].partition_broadcast(P)).then_inc(gb_in, 16)
                act.sem_inc(y_read, 2)
                for s in range(2):
                    act.sem_inc(yo_stored[s], 16)
                out_blocks = expert_out.rearrange("(b p) d -> b p d", p=P)
                with act.Fori(0, NB // 2) as it:
                    for s in range(2):
                        act.wait_ge(h_filled, it * 2 + (s + 3))
                        nc.scalar.activation(sil[:, s, :], pair[1][:, s * 512:s * 512 + FF], ACT.Silu).then_inc(sil_ready, 1)
                        act.wait_ge(y_filled, it * 2 + (s + 3))
                        act.wait_ge(yo_stored[s], it * 16 + 16)
                        nc.scalar.copy(yo[:, s, :], (pair[2], opair)[s][:, :]).then_inc(y_read, 1)
                        act.wait_ge(y_read, it * 2 + (s + 3))
                        act.dma_start(out_blocks[ds(it * 2 + s, 1)].rearrange("a p d -> p (a d)"), yo[:, s, :]).then_inc(yo_stored[s], 16)
                for t in range(TT):
                    act.wait_ge(mixed, t + 1)
                    nc.scalar.activation(hT[:, 0:D], picks[:, 2 * (t % 2), :], ACT.Square,
                                         accum_out=ss[:, t:t + 1]).then_inc(sq3, 1)
                    act.wait_ge(sq3, 2 * TT + t + 1)
                    act.wait_ge(ms3, 2 * TT + t + 1)
                    nc.scalar.activation(rs[:, t:t + 1], rs[:, t:t + 1], ACT.Sqrt).then_inc(root3, 1)
                    act.wait_ge(x2_new, TT + t + 1)
                    act.dma_start(x_res[t * P:(t + 1) * P, :], x2[:, t, :]).then_inc(x_stored, 16)
                act.wait_ge(x_stored, 16 * TT)
                act.wait_ge(root3, 3 * TT)
                act.sem_inc(layer_done, 1)
                act.wait_ge(go["act"], 1)
                act.sem_clear(go["act"])

        @block.vector
        def _(dve):
            V = nc.vector
            dve.wait_ge(consts_in, 16)
            V.tensor_copy(tok_ids, const("tok"))
            with dve.Fori(0, DEPTH) as L:
                steps = [0]

                def link(ins):
                    ins.then_inc(dve_step, 1)
                    steps[0] += 1
                    dve.wait_ge(dve_step, steps[0])

                for j in range(NMOD):
                    ps = await_job(dve, ("mod", j))
                    dve.wait_ge(aux_in[j % 2], 16 * (j // 2 + 1))
                    if j >= 2:
                        dve.wait_ge(mod_stored[j % 2], 16 * (j // 2))
                    st, ax = modst[0:2, j % 2, :], aux[0:2, j % 2, :]
                    one = 1.0 if j // 2 in (1, 4) else 0.0
                    V.scalar_tensor_tensor(out=st, in0=ps[0:2, 0:512], scalar=one, in1=ax[:, 0:512],
                                           op0=ALU.add, op1=ALU.add).then_inc(freed[PAIR_OF[("mod", j)]], 1)
                    await_read(dve, ("mod", j))
                    V.tensor_tensor(st, st, ax[:, 512:1024], ALU.mult).then_inc(mod_row, 1)

                dve.wait_ge(sq_ready, TT)
                V.tensor_scalar(rs[:, 0:TT], ss[:, 0:TT], 1.0 / D, EPS, ALU.mult, ALU.add).then_inc(ms_ready, 1)
                dve.wait_ge(root_ready, 1)
                link(V.reciprocal(rstd[:, 0:TT], rs[:, 0:TT]))
                dve.wait_ge(bc_in, 64)
                dve.wait_ge(x_in, 16)
                for t in range(TT):
                    rows = bc1[min(t, 1)]
                    if t >= 2:
                        await_job(dve, ("xt", t - 2))
                    link(V.scalar_tensor_tensor(out=hb[:, t % 2, :], in0=xt[:, t, :], scalar=rstd[:, t:t + 1],
                                                in1=rows[:, 0, :], op0=ALU.mult, op1=ALU.mult))
                    V.tensor_tensor(hb[:, t % 2, :], hb[:, t % 2, :], rows[:, 1, :], ALU.add).then_inc(h_ready, 1)
                for t in range(TT):
                    ps = await_job(dve, ("nv", t))
                    V.tensor_copy(nv[:, t, :], ps[:, 0:512]).then_inc(freed[PAIR_OF[("nv", t)]], 1)
                for a, b in ((0, C_AT), (C_AT + N_CTX, L_AT), (L_AT + N_LAT, PADT)):
                    V.memset(u_pad[:, :, a:b], 0.0)
                for m in range(NM):
                    ps = await_job(dve, ("u", m))
                    V.tensor_copy(u_pad[:, m, C_AT:C_AT + N_CTX], ps[:, MID:MID + N_CTX])
                    V.tensor_copy(u_pad[:, m, L_AT:L_AT + N_LAT], ps[:, MID + N_CTX:MID + T])\
                        .then_inc(freed[PAIR_OF[("u", m)]], 1)

                def low_transposed(t):
                    ps = await_job(dve, ("lowt", t))
                    tok = slice(t * P, (t + 1) * P)
                    V.tensor_tensor(cqT[:, :, tok], ps[:, 0:QL].rearrange("p (k c) -> p k c", k=QT),
                                    lown[:, 0:QT].unsqueeze(2).to_broadcast([P, QT, P]), ALU.mult)
                    V.tensor_tensor(ckvT[:, :, tok], ps[:, QL:QL + KVL].rearrange("p (k c) -> p k c", k=KVT),
                                    lown[:, QT:QT + KVT].unsqueeze(2).to_broadcast([P, KVT, P]), ALU.mult)
                    V.tensor_copy(kpeT[HD:QKD, tok], ps[HD:QKD, QL + KVL:QL + KVL + P])\
                        .then_inc(freed[PAIR_OF[("lowt", t)]], 1)

                dve.wait_ge(small_in, 80)
                for s in range(2):
                    dve.wait_ge(mod_stored[s], 16 * NMOD // 2)
                for t in range(TT):
                    dve.wait_ge(low_sq, t + 1)
                    V.tensor_scalar(rs2[:, 2 * t:2 * t + 1], ss2[:, 2 * t:2 * t + 1], 1.0 / QL, EPS, ALU.mult, ALU.add)
                    V.tensor_scalar(rs2[:, 2 * t + 1:2 * t + 2], ss2[:, 2 * t + 1:2 * t + 2], 1.0 / KVL, EPS,
                                    ALU.mult, ALU.add).then_inc(low_ms, 1)
                    dve.wait_ge(low_root, t + 1)
                    link(V.reciprocal(rstd2[:, 2 * t:2 * t + 2], rs2[:, 2 * t:2 * t + 2]))
                    await_read(dve, ("low", t))
                    tm = ltm[:, t % 2, :]
                    V.tensor_scalar(tm[:, 0:QL], tm[:, 0:QL], rstd2[:, 2 * t:2 * t + 1], None, ALU.mult)
                    last = V.tensor_scalar(tm[:, QL:QL + KVL], tm[:, QL:QL + KVL], rstd2[:, 2 * t + 1:2 * t + 2],
                                           None, ALU.mult)
                    if t:
                        kp = tm[:, QL + KVL:LOW]
                        k4 = kp.rearrange("p (a j f) -> p a j f", a=2, j=2)
                        s4 = const("sin")[:, (t - 1) * RD:t * RD].rearrange("p (a j f) -> p a j f", a=2, j=2)
                        r4 = rot.rearrange("p (a j f) -> p a j f", a=2, j=2)
                        V.tensor_tensor(r4[:, :, 0, :], k4[:, :, 1, :], s4[:, :, 0, :], ALU.mult)
                        link(V.tensor_tensor(r4[:, :, 1, :], k4[:, :, 0, :], s4[:, :, 1, :], ALU.mult))
                        link(V.tensor_tensor(kp, kp, const("cos")[:, (t - 1) * RD:t * RD], ALU.mult))
                        last = V.tensor_tensor(kp, kp, rot, ALU.add)
                    last.then_inc(low_scaled, 1)
                    if t:
                        low_transposed(t - 1)
                low_transposed(TT - 1)

                units = attention_steps()

                def attention(kind, base):
                    def maxima(i):
                        h, t = units[i]
                        ps = await_job(dve, (kind + "s", i))
                        if kind == "na" and t:
                            if i >= 3:
                                await_job(dve, (kind + "t", i - 3))
                            r0 = 6 - 2 * (t - 1)
                            V.tensor_tensor_reduce(probs[i % 3][:, 0:N_LAT], ps[:, MID:MID + N_LAT],
                                                   tb[:, h, r0 * GW:r0 * GW + N_LAT], 1.0, LEAST,
                                                   ALU.add, ALU.max, mxs[i % 2][:, 0:1])
                            V.tensor_scalar(probs[i % 3][:, N_LAT:T], ps[:, MID + N_LAT:MID + T], 1.0, LEAST,
                                            ALU.mult, ALU.max, accum_out=mxs[i % 2][:, 1:2])\
                                .then_inc(freed[PAIR_OF[(kind + "s", i)]], 1)
                            await_read(dve, (kind + "s", i))
                            V.tensor_scalar(negms[i % 3], mxs[i % 2][:, 0:1], mxs[i % 2][:, 1:2], -1.0,
                                            ALU.max, ALU.mult).then_inc(biased, 1)
                        else:
                            n = T if t else P
                            link(V.reduce_max(mxs[i % 2][:, 0:1], ps[:, MID:MID + n], AX_X))
                            V.tensor_scalar(negms[i % 3], mxs[i % 2][:, 0:1], -1.0 if kind == "na" else -QKD ** -0.5,
                                            None, ALU.mult).then_inc(biased, 1)

                    def normalise(i):
                        n = T if units[i][1] else P
                        h, t = units[i]
                        if kind == "na" and t:
                            dve.wait_ge(exped, h * (TT - 1) + t)
                        else:
                            await_read(dve, (kind + "s", i))
                        inv = rinv[:, i % 2:i % 2 + 1]
                        link(V.reciprocal(inv, rsums[i % 3]))
                        V.tensor_scalar(probs[i % 3][:, 0:n], probs[i % 3][:, 0:n], inv, None, ALU.mult)\
                            .then_inc(scaled, 1)

                    for i in range(len(units) + LAG_PV):
                        if i < len(units):
                            maxima(i)
                        if 0 <= i - 1 < len(units):
                            normalise(i - 1)
                        done = i - LAG_PV
                        if done >= 0 and done % (2 * TT) == 2 * TT - 1:
                            m = done // (2 * TT)
                            n = 1 if kind == "na" else 2
                            dve.wait_ge(pv_done, base + done + 1)
                            if n == 2 and m == 0:
                                dve.wait_ge(pooled, NM)
                            V.tensor_copy(yT[n][:, m, :], opair[:, 0:T]).then_inc(o_freed, 1)

                dve.wait_ge(bias_masked, 1)
                attention("na", 0)
                for h in range(NH):
                    ps = await_job(dve, ("qm", h))
                    lat = slice(MID + N_CTX, MID + T)
                    V.tensor_copy(qT[0:QKD, h, 0:N_CTX], ps[0:QKD, MID:MID + N_CTX])
                    V.tensor_copy(qT[0:HD, h, N_CTX:T], ps[0:HD, lat])
                    V.tensor_tensor(qT[HD:QKD, h, N_CTX:T], ps[HD:QKD, lat], const("rope")[HD:QKD], ALU.mult)
                    V.tensor_tensor(swapped[HD:QKD], ps[QKD:P, lat], const("rope")[QKD:P], ALU.mult)\
                        .then_inc(freed[PAIR_OF[("qm", h)]], 1)
                    await_read(dve, ("qm", h))
                    V.tensor_tensor(qT[HD:QKD, h, N_CTX:T], qT[HD:QKD, h, N_CTX:T], swapped[HD:QKD], ALU.add)\
                        .then_inc(q_ready, 1)
                    dve.wait_ge(q_ready, h + 1)
                attention("ml", len(units))

                for i, (m, n) in enumerate(MERGE):
                    ps = await_job(dve, ("branch", m, n))
                    await_read(dve, ("gate", m, n))
                    out = mergedT[:, m, :] if n == 0 else prod[:, i % 2, :]
                    V.tensor_tensor(out, ps[:, MID:MID + T], sig[:, i % 2, :], ALU.mult)\
                        .then_inc(freed[PAIR_OF[("branch", m, n)]], 1)
                    if n:
                        await_read(dve, ("branch", m, n))
                        ins = V.tensor_tensor(mergedT[:, m, :], mergedT[:, m, :], prod[:, i % 2, :], ALU.add)
                        if n == 2:
                            ins.then_inc(merged, 1)

                def inverse_root(t, count):
                    dve.wait_ge(sq3, count)
                    V.tensor_scalar(rs[:, t:t + 1], ss[:, t:t + 1], 1.0 / D, EPS, ALU.mult, ALU.add).then_inc(ms3, 1)
                    dve.wait_ge(root3, count)
                    link(V.reciprocal(rstd[:, t:t + 1], rs[:, t:t + 1]))

                dve.wait_ge(gb_in, 32)
                dve.wait_ge(x2_in, 16)
                for t in range(TT):
                    inverse_root(t, t + 1)
                    V.scalar_tensor_tensor(out=yb[:, t % 2, :], in0=pair[PAIR_OF[("y", t)]][:, :], scalar=rstd[:, t:t + 1],
                                           in1=gb1[:, min(t, 1), :], op0=ALU.mult, op1=ALU.mult)\
                        .then_inc(freed[PAIR_OF[("y", t)]], 1)
                    await_read(dve, ("y", t))
                    V.tensor_tensor(x2[:, t, :], x2[:, t, :], yb[:, t % 2, :], ALU.add).then_inc(x2_new, 1)
                dve.wait_ge(bc2_in, 64)
                for t in range(TT):
                    inverse_root(t, TT + t + 1)
                    g = min(t, 1)
                    link(V.scalar_tensor_tensor(out=h2[:, t, :], in0=x2[:, t, :], scalar=rstd[:, t:t + 1],
                                                in1=bc2[:, 2 * g, :], op0=ALU.mult, op1=ALU.mult))
                    V.tensor_tensor(h2[:, t, :], h2[:, t, :], bc2[:, 2 * g + 1, :], ALU.add).then_inc(h2_ready, 1)
                for t in range(TT):
                    ps = await_job(dve, ("lg", t))
                    V.tensor_copy(lg[:, t, :], ps[:, 0:LG]).then_inc(freed[PAIR_OF[("lg", t)]], 1)
                await_read(dve, ("lg", TT - 1))

                def wide(v, n=EG):
                    return v.to_broadcast([P, TT, n])

                rev = const("rev").rearrange("p (t n) -> p t n", t=TT)

                def first_max(values, mark, top):
                    link(V.tensor_tensor(mark, values, wide(top), ALU.is_equal))
                    link(V.tensor_tensor(w4, mark, rev, ALU.mult))
                    link(V.reduce_max(big, w4, AX_X))
                    link(V.tensor_tensor(mark, w4, wide(big), ALU.is_equal))

                lgg = lg[:, :, 0:NG]
                link(V.reduce_max(gmax, lgg, AX_X))
                V.tensor_tensor(e4, lgg, wide(gmax), ALU.subtract).then_inc(routed_a, 1)
                first_max(lgg, oh_g, gmax)
                g16 = [P, TT, NG, EG]
                v4 = "p t (g e) -> p t g e"
                link(V.tensor_tensor(ch1.rearrange(v4, g=NG), lg[:, :, NG:LG].rearrange(v4, g=NG),
                                     oh_g.unsqueeze(3).to_broadcast(g16), ALU.mult))
                link(V.tensor_reduce(el, ch1.rearrange("p t (g e) -> p t e g", g=NG), AX_X, ALU.add))
                link(V.reduce_max(m1, el, AX_X))
                first_max(el, oh1, m1)
                link(V.scalar_tensor_tensor(out=elm, in0=oh1, scalar=NEG, in1=el, op0=ALU.mult, op1=ALU.add))
                link(V.reduce_max(m2, elm, AX_X))
                first_max(elm, oh2, m2)
                V.tensor_tensor(m2, m2, m1, ALU.subtract).then_inc(routed_a, 1)
                V.tensor_tensor(ch1.rearrange(v4, g=NG), oh_g.unsqueeze(3).to_broadcast(g16),
                                oh1.unsqueeze(2).to_broadcast(g16), ALU.mult)
                link(V.tensor_tensor(ch2.rearrange(v4, g=NG), oh_g.unsqueeze(3).to_broadcast(g16),
                                     oh2.unsqueeze(2).to_broadcast(g16), ALU.mult))
                V.tensor_tensor(chs, ch1, ch2, ALU.add).then_inc(chosen, 1)
                dve.wait_ge(routed_b, 2)
                V.tensor_reduce(gsum, e4, AX_X, ALU.add)
                link(V.tensor_scalar(m1, m2, 1.0, None, ALU.add))
                link(V.tensor_tensor(gsum, gsum, m1, ALU.mult))
                link(V.reciprocal(gate1, gsum))
                link(V.tensor_tensor(gate2, gate1, m2, ALU.mult))
                ps = await_job(dve, ("cnt", 0))
                pos = ps[:, 0:TT * NE].rearrange("p (t n) -> p t n", t=TT)
                tot = ps[:, 128:128 + TT * NE].rearrange("p (t n) -> p t n", t=TT)
                V.tensor_copy(slots[:, 0, :], pos[:, 0, :])
                link(V.tensor_copy(n_e, tot[:, 0, :]))
                for t in range(1, TT):
                    link(V.tensor_tensor(slots[:, t, :], pos[:, t, :], n_e, ALU.add))
                    link(V.tensor_tensor(n_e, tot[:, t, :], n_e, ALU.add))
                link(V.tensor_scalar(blocks, n_e, 0.0, None, ALU.is_gt))
                for j in range(1, TT):
                    link(V.scalar_tensor_tensor(out=blocks, in0=n_e, scalar=float(j * BLOCK), in1=blocks,
                                                op0=ALU.is_gt, op1=ALU.add))
                link(V.tensor_tensor_scan(blk_end, ones[:, 0:NE], blocks, 0.0, ALU.mult, ALU.add))
                link(V.tensor_tensor(blk_start, blk_end, blocks, ALU.subtract))
                for t in range(TT):
                    last = V.scalar_tensor_tensor(out=slots[:, t, :], in0=blk_start, scalar=float(BLOCK),
                                                  in1=slots[:, t, :], op0=ALU.mult, op1=ALU.add)
                link(last)
                V.tensor_tensor(ch1, ch1, slots, ALU.mult)
                link(V.tensor_tensor(ch2, ch2, slots, ALU.mult))
                V.tensor_reduce(slot1, ch1, AX_X, ALU.add)
                link(V.tensor_reduce(slot2, ch2, AX_X, ALU.add))
                V.tensor_copy(slot_ids[:, 0:TT].unsqueeze(2), slot1)
                V.tensor_copy(slot_ids[:, TT:2 * TT].unsqueeze(2), slot2).then_inc(slots_ready, 1)
                link(V.tensor_tensor(bcmp, blk_end.unsqueeze(1).to_broadcast([P, NB, NE]),
                                     const("blk").unsqueeze(2).to_broadcast([P, NB, NE]), ALU.is_le))
                link(V.tensor_reduce(bexp, bcmp, AX_X, ALU.add))
                link(V.tensor_scalar(bexp, bexp, float(NE - 1), None, ALU.min))
                V.tensor_copy(blk_ids, bexp).then_inc(blocks_ready, 1)

                dve.sem_inc(t_freed, 1)
                dve.sem_inc(hid_ready, 2)

                def transposed(b, s):
                    dve.wait_ge(t_filled, b + 1)
                    V.tensor_copy(xgT[:, s, :], pair[0][:, :]).then_inc(t_freed, 1)

                def hidden(b, s):
                    dve.wait_ge(sil_ready, b + 1)
                    V.tensor_tensor(hid[:, s, :], sil[:, s, :], pair[1][:, s * 512 + FF:s * 512 + 2 * FF], ALU.mult)\
                        .then_inc(hid_ready, 1)

                transposed(0, 0)
                with dve.Fori(0, NB // 2 - 1) as it:
                    hidden(it * 2, 0)
                    transposed(it * 2 + 1, 1)
                    hidden(it * 2 + 1, 1)
                    transposed(it * 2 + 2, 0)
                hidden(NB - 2, 0)
                transposed(NB - 1, 1)
                hidden(NB - 1, 1)

                dve.wait_ge(gb_in, 64)
                for t in range(TT):
                    s = t % 2
                    a, b = picks[:, 2 * s, :], picks[:, 2 * s + 1, :]
                    dve.wait_ge(picked[s], L * PICKS[s] + 32 * (t // 2 + 1))
                    link(V.tensor_scalar(a, a, gate1[:, t, :], None, ALU.mult))
                    V.scalar_tensor_tensor(out=a, in0=b, scalar=gate2[:, t, :], in1=a, op0=ALU.mult, op1=ALU.add)\
                        .then_inc(mixed, 1)
                    inverse_root(t, 2 * TT + t + 1)
                    link(V.scalar_tensor_tensor(out=a, in0=a, scalar=rstd[:, t:t + 1], in1=gb2[:, min(t, 1), :],
                                                op0=ALU.mult, op1=ALU.mult))
                    V.tensor_tensor(x2[:, t, :], x2[:, t, :], a, ALU.add).then_inc(x2_new, 1)
                dve.wait_ge(x2_new, 2 * TT)
                dve.sem_inc(layer_done, 1)
                dve.wait_ge(go["dve"], 1)
                dve.sem_clear(go["dve"])

        @block.gpsimd
        def _(pool):
            G = nc.gpsimd
            G.memset(src_ids, 0).then_inc(ids_zeroed, 1)
            pool.wait_ge(ids_zeroed, 1)
            with nc.allow_non_contiguous_dma(reason="four-byte rows"):
                pool.dma_start(slot_token.rearrange("(b p) o -> p (b o)", p=P), src_ids).then_inc(list_zeroed, 16)
            pool.wait_ge(list_zeroed, 16)
            pool.wait_ge(consts_in, 16)
            with pool.Fori(0, DEPTH) as L:
                steps = [0]

                def link(ins):
                    ins.then_inc(pool_step, 1)
                    steps[0] += 1
                    pool.wait_ge(pool_step, steps[0])

                pool.wait_ge(bias_in, 32)
                tbr = r1[:, NQ_W:NQ_W + T_W].rearrange("p (r c) -> p r c", c=GW)
                G.tensor_tensor(tbr, tbr, const("mask").unsqueeze(1).to_broadcast([P, NH * DR, GW]), ALU.add)\
                    .then_inc(bias_masked, 1)

                await_read(pool, ("u", NM - 1))
                await_job(pool, ("xt", TT - 1))
                edge = const("edge").rearrange("p (g a b) -> p g a b", g=NM, a=2)
                for g, w in enumerate(POOL_W):
                    u = u_pad[:, g, :]
                    link(G.tensor_tensor(sum_a[:, 1:PADT], u[:, 0:PADT - 1], u[:, 1:PADT], ALU.add))
                    cur, nxt, lo, hi = sum_a, sum_b, 1, PADT
                    for d in (1, 2, 4)[:g]:
                        link(G.tensor_tensor(nxt[:, lo + d:hi - d], cur[:, lo:hi - 2 * d], cur[:, lo + 2 * d:hi], ALU.add))
                        cur, nxt, lo, hi = nxt, cur, lo + d, hi - d
                    link(G.tensor_scalar(nxt[:, C_AT:L_AT + N_LAT], cur[:, C_AT:L_AT + N_LAT], 1.0 / w, None, ALU.mult))
                    for i, (a, b) in enumerate(((C_AT, L_AT), (C_AT + N_CTX - 8, L_AT + N_LAT - 8))):
                        for c in (a, b):
                            ins = G.tensor_tensor(nxt[:, c:c + 8], nxt[:, c:c + 8], edge[:, g, i, :], ALU.mult)
                    link(ins)
                    G.tensor_tensor(u[:, C_AT:L_AT + N_LAT], nxt[:, C_AT:L_AT + N_LAT], u[:, C_AT:L_AT + N_LAT],
                                    ALU.subtract).then_inc(pooled, 1)
                    pool.wait_ge(pooled, g + 1)

                await_job(pool, ("vm", 0))
                await_read(pool, ("lowt", TT - 1))
                pool.wait_ge(caches_in, 64)
                for h in range(NH):
                    G.tensor_copy(kT[HD:QKD, h, :], kpeT[HD:QKD, :]).then_inc(kpe_copied, 1)

                pool.wait_ge(slots_ready, 1)
                for i in range(2 * TT):
                    pool.indirect_dma_start(slot_token, bass.IndirectOffsetOnAxis(ap=slot_ids[:, i:i + 1], axis=0),
                                            tok_ids[:, i % TT:i % TT + 1], None).then_inc(scattered, 16)
                pool.wait_ge(list_in, 16)
                pool.wait_ge(h2_stored, 16 * TT)
                for b in range(NB):
                    if b >= 2:
                        pool.wait_ge(t_filled, b - 1)
                    pool.indirect_dma_start(xg[:, b % 2, :], None, h2_rows,
                                            bass.IndirectOffsetOnAxis(ap=src_ids[:, b:b + 1], axis=0)).then_inc(xg_in[b % 2], 16)
                for s in range(2):
                    pool.wait_ge(yo_stored[s], 16 * (NB // 2 + 1))
                for t in range(TT):
                    if t >= 2:
                        pool.wait_ge(x2_new, TT + t - 1)
                    for k in range(2):
                        i = k * TT + t
                        pool.indirect_dma_start(picks[:, 2 * (t % 2) + k, :], None, expert_out,
                                                bass.IndirectOffsetOnAxis(ap=slot_ids[:, i:i + 1], axis=0))\
                            .then_inc(picked[t % 2], 16)
                for s in range(2):
                    pool.wait_ge(picked[s], L * PICKS[s] + PICKS[s])
                pool.sem_inc(layer_done, 1)
                pool.wait_ge(go["pool"], 1)
                pool.sem_clear(go["pool"])

        @block.tensor
        def _(pe):
            pe.wait_ge(cv_ready, 1)
            pe.wait_ge(consts_in, 16)
            with pe.Fori(0, DEPTH) as L:
                def chunk(key, k, n):
                    pe.wait_ge(landed[SLOT_OF[key]], 16 * FILL_OF[key])
                    return view(ring, SLOT_OF[key] * SLOT, k * n, k=k)

                def mm(out, lhsT, rhs, first, last):
                    return nc.tensor.matmul(out, lhsT, rhs, start=first, stop=last, skip_group_check=True)

                def channels(key, w, c0, kt, rhs, width, at_, rows=P):
                    ps = pair_for(pe, key)
                    half = width // 2
                    for j in range(2):
                        for k in range(kt):
                            last = mm(ps[0:rows, at_ + j * half:at_ + (j + 1) * half], w[:, k, c0:c0 + rows],
                                      rhs[:, k, j * half:(j + 1) * half], k == 0, k == kt - 1)
                    last.then_inc(filled[PAIR_OF[key]], 1)

                def tokens(key, parts, kt, lhs, t):
                    ps = pair_for(pe, key)
                    for w, a, n in parts:
                        for k in range(kt):
                            last = mm(ps[:, a:a + n], lhs[:, k, t * P:(t + 1) * P], w[:, k, :], k == 0, k == kt - 1)
                    last.then_inc(filled[PAIR_OF[key]], 1)

                def turned(key, pieces):
                    ps = pair_for(pe, key)
                    for s, a in pieces:
                        last = nc.tensor.transpose(ps[0:s.shape[1], a:a + P], s, ident)
                    last.then_inc(filled[PAIR_OF[key]], 1)

                for j in range(NMOD):
                    w = chunk(("mod", j), KD, 512)
                    ps = pair_for(pe, ("mod", j))
                    for k in range(KD):
                        last = mm(ps[0:2, 0:512], cvec[:, k, :], w[:, k, :], k == 0, k == KD - 1)
                    last.then_inc(filled[PAIR_OF[("mod", j)]], 1)
                for t in range(TT):
                    pe.wait_ge(h_ready, t + 1)
                    turned(("xt", t), [(hb[:, t % 2, k * P:(k + 1) * P], k * P) for k in range(KD)])
                await_read(pe, ("xt", TT - 1))
                w = chunk(("nk",), KD, 512)
                for m in range(NM):
                    channels(("nk", m), w, m * P, KD, h_t, T, MID)
                w = chunk(("nv",), KD, 512)
                for t in range(TT):
                    tokens(("nv", t), [(w, 0, 512)], KD, h_t, t)
                w = chunk(("nq",), KD, 512)
                for m in range(NM):
                    channels(("nq", m), w, m * P, KD, h_t, T, MID)
                w = chunk(("u",), KD, 512)
                for m in range(NM):
                    channels(("u", m), w, m * P, KD, h_t, T, MID)
                wa, wb = chunk(("low", 0), KD, LOW // 2), chunk(("low", 1), KD, LOW // 2)

                def low_transposes(t):
                    pe.wait_ge(low_scaled, t + 1)
                    tm = ltm[:, t % 2, :]
                    pieces = [(tm[:, k * P:(k + 1) * P], k * P) for k in range(QT + KVT)]
                    pieces.append((tm[:, QL + KVL - HD:LOW], QL + KVL))
                    turned(("lowt", t), pieces)

                for t in range(TT):
                    tokens(("low", t), [(wa, LMID, LOW // 2), (wb, 512, LOW // 2)], KD, h_t, t)
                    if t:
                        low_transposes(t - 1)
                low_transposes(TT - 1)

                units = attention_steps()

                def attention(kind, base):
                    n_pairs = NM * (kind == "ml")

                    def scores(i):
                        h, t = units[i]
                        ps = pair_for(pe, (kind + "s", i))
                        if kind == "na":
                            m, p0 = h // 2, HD * (h % 2)
                            q, k = nqT[p0:p0 + HD, m, t * P:(t + 1) * P], nkT[p0:p0 + HD, m, :]
                        else:
                            q, k = qT[0:QKD, h, t * P:(t + 1) * P], kT[0:QKD, h, :]
                        if t == 0:
                            last = mm(ps[:, MID:MID + P], q, k[:, 0:P], True, True)
                        else:
                            for j in range(2):
                                last = mm(ps[:, MID + j * (T // 2):MID + (j + 1) * (T // 2)], q,
                                          k[:, P + j * (T // 2):P + (j + 1) * (T // 2)], True, True)
                        last.then_inc(filled[PAIR_OF[(kind + "s", i)]], 1)

                    def transposes(i):
                        pe.wait_ge(scaled, base + i + 1)
                        n = TT if units[i][1] else 1
                        ps = pair_for(pe, (kind + "t", i))
                        for j in range(n):
                            last = nc.tensor.transpose(ps[:, j * P:(j + 1) * P], probs[i % 3][:, j * P:(j + 1) * P], ident)
                        last.then_inc(filled[PAIR_OF[(kind + "t", i)]], 1)

                    def values(i):
                        h, t = units[i]
                        await_read(pe, (kind + "t", i))
                        v = nv if kind == "na" else vm
                        p0, m = HD * (h % 2), n_pairs + h // 2
                        if i % (2 * TT) == 0 and m:
                            pe.wait_ge(o_freed, m)
                        keys = range(1, KT) if t else range(0, 1)
                        for j, kt in enumerate(keys):
                            last = mm(opair[p0:p0 + HD, t * P:(t + 1) * P], v[:, kt, h * HD:(h + 1) * HD],
                                      probT[i % 2][:, j * P:(j + 1) * P], j == 0, j == len(keys) - 1)
                        last.then_inc(pv_done, 1)

                    for i in range(len(units) + LAG_PV):
                        if i < len(units):
                            scores(i)
                        if 0 <= i - LAG_PT < len(units):
                            transposes(i - LAG_PT)
                        if 0 <= i - LAG_PV < len(units):
                            values(i - LAG_PV)

                pe.wait_ge(caches_in, 64)
                await_read(pe, ("u", NM - 1))
                attention("na", 0)
                await_read(pe, ("lowt", TT - 1))
                w = chunk(("ukv",), KVT, 1024)
                for t in range(KT):
                    tokens(("vm", t), [(w[:, :, 512:1024], 0, 512)], KVT, ckvT, t)
                for h in range(NH):
                    channels(("kn", h), w, h * HD, KVT, ckvT, KEYS, KMID, rows=HD)
                w = chunk(("uq",), QT, 1024)
                for h in range(NH):
                    channels(("qm", h), w, h * P, QT, cqT, T, MID)
                await_read(pe, ("kn", NH - 1))
                pe.wait_ge(q_ready, NH)
                pe.wait_ge(kpe_copied, NH)
                attention("ml", len(units))

                pe.wait_ge(small_in, 80)
                pe.wait_ge(pooled, NM)
                for g in range(NM):
                    ps = pair_for(pe, ("pool", g))
                    wg = wpool_sb[:, g * P:(g + 1) * P]
                    mm(ps[:, 1024 - T:512], wg, u_pad[:, g, C_AT:C_AT + N_CTX], True, True)
                    mm(ps[:, 512:1024], wg, u_pad[:, g, L_AT:L_AT + N_LAT], True, True)\
                        .then_inc(filled[PAIR_OF[("pool", g)]], 1)
                for m, n in MERGE:
                    if m % 4 == 0:
                        wg = chunk(("gate", m // 4, n), KD, 512)
                        wb = chunk(("branch", m // 4, n), NM, 512)
                    channels(("gate", m, n), wg, (m % 4) * P, KD, h_t, T, MID)
                    if n == 0 and m == 0:
                        await_read(pe, ("pool", NM - 1))
                    if n == 2 and m == 0:
                        pe.wait_ge(o_freed, 2 * NM)
                    channels(("branch", m, n), wb, (m % 4) * P, NM, yT[n], T, MID)
                pe.wait_ge(merged, KD)
                wa, wb = chunk(("out", 0), KD, 512), chunk(("out", 1), KD, 512)
                for t in range(TT):
                    tokens(("y", t), [(wa, 0, 512), (wb, 512, 512)], KD, mergedT, t)
                for t in range(TT):
                    pe.wait_ge(h2_ready, t + 1)
                    turned(("ht", t), [(h2[:, t, k * P:(k + 1) * P], k * P) for k in range(KD)])
                    await_read(pe, ("ht", t))
                    ps = pair_for(pe, ("lg", t))
                    for k in range(KD):
                        last = mm(ps[:, 0:LG], h2T[:, t % 2, k * P:(k + 1) * P], router_sb[:, k * LG:(k + 1) * LG],
                                  k == 0, k == KD - 1)
                    last.then_inc(filled[PAIR_OF[("lg", t)]], 1)
                pe.wait_ge(chosen, 1)
                ps = pair_for(pe, ("cnt", 0))
                cf = chs.rearrange("p t n -> p (t n)")
                mm(ps[:, 0:TT * NE], tri, cf, True, True)
                mm(ps[:, 128:128 + TT * NE], ones, cf, True, True).then_inc(filled[PAIR_OF[("cnt", 0)]], 1)

                pe.sem_inc(h_filled, 2)
                pe.sem_inc(y_filled, 2)
                pe.wait_ge(slots_ready, 1)

                def gathered(b, s, rnd):
                    pe.wait_ge(xg_in[s], L * (16 * (NB // 2)) + (rnd * 16 + 16))
                    pe.wait_ge(t_freed, b + 1)
                    for k in range(KD):
                        last = nc.tensor.transpose(pair[0][:, k * P:(k + 1) * P], xg[:, s, k * P:(k + 1) * P], ident)
                    last.then_inc(t_filled, 1)

                def up(b, s, rnd):
                    pe.wait_ge(up_in[s], rnd * 32 + 32)
                    pe.wait_ge(t_freed, b + 2)
                    pe.wait_ge(hid_ready, b + 1)
                    for j in range(2 * FT):
                        w = w13[s][:, (j // FT) * 2048:(j // FT + 1) * 2048].rearrange("p (k f) -> p k f", k=KD)
                        for k in range(KD):
                            last = mm(pair[1][:, s * 512 + j * P:s * 512 + (j + 1) * P],
                                      w[:, k, (j % FT) * P:(j % FT + 1) * P], xgT[:, s, k * P:(k + 1) * P],
                                      k == 0, k == KD - 1)
                    last.then_inc(h_filled, 1)

                def down(b, s, rnd):
                    pe.wait_ge(down_in[s], rnd * 16 + 16)
                    pe.wait_ge(hid_ready, b + 3)
                    pe.wait_ge(y_read, b + 1)
                    out = (pair[2], opair)[s]
                    for j in range(2):
                        for k in range(FT):
                            last = mm(out[:, j * 512:(j + 1) * 512], hid[:, s, k * P:(k + 1) * P],
                                      w2s[s][:, k * D + j * 512:k * D + (j + 1) * 512], k == 0, k == FT - 1)
                    last.then_inc(y_filled, 1)

                gathered(0, 0, 0)
                with pe.Fori(0, NB // 2 - 1) as it:
                    up(it * 2, 0, it)
                    gathered(it * 2 + 1, 1, it)
                    down(it * 2, 0, it)
                    up(it * 2 + 1, 1, it)
                    gathered(it * 2 + 2, 0, it + 1)
                    down(it * 2 + 1, 1, it)
                rnd = NB // 2 - 1
                up(NB - 2, 0, rnd)
                gathered(NB - 1, 1, rnd)
                down(NB - 2, 0, rnd)
                up(NB - 1, 1, rnd)
                down(NB - 1, 1, rnd)
                pe.wait_ge(y_filled, NB + 2)
                pe.sem_inc(layer_done, 1)
                pe.wait_ge(go["pe"], 1)
                pe.sem_clear(go["pe"])


def kernel(**inputs):
    import numpy as np
    import concourse.bacc as bacc
    from concourse import mybir as mb
    from concourse.bass_utils import run_bass_kernel_spmd

    a = {k: np.asarray(v) for k, v in inputs.items()}
    f = np.float32
    ar = {}
    ar["x0"] = np.concatenate([a["x_prompt"][0], a["x_sample"][0]])
    ar["k_cache_t"] = a["cache_na_k"][0].reshape(DEPTH, N_CACHE, NH * HD).transpose(0, 2, 1)
    ar["v_cache"] = a["cache_na_v"][0].reshape(DEPTH, N_CACHE, NH * HD)
    ar["ckv_cache_t"] = a["cache_mla_ckv"][0].transpose(0, 2, 1)
    ar["kpe_cache_t"] = a["cache_mla_kpe"][0].transpose(0, 2, 1)
    ar["c_t"] = np.stack([a["c_ctx"], a["c"][0]]).reshape(2, KD, P).transpose(2, 1, 0).reshape(P, 2 * KD)
    ones = np.ones((DEPTH, D), f)
    gains = np.stack([ones, a["g_pre_mix"], a["g_post_mix"], ones, a["g_pre_ffn"], a["g_post_ffn"]], 1)
    aux = np.stack([a["b_mod"].reshape(DEPTH, NMOD, 512), gains.reshape(DEPTH, NMOD, 512)], 2).reshape(DEPTH, NMOD, 1, 1024)
    ar["mod_aux"] = np.concatenate([aux, aux], 2)
    ar["w_mod"], ar["w_in"], ar["w_pool"] = a["w_mod"], a["w_in"], a["w_pool"]
    ar["pool_scale"] = a["pool_scale"].reshape(DEPTH, NM, P).transpose(0, 2, 1)
    pad = GW - WIN
    wide = np.concatenate([np.zeros((DEPTH, NH, 15, pad), f), a["na_rpb"], np.zeros((DEPTH, NH, 15, pad), f)], -1)
    rows = np.stack([wide[..., GW - 1 - q:2 * GW - 1 - q] for q in range(GW)], 1)
    ar["rpb_rows"] = rows
    ar["q_norm"] = a["mla_q_norm"].reshape(DEPTH, QT, P).transpose(0, 2, 1)
    ar["kv_norm"] = a["mla_kv_norm"].reshape(DEPTH, KVT, P).transpose(0, 2, 1)
    uq = a["mla_w_uq"].reshape(DEPTH, QL, NH, QKD)
    rope = uq[..., HD:].reshape(DEPTH, QL, NH, 2, 2, RD // 4)
    ar["w_uq"] = np.concatenate([uq, rope[..., ::-1, :].reshape(DEPTH, QL, NH, RD)], -1).reshape(DEPTH, QL, NH * P)
    ukv = a["mla_w_ukv"].reshape(DEPTH, KVL, NH, 2, HD)
    ar["w_ukv"] = ukv.transpose(0, 1, 3, 2, 4).reshape(DEPTH, KVL, 2 * NH * HD)
    ar["w_branch"], ar["w_out"] = a["w_branch"], a["w_out"]
    ar["w_router"] = np.concatenate([a["w_group_router"], a["w_expert_router"]], -1)
    ar["w_gate"] = a["w_exp_gate"].reshape(DEPTH * NE, D, FF)
    ar["w_up"] = a["w_exp_up"].reshape(DEPTH * NE, D, FF)
    ar["w_down"] = a["w_exp_down"].reshape(DEPTH * NE, FF, D)

    p = np.arange(P)
    c0 = np.clip(np.arange(GW) - WIN // 2, 0, GW - WIN)
    kc = np.arange(GW)
    mask = np.where((kc[None] >= c0[:, None]) & (kc[None] < c0[:, None] + WIN), 0.0, NEG)
    nf = RD // 4
    inv = 10000.0 ** (-np.arange(nf, dtype=f) / nf)
    tok = np.arange(N_LAT)
    ang = np.stack([(tok // GW)[:, None] * inv, (tok % GW)[:, None] * inv], 1).astype(f)
    cos = np.stack([np.cos(ang)] * 2, 2).reshape(N_LAT, RD)
    sin = np.stack([-np.sin(ang), np.sin(ang)], 2).reshape(N_LAT, RD)
    ropes = np.zeros((P, N_LAT))
    ropes[HD:QKD], ropes[QKD:P] = cos.T, sin.T
    tiled = {
        "ident": np.eye(P), "tri": p[:, None] < p[None], "ones": np.ones((P, P)), "mask": np.concatenate([mask, mask]),
        "rope": ropes,
        "cos": cos.reshape(4, P, RD).transpose(1, 0, 2).reshape(P, 4 * RD),
        "sin": sin.reshape(4, P, RD).transpose(1, 0, 2).reshape(P, 4 * RD),
        "rev": np.tile(np.arange(EG, 0, -1), (P, TT)),
        "tok": np.arange(TT)[None] * P + p[:, None], "blk": np.tile(np.arange(NB), (P, 1)),
    }
    n = 64
    t = np.concatenate([np.arange(8), np.arange(n - 8, n)])
    tiled["edge"] = np.tile(np.concatenate([w / (np.clip(t + w - w // 2, 0, n) - np.clip(t - w // 2, 0, n)) for w in POOL_W]), (P, 1))
    ar["consts"] = np.concatenate([tiled[n].astype(f) for n, _ in CONST_COLS], 1)

    outs = {"x_res": (T, D), "o_nk_t": (DEPTH, NH * HD, N_CTX), "o_nv": (DEPTH, N_CTX, NH * HD),
            "o_ckv_t": (DEPTH, KVL, N_CTX), "o_kpe": (DEPTH, N_CTX, RD)}
    nc = bacc.Bacc("TRN2", target_bir_lowering=False, num_devices=1)
    arrays, args = {}, {}
    for name, v in ar.items():
        v = np.ascontiguousarray(v)
        arrays["in_" + name] = v
        args[name] = nc.dram_tensor("in_" + name, v.shape, mb.dt.from_np(v.dtype), kind="ExternalInput").ap()
    for name, shape in outs.items():
        args[name] = nc.dram_tensor("out_" + name, shape, mb.dt.float32, kind="ExternalOutput").ap()
    bass_hybrid_step(nc, **args)
    r = run_bass_kernel_spmd(nc, [arrays], core_ids=[0]).results[0]
    x = r["out_x_res"]
    return (x[None, :N_CTX], x[None, N_CTX:],
            r["out_o_nk_t"].transpose(0, 2, 1).reshape(1, DEPTH, N_CTX, NH, HD),
            r["out_o_nv"].reshape(1, DEPTH, N_CTX, NH, HD),
            r["out_o_ckv_t"].transpose(0, 2, 1)[None], r["out_o_kpe"][None])
```

```python
import concourse.bass as bass
from concourse import mybir
from contextlib import ExitStack

F32 = mybir.dt.float32
F32R = mybir.dt.float32r
U32 = mybir.dt.uint32
ALU = mybir.AluOpType
ACT = mybir.ActivationFunctionType
AX_X = mybir.AxisListType.X
ds = bass.ds

P = 128
D = 1024
KD = D // P
N_CTX, N_LAT = 128, 512
T = N_CTX + N_LAT
TT = T // P
N_CACHE = 128
KEYS = T + N_CACHE
KT = KEYS // P
DEPTH = 2
GW = 64
ROWS = N_LAT // GW
WIN = 16
NH, HD = 8, 64
NM = NH * HD // P
RD = 32
QKD = HD + RD
QL, KVL = 384, 256
QT, KVT = QL // P, KVL // P
LOW = QL + KVL + RD
MOD = 6 * D
NMOD = MOD // 512
EPS = 1e-6
NG, EG = 4, 4
NE = NG * EG
FF = 256
FT = FF // P
DR = 14
POOL_W = (2, 4, 8, 16)
PADT = 8 + N_CTX + 16 + N_LAT + 8
C_AT, L_AT = 8, 8 + N_CTX + 16
BLOCK = P
NB = (2 * T + NE * (BLOCK - 1)) // BLOCK
NB += NB % 2
NEG = -1e30
LEAST = -3e38

U_AT, NQ_AT, NK_AT, NV_AT, LOW_AT, G_AT = 0, 512, 1024, 1536, 2048, 2048 + LOW

NPAIR = 3
NSLOT = 3
SLOT = 4096
LAG_PT, LAG_PV = 2, 3


def attention_steps():
    return [(h, t) for h in range(NH) for t in range(TT)]


MERGE = [(m, n) for c in range(2) for n in range(3) for m in range(4 * c, 4 * c + 4)]

CONST_COLS = [("ident", P), ("tri", P), ("ones", P), ("mask", GW), ("rope", N_LAT), ("cos", 4 * RD), ("sin", 4 * RD),
              ("rev", TT * EG), ("tok", TT), ("blk", NB), ("edge", 4 * 16)]


MODS = [(j, 0) for j in range(4, NMOD)] + [(j, 1) for j in range(4)]
N_IN = 6
MOD_AT = {("na", 1, 0): 0, ("na", 3, 0): 1, ("na", 5, 0): 2, ("na", 7, 0): 3, ("ml", 1, 0): 4, ("ml", 3, 0): 5}
TAIL = [("y", 0), ("y", 1), ("ht", 0), ("y", 2), ("lg", 0), ("ht", 1), ("y", 3), ("lg", 1), ("ht", 2), ("y", 4),
        ("lg", 2), ("ht", 3), ("mod", 6), ("lg", 3), ("ht", 4), ("mod", 7), ("lg", 4), ("mod", 8), ("mod", 9),
        ("cnt", 0), ("mod", 10), ("mod", 11)]


def mod_before(n):
    return n - 1 if n < N_IN else n - 2 if n >= N_IN + 2 else None


def plan_jobs():
    jobs = [("xt", t) for t in range(TT)]
    jobs += [("nk", m) for m in range(NM)] + [("nv", a, t) for a in range(2) for t in range(TT)]
    jobs += [("nq", m) for m in range(NM)] + [("u", m) for m in range(NM)]
    for t in range(TT):
        jobs.append(("low", t))
        if t:
            jobs.append(("lowt", t - 1))
    jobs.append(("lowt", TT - 1))

    def attention(kind):
        units = attention_steps()
        for i in range(len(units) + LAG_PV):
            if i < len(units):
                jobs.append((kind + "s", i))
                if (kind, *units[i]) in MOD_AT:
                    jobs.append(("mod", MOD_AT[(kind, *units[i])]))
            if 0 <= i - LAG_PT < len(units):
                jobs.append((kind + "t", i - LAG_PT))

    attention("na")
    jobs += [("vm", t) for t in range(KT)] + [("kn", h) for h in range(NH)] + [("qm", h) for h in range(NH)]
    attention("ml")
    jobs += [("pool", g) for g in range(NM)]
    for m, n in MERGE:
        jobs += [("gate", m, n), ("branch", m, n)]
    return jobs + TAIL


HALVES = [(("nk",), a, ("nk", 2 * a + 1)) for a in range(2)] + [(("nv",), a, ("nv", a, TT - 1)) for a in range(2)]
HALVES += [((kind,), a, (kind, 2 * a + 1)) for kind in ("nq", "u") for a in range(2)]
N_WIN = len(HALVES)
HALVES += [(("gate", c, n), a, ("gate", 4 * c + 2 * a + 1, n)) for c in range(2) for n in range(3) for a in range(2)]
HALF_OF = {(key, a): i for i, (key, a, _) in enumerate(HALVES)}


def plan_chunks():
    def mods(a, b):
        return [(("mod", n), ("mod", n)) for n in range(a, b)]

    chunks = [((kind,), None) for kind in ("nk", "nv", "nq", "u")]
    chunks += [(("low", 0), ("low", TT - 1)), (("low", 1), ("low", TT - 1))]
    chunks += mods(0, 4) + [(("ukv",), ("kn", NH - 1)), (("uq",), ("qm", NH - 1))] + mods(4, N_IN)
    for c in range(2):
        for n in range(3):
            chunks += [(("gate", c, n), None), (("branch", c, n), ("branch", 4 * c + 3, n))]
    chunks += [(("out", 0), ("y", TT - 1)), (("out", 1), ("y", TT - 1))] + mods(N_IN, NMOD)
    return chunks


def bass_hybrid_step(nc, x0, k_cache_t, v_cache, ckv_cache_t, kpe_cache_t, c_t, mod_aux, w_mod, w_in, w_pool,
                     pool_scale, rpb_rows, q_norm, kv_norm, w_uq, w_ukv, w_branch, w_out, w_router,
                     w_gate, w_up, w_down, consts, zeros,
                     x_res, o_nk_t, o_nv, o_ckv_t, o_kpe):
    jobs, chunks = plan_jobs(), plan_chunks()
    PAIR_OF = {key: i % NPAIR for i, key in enumerate(jobs)}
    USE_OF = {key: i // NPAIR + 1 for i, key in enumerate(jobs)}
    SLOT_OF = {key: i % NSLOT for i, (key, _) in enumerate(chunks)}
    FILL_OF = {key: i // NSLOT + 1 for i, (key, _) in enumerate(chunks)}

    with ExitStack() as ctx:
        sems = []

        def sem(name):
            s = ctx.enter_context(nc.semaphore(name))
            sems.append(s)
            return s

        def sb(name, shape, dt=F32):
            return ctx.enter_context(nc.sbuf_tensor(name, shape, dt))

        def twins(name, n):
            with nc.sbuf_tensor(name + "_r", [P, n], F32R) as as_r:
                pass
            return sb(name, [P, n]), as_r

        ring = sb("ring", [P, NSLOT * SLOT])
        hT = sb("hT", [P, KD * T])
        ysT, ysT_r = twins("ysT", 2 * NM * T)
        NQ_W, T_W, NK_W, NV_W = NM * T, NH * DR * GW, NM * KEYS, KT * 512
        R1_W = NQ_W + T_W + NK_W + NV_W
        r1, r1_r = twins("r1", R1_W)
        PART = KD * 256
        mid, mid_r = twins("mid", 4 * PART)
        LOW_W = QT * T + KVT * KEYS
        assert LOW_W + KEYS + 2 * LOW + 4 * T <= 4 * PART
        u_sb = sb("u_sb", [P, NM * PADT])
        cst = sb("cst", [P, consts.shape[1]])
        small = sb("small", [P, 1000])
        wpool_sb = sb("wpool_sb", [P, NM * P])
        router_sb = sb("router_sb", [P, KD * (NG + NE)])
        cols = sb("cols", [P, 2 * KD + NM + QT + KVT + 4])
        ids = sb("ids", [P, 64], U32)

        def view(buf, at, n, **kw):
            v = buf[:, at:at + n]
            if kw:
                (name, size), = kw.items()
                v = v.rearrange(f"p ({name} z) -> p {name} z", **{name: size})
            return v

        low_t = view(mid, 0, LOW_W)
        kpeT = view(mid, LOW_W, KEYS)
        low_tm = view(mid, LOW_W + KEYS, 2 * LOW)
        pp = view(mid, LOW_W + KEYS + 2 * LOW, 4 * T)
        w_high = [view(mid_r, 2 * i * PART, PART, k=KD) for i in range(2)]
        w_low = [view(mid_r, (2 * i + 1) * PART, PART, k=KD) for i in range(2)]
        h_high, h_low = view(ysT_r, 0, TT * D, t=TT), view(r1_r, NQ_W, TT * D, t=TT)
        g_high, g_low = view(r1_r, 0, KD * T, k=KD), view(r1_r, KD * T, KD * T, k=KD)

        xt = view(ysT, 0, TT * D, t=TT)
        bc1 = [view(u_sb, 0, 2 * D, a=2),
               view(r1, NQ_W + T_W + NK_W, 2 * D, a=2)]
        hb = view(pp, 0, 2 * D, a=2)
        h_t = view(hT, 0, KD * T, k=KD)
        nqT = view(r1, 0, NQ_W, m=NM)
        tb = view(r1, NQ_W, T_W, h=NH)
        nkT = view(r1, NQ_W + T_W, NK_W, m=NM)
        nv = view(r1, NQ_W + T_W + NK_W, NV_W, t=KT)
        qT = view(r1, 0, NH * T, h=NH)
        kT = view(r1, NH * T, NH * KEYS, h=NH)
        vm = view(r1, NH * T + NH * KEYS, KT * 512, t=KT)
        assert NH * T + NH * KEYS + KT * 512 <= R1_W
        cqT = view(low_t, 0, QT * T, k=QT)
        ckvT = view(low_t, QT * T, KVT * KEYS, k=KVT)
        ltm = view(low_tm, 0, 2 * LOW, a=2)
        probs = [view(pp, 0, T), view(pp, T, T), view(low_tm, 0, T)]
        probT = [view(pp, 2 * T, T), view(pp, 3 * T, T)]
        yT = [None, view(ysT, 0, NM * T, m=NM), view(ysT, NM * T, NM * T, m=NM)]
        u_pad = view(u_sb, 0, NM * PADT, m=NM)
        sum_a = view(ysT, NM * T, PADT)
        sum_b = view(ysT, NM * T + PADT, PADT)
        mergedT = view(hT, 0, KD * T, k=KD)
        yT[0] = view(r1, 2 * KD * T, NM * T, m=NM)
        sig = view(r1, (2 * KD + NM) * T, 2 * T, a=2)
        prod = view(r1, (2 * KD + NM + 2) * T, 2 * T, a=2)
        x2 = view(r1, KD * T, TT * D, t=TT)
        gb1 = view(u_sb, 0, 2 * D, a=2)
        bc2 = view(r1, 0, 4 * D, a=4)
        yb = view(pp, 0, 2 * D, a=2)
        h2 = view(ysT, 0, TT * D, t=TT)
        h2T = view(low_t, 0, 2 * D, a=2)
        squares = view(r1, 4 * D, D)
        tail = (2 * KD + NM + 4) * T
        assert NH * T + NH * KEYS + KT * 512 + 1024 <= R1_W and tail + 512 <= R1_W
        aux_na, aux_ml = view(ysT, NM * T + 2 * PADT, 1024), view(r1, R1_W - 1024, 1024)
        st_in = view(low_tm, T, 512)
        aux = [aux_na] * 4 + [aux_ml] * 2 + [view(low_tm, 0, 1024), view(low_t, 2 * D, 1024)] * 3
        modst = [st_in] * N_IN + [view(r1, tail, 512), view(pp, 2 * D, 512)] * 3
        w13 = [view(ring, (1 - s) * 6144, 4096) for s in range(2)]
        w2s = [view(ring, (1 - s) * 6144 + 4096, 2048) for s in range(2)]
        pro_w = [view(ring, i * SLOT, SLOT, k=KD) for i in range(3)] + [view(r1, 0, SLOT, k=KD)]
        pro_aux = view(r1, SLOT, 4 * 1024, a=4)
        pro_st = view(r1, 2 * SLOT, 4 * 512, a=4)
        xg = view(r1, 0, 2 * D, a=2)
        xgT = view(r1, 2 * D, 2 * D, a=2)
        yo = view(r1, 10 * D, 2 * D, a=2)
        sil = view(r1, 12 * D, 2 * FF, a=2)
        hid = view(r1, 12 * D + 2 * FF, 2 * FF, a=2)
        gb2 = view(u_sb, 0, 2 * D, a=2)
        picks = [view(ysT, 2 * t * D, 2 * D, a=2) if t < 2 else view(r1, (0, 2, 10)[t - 2] * D, 2 * D, a=2) for t in range(TT)]
        assert 10 * D >= 2 * KD * T and 12 * D + 4 * FF <= R1_W

        at = 0
        where = {}
        for name, n in CONST_COLS:
            where[name] = (at, at + n)
            at += n

        def const(name):
            a, b = where[name]
            return cst[:, a:b]

        ident, tri, ones = const("ident"), const("tri"), const("ones")
        cvec = view(cols, 0, 2 * KD, k=KD)
        psc = cols[:, 2 * KD:2 * KD + NM]
        lown = cols[:, 2 * KD + NM:2 * KD + NM + QT + KVT]

        sm_at = [0]

        def sm(n):
            a = sm_at[0]
            sm_at[0] += n
            assert sm_at[0] <= 1000
            return small[:, a:a + n]

        ss, rs, rstd = sm(8), sm(8), sm(8)
        ss2, rs2, rstd2 = sm(12), sm(12), sm(12)
        mx, negm, rsum, rinv = sm(2), sm(1), sm(3), sm(2)
        mxs = [mx, sm(2)]
        negms = [negm] + [sm(1) for _ in range(2)]
        rsums = [rsum[:, i:i + 1] for i in range(3)]
        cvraw = sm(2 * KD)
        LG = NG + NE
        lg = sm(TT * LG).rearrange("p (t n) -> p t n", t=TT)

        def smt(n):
            return sm(TT * n).rearrange("p (t n) -> p t n", t=TT)

        gmax, gsum, gate1, gate2, m1, m2 = smt(1), smt(1), smt(1), smt(1), smt(1), smt(1)
        e4, oh_g, el, oh1, oh2, w4 = smt(4), smt(4), smt(4), smt(4), smt(4), smt(4)
        ch1, ch2, chs = smt(NE), smt(NE), smt(NE)
        slots = smt(NE)
        slot1, slot2 = smt(1), smt(1)
        elm, big = smt(4), smt(1)
        rot = sm(RD)
        swapped = view(low_tm, T, N_LAT)
        n_e, blocks, blk_end, blk_start = sm(NE), sm(NE), sm(NE), sm(NE)
        bexp, npair_f, halves = sm(NB), sm(1), sm(NB // 2)
        bcmp = view(pp, 0, NB * NE, a=NB)
        slot_ids = ids[:, 0:2 * TT]
        tok_ids = ids[:, 2 * TT:3 * TT]
        blk_ids = ids[:, 16:16 + NB]
        pair_count = ids[:, 16 + NB:17 + NB]
        src_id = [ids[:, 60:61], ids[:, 61:62]]
        src_ids = sb("src_ids", [P, NB], U32)[:, :]

        pair = [ctx.enter_context(nc.psum_tensor(f"pair{i}", [P, 1024], F32)) for i in range(NPAIR)]
        opair = ctx.enter_context(nc.psum_tensor("opair", [P, 1024], F32))
        MID = 512 - T // 2
        TMID = 512 - 2 * P
        KMID = 512 - KEYS // 2
        LMID = 512 - LOW // 2

        mod_rows = nc.dram_tensor("mod_rows", [2, MOD], F32).ap()
        h2_rows = nc.dram_tensor("h2_rows", [T, D], F32).ap()
        slot_token = nc.dram_tensor("slot_token", [NB * BLOCK, 1], U32).ap()
        expert_out = nc.dram_tensor("expert_out", [NB * BLOCK, D], F32).ap()

        consts_in, x_copied, ids_zeroed, list_zeroed, rows_zeroed, cv_in, cv_ready = (
            ctx.enter_context(nc.semaphore(n)) for n in ("consts_in", "x_copied", "ids_zeroed", "list_zeroed", "rows_zeroed", "cv_in", "cv_ready"))
        pro_in = [ctx.enter_context(nc.semaphore(f"pro_in{i}")) for i in range(4)]
        pro_aux_in, pro_filled, pro_step, pro_rows, pro_stored = (
            ctx.enter_context(nc.semaphore(n)) for n in ("pro_aux_in", "pro_filled", "pro_step", "pro_rows", "pro_stored"))
        layer_done = ctx.enter_context(nc.semaphore("layer_done"))
        go = {e: ctx.enter_context(nc.semaphore("go_" + e)) for e in ("pe", "act", "dve", "pool")}
        filled = [sem(f"filled{i}") for i in range(NPAIR)]
        freed = [sem(f"freed{i}") for i in range(NPAIR)]
        landed = [sem(f"landed{i}") for i in range(NSLOT)]
        aux_in = [sem(f"aux_in{i}") for i in range(2)]
        mod_row, bc_in, x_in = sem("mod_row"), sem("bc_in"), [sem(f"x_in{i}") for i in range(TT)]
        mod_stored = [sem(f"mod_stored{i}") for i in range(2)]
        bias_in, bias_masked, caches_in, small_in, kpe_in = (sem(n) for n in ("bias_in", "bias_masked", "caches_in", "small_in", "kpe_in"))
        pooled, pool_step, kpe_copied = (sem(n) for n in ("pooled", "pool_step", "kpe_copied"))
        dve_step, act_step = sem("dve_step"), sem("act_step")
        ms_ready, root_ready = sem("ms_ready"), sem("root_ready")
        sq_ready, h_ready = sem("sq_ready"), sem("h_ready")
        high_ready, parts_ready, h_high_ready, h_parts_ready, g_high_ready, g_parts_ready = (
            sem(n) for n in ("high_ready", "parts_ready", "h_high_ready", "h_parts_ready", "g_high_ready", "g_parts_ready"))
        low_sq, low_ms, low_root, low_scaled = sem("low_sq"), sem("low_ms"), sem("low_root"), sem("low_scaled")
        caches_out, kpe_out = sem("caches_out"), sem("kpe_out")
        q_ready = sem("q_ready")
        biased, exped, scaled, pv_done, o_freed = (sem(n) for n in ("biased", "exped", "scaled", "pv_done", "o_freed"))
        merged, x2_in, gb_in, bc2_in = sem("merged"), sem("x2_in"), sem("gb_in"), sem("bc2_in")
        x2_new, h2_ready, h2_stored = sem("x2_new"), sem("h2_ready"), sem("h2_stored")
        routed_a, routed_b, chosen, slots_ready, list_in, blocks_ready = (
            sem(n) for n in ("routed_a", "routed_b", "chosen", "slots_ready", "list_in", "blocks_ready"))
        scattered, id_ready, ran_on = sem("scattered"), sem("id_ready"), sem("ran_on")
        xg_in = [sem(f"xg_in{i}") for i in range(2)]
        picked = [sem(f"picked{i}") for i in range(TT)]
        up_in = [sem(f"up_in{i}") for i in range(2)]
        down_in = [sem(f"down_in{i}") for i in range(2)]
        t_filled, t_freed, h_filled, sil_ready, hid_ready, y_filled, y_read = (
            sem(n) for n in ("t_filled", "t_freed", "h_filled", "sil_ready", "hid_ready", "y_filled", "y_read"))
        yo_stored = [sem(f"yo_stored{i}") for i in range(2)]
        mixed, x_stored, sq3, ms3, root3 = (sem(n) for n in ("mixed", "x_stored", "sq3", "ms3", "root3"))

        def pair_for(eng, key):
            if USE_OF[key] > 1:
                eng.wait_ge(freed[PAIR_OF[key]], USE_OF[key] - 1)
            return pair[PAIR_OF[key]]

        def await_job(eng, key):
            eng.wait_ge(filled[PAIR_OF[key]], USE_OF[key])
            return pair[PAIR_OF[key]]

        def await_read(eng, key):
            eng.wait_ge(freed[PAIR_OF[key]], USE_OF[key])

        def half_source(eng, i):
            key, a, _ = HALVES[i]
            eng.wait_ge(landed[SLOT_OF[key]], 16 * FILL_OF[key])
            return view(ring, SLOT_OF[key] * SLOT, SLOT, k=KD)[:, :, a * 256:(a + 1) * 256]

        def await_mod_stored(eng, n):
            eng.wait_ge(mod_stored[n % 2], 16 * (n // 2 + 1))

        block = ctx.enter_context(nc.Block())

        @block.sync
        def _(sp):
            sp.dma_start(cst[:, :], consts).then_inc(consts_in, 16)
            sp.dma_start(cvraw, c_t).then_inc(cv_in, 16)
            for i in range(4):
                sp.dma_start(pro_w[i], w_mod[0, :, i * 512:(i + 1) * 512].rearrange("(k p) n -> p k n", p=P)).then_inc(pro_in[i], 16)
            sp.dma_start(pro_aux[0:2], mod_aux[0, 0:4].rearrange("b r n -> r b n")).then_inc(pro_aux_in, 16)
            sp.dma_start(x_res, x0).then_inc(x_copied, 16)
            sp.wait_ge(pro_rows, 4)
            sp.dma_start(mod_rows[:, 0:4 * 512].rearrange("r (b n) -> r b n", b=4), pro_st[0:2]).then_inc(pro_stored, 16)
            with sp.Fori(0, DEPTH) as L:
                def src(key):
                    kind = key[0]
                    wl = w_in[ds(L, 1)].rearrange("a (k p) n -> p (a k) n", p=P)
                    if kind == "mod":
                        j, ahead = MODS[key[1]]
                        w = w_mod[ds((L + ahead) % DEPTH, 1)].rearrange("a (k p) n -> p (a k) n", p=P)
                        return w[:, :, j * 512:(j + 1) * 512]
                    if kind in ("u", "nq", "nk", "nv"):
                        c0 = {"u": U_AT, "nq": NQ_AT, "nk": NK_AT, "nv": NV_AT}[kind]
                        return wl[:, :, c0:c0 + 512]
                    if kind == "low":
                        c0 = LOW_AT + key[1] * (LOW // 2)
                        return wl[:, :, c0:c0 + LOW // 2]
                    if kind == "ukv":
                        return w_ukv[ds(L, 1)].rearrange("a (k p) n -> p (a k) n", p=P)
                    if kind == "uq":
                        return w_uq[ds(L, 1)].rearrange("a (k p) n -> p (a k) n", p=P)
                    if kind == "gate":
                        c0 = G_AT + key[2] * D + key[1] * 512
                        return wl[:, :, c0:c0 + 512]
                    if kind == "branch":
                        w = w_branch[ds(L, 1)].rearrange("a n (k p) d -> p (a n k) d", p=P)
                        return w[:, 4 * key[2]:4 * key[2] + 4, key[1] * 512:(key[1] + 1) * 512]
                    w = w_out[ds(L, 1)].rearrange("a (k p) n -> p (a k) n", p=P)
                    return w[:, :, key[1] * 512:(key[1] + 1) * 512]

                stored = [0]

                def store_mods(upto):
                    while stored[0] <= upto:
                        n = stored[0]
                        j = MODS[n][0]
                        sp.wait_ge(mod_row, n + 1)
                        sp.dma_start(mod_rows[:, j * 512:(j + 1) * 512], modst[n][0:2]).then_inc(mod_stored[n % 2], 16)
                        stored[0] += 1

                sp.wait_ge(pro_stored, 16)
                for g in range(2):
                    for i, c0 in enumerate((D, 0)):
                        sp.dma_start(bc1[g][:, i, :], mod_rows[g:g + 1, c0:c0 + D].partition_broadcast(P)).then_inc(bc_in, 16)
                sp.wait_ge(x_in[TT - 1], 16)
                h2_out = h2_rows.rearrange("(t p) d -> p t d", p=P)
                for i, (key, _) in enumerate(chunks):
                    if i >= NSLOT:
                        before, last_reader = chunks[i - NSLOT]
                        if last_reader is None:
                            sp.wait_ge(parts_ready, HALF_OF[(before, 1)] + 1)
                        else:
                            await_job(sp, last_reader)
                        if before[0] == "mod":
                            store_mods(before[1])
                    if key[0] == "mod":
                        n = key[1]
                        j, ahead = MODS[n]
                        if mod_before(n) is not None:
                            store_mods(mod_before(n))
                        if n == 0:
                            await_job(sp, ("u", NM - 1))
                        if n == 4:
                            sp.wait_ge(o_freed, NM)
                        if n == N_IN:
                            store_mods(n - 1)
                            await_mod_stored(sp, n - 1)
                            await_job(sp, ("gate", KD - 1, 2))
                        sp.dma_start(aux[n][0:2], mod_aux[ds((L + ahead) % DEPTH, 1)][:, j:j + 1].rearrange("a b r n -> (a b r) n"))\
                            .then_inc(aux_in[n % 2], 16)
                    s = src(key)
                    k, n = s.shape[1], s.shape[2]
                    dst = view(ring, SLOT_OF[key] * SLOT, k * n, k=k)
                    sp.dma_start(dst, s).then_inc(landed[SLOT_OF[key]], 16)

                for t in range(TT):
                    sp.wait_ge(h2_ready, t + 1)
                    sp.dma_start(h2_out[:, t, :], h2[:, t, :]).then_inc(h2_stored, 16)
                sp.wait_ge(scattered, 32 * TT)
                with nc.allow_non_contiguous_dma(reason="four-byte rows"):
                    sp.dma_start(src_ids, slot_token.rearrange("(b p) o -> p (b o)", p=P)).then_inc(list_in, 16)
                sp.wait_ge(blocks_ready, 1)
                n_pairs = sp.value_load(pair_count[0:1], min_val=1, max_val=NB // 2)
                await_job(sp, ("mod", NMOD - 2))
                with sp.Fori(0, n_pairs) as it:
                    for s in range(2):
                        if s:
                            await_job(sp, ("mod", NMOD - 1))
                        e = sp.value_load(blk_ids[0:1, ds(it * 2 + s, 1)], min_val=0, max_val=NE - 1)
                        sp.wait_ge(h_filled, it * 2 + (s + 1))
                        for w, at_ in ((w_gate, 0), (w_up, 2048)):
                            sp.dma_start(w13[s][:, at_:at_ + 2048].rearrange("p (k f) -> p k f", k=KD),
                                         w[ds(L * NE + e, 1)].rearrange("a (k p) f -> p (a k) f", p=P)).then_inc(up_in[s], 16)
                        sp.wait_ge(y_filled, it * 2 + (s + 1))
                        sp.dma_start(w2s[s].rearrange("p (k f) -> p k f", k=FT),
                                     w_down[ds(L * NE + e, 1)].rearrange("a (k p) f -> p (a k) f", p=P)).then_inc(down_in[s], 16)
                store_mods(NMOD - 1)
                for n in (NMOD - 2, NMOD - 1):
                    await_mod_stored(sp, n)

                sp.wait_ge(layer_done, 4)
                for s in sems:
                    sp.sem_clear(s)
                sp.sem_clear(layer_done)
                for e in ("pe", "act", "dve", "pool"):
                    sp.sem_inc(go[e], 1)

        @block.scalar
        def _(act):
            act.wait_ge(cv_in, 16)
            nc.scalar.activation(cols[:, 0:2 * KD], cvraw, ACT.Silu).then_inc(cv_ready, 1)
            act.wait_ge(x_copied, 16)
            with act.Fori(0, DEPTH) as L:
                def layer(t):
                    return t[ds(L, 1)]

                steps = [0]

                def chain(ins):
                    ins.then_inc(act_step, 1)
                    steps[0] += 1
                    act.wait_ge(act_step, steps[0])

                for t in range(TT):
                    act.dma_start(xt[:, t, :], x_res[t * P:(t + 1) * P, :]).then_inc(x_in[t], 16)
                act.dma_start(cols[:, 2 * KD:2 * KD + NM], layer(pool_scale).rearrange("a p n -> p (a n)")).then_inc(small_in, 16)
                act.dma_start(lown[:, 0:QT], layer(q_norm).rearrange("a p n -> p (a n)")).then_inc(small_in, 16)
                act.dma_start(lown[:, QT:QT + KVT], layer(kv_norm).rearrange("a p n -> p (a n)")).then_inc(small_in, 16)
                act.dma_start(view(wpool_sb, 0, NM * P, g=NM), layer(w_pool).rearrange("a g c d -> c (a g) d")).then_inc(small_in, 16)
                act.dma_start(view(router_sb, 0, KD * LG, k=KD), layer(w_router).rearrange("a (k p) n -> p (a k) n", p=P)).then_inc(small_in, 16)
                def split_high(i):
                    if i >= 2:
                        await_job(act, HALVES[i - 2][2])
                    w = half_source(act, i)
                    nc.scalar.copy(w_high[i % 2], w).then_inc(high_ready, 1)

                for t in range(TT):
                    act.wait_ge(x_in[t], 16)
                    nc.scalar.activation(hT[:, t * D:(t + 1) * D], xt[:, t, :],
                                         ACT.Square, accum_out=ss[:, t:t + 1]).then_inc(sq_ready, 1)
                    act.wait_ge(ms_ready, t + 1)
                    nc.scalar.activation(rs[:, t:t + 1], rs[:, t:t + 1], ACT.Sqrt).then_inc(root_ready, 1)
                act.wait_ge(pro_stored, 16)
                act.dma_start(nkT[:, :, T:KEYS], layer(k_cache_t).rearrange("a (m p) t -> p (a m) t", p=P)).then_inc(caches_in, 16)
                act.dma_start(nv[:, KT - 1, :], layer(v_cache).rearrange("a p n -> p (a n)")).then_inc(caches_in, 16)
                for t in range(TT):
                    ps = await_job(act, ("xt", t))
                    nc.scalar.copy(h_high[:, t, :], ps[:, :]).then_inc(h_high_ready, 1)
                    nc.scalar.copy(h_t[:, :, t * P:(t + 1) * P], ps[:, :].rearrange("p (k c) -> p k c", k=KD))\
                        .then_inc(freed[PAIR_OF[("xt", t)]], 1)
                    if t == 2:
                        split_high(0)
                split_high(1)
                for m in range(NM):
                    ps = await_job(act, ("nk", m))
                    nc.scalar.copy(nkT[:, m, 0:T], ps[:, TMID:TMID + T]).then_inc(freed[PAIR_OF[("nk", m)]], 1)
                    if m % 2:
                        split_high(2 + m // 2)
                await_read(act, ("nk", NM - 1))
                act.dma_start(layer(o_nk_t).rearrange("a (m p) t -> p (a m) t", p=P), nkT[:, :, 0:N_CTX]).then_inc(caches_out, 16)
                split_high(4)
                split_high(5)
                await_read(act, ("nv", 1, 0))
                act.dma_start(layer(o_nv).rearrange("a p n -> p (a n)"), nv[:, 0, :]).then_inc(caches_out, 16)
                for m in range(NM):
                    ps = await_job(act, ("nq", m))
                    nc.scalar.mul(nqT[:, m, :], ps[:, TMID:TMID + T], HD ** -0.5).then_inc(freed[PAIR_OF[("nq", m)]], 1)
                    if m % 2:
                        split_high(6 + m // 2)
                await_job(act, ("u", NM - 1))
                act.dma_start(ckvT[:, :, T:KEYS], layer(ckv_cache_t).rearrange("a (k p) t -> p (a k) t", p=P)).then_inc(caches_in, 16)
                act.dma_start(kpeT[HD:QKD, T:KEYS], layer(kpe_cache_t).rearrange("a p t -> p (a t)")).then_inc(caches_in, 16)
                tr = layer(rpb_rows).rearrange("a q h r c -> q (a h) r c")
                tb4 = tb.rearrange("p h (r c) -> p h r c", c=GW)
                act.dma_start(tb4[0:GW], tr[:, :, 1:1 + DR, :]).then_inc(bias_in, 16)
                act.dma_start(tb4[GW:P], tr[:, :, 0:DR, :]).then_inc(bias_in, 16)

                for t in range(TT):
                    ps = await_job(act, ("low", t))
                    nc.scalar.activation(pp[:, 0:QL], ps[:, LMID:LMID + QL], ACT.Square,
                                         accum_out=ss2[:, 2 * t:2 * t + 1])
                    nc.scalar.activation(pp[:, QL:QL + KVL], ps[:, LMID + QL:LMID + QL + KVL], ACT.Square,
                                         accum_out=ss2[:, 2 * t + 1:2 * t + 2]).then_inc(low_sq, 1)
                    if t >= 2:
                        await_job(act, ("lowt", t - 2))
                        if t == 2:
                            act.wait_ge(kpe_out, 16)
                    nc.scalar.copy(ltm[:, t % 2, :], ps[:, LMID:LMID + LOW]).then_inc(freed[PAIR_OF[("low", t)]], 1)
                    if t == 0:
                        await_read(act, ("low", 0))
                        act.dma_start(layer(o_kpe).rearrange("a p n -> p (a n)"), ltm[:, 0, QL + KVL:LOW]).then_inc(kpe_out, 16)
                    act.wait_ge(low_ms, t + 1)
                    nc.scalar.activation(rs2[:, 2 * t:2 * t + 2], rs2[:, 2 * t:2 * t + 2], ACT.Sqrt).then_inc(low_root, 1)
                await_read(act, ("lowt", 0))
                act.dma_start(layer(o_ckv_t).rearrange("a (k p) t -> p (a k) t", p=P), ckvT[:, :, 0:N_CTX]).then_inc(caches_out, 16)

                units = attention_steps()

                def attention(kind, base):
                    for i in range(len(units) + LAG_PV):
                        j = i - LAG_PT
                        if 0 <= j < len(units):
                            n = T if units[j][1] else P
                            ps = await_job(act, (kind + "t", j))
                            if j >= 2:
                                act.wait_ge(pv_done, base + j - 1)
                            nc.scalar.copy(probT[j % 2][:, 0:n], ps[:, 0:n]).then_inc(freed[PAIR_OF[(kind + "t", j)]], 1)
                        if i < len(units):
                            t = units[i][1]
                            n = T if t else P
                            act.wait_ge(biased, base + i + 1)
                            if kind == "na" and t:
                                nc.scalar.activation(probs[i % 3][:, 0:n], probs[i % 3][:, 0:n], ACT.Exp,
                                                     bias=negms[i % 3], accum_out=rsums[i % 3]).then_inc(exped, 1)
                            else:
                                ps = pair[PAIR_OF[(kind + "s", i)]]
                                if i >= 3:
                                    await_job(act, (kind + "t", i - 3))
                                nc.scalar.activation(probs[i % 3][:, 0:n], ps[:, MID:MID + n], ACT.Exp,
                                                     bias=negms[i % 3], scale=1.0 if kind == "na" else QKD ** -0.5,
                                                     accum_out=rsums[i % 3])\
                                    .then_inc(freed[PAIR_OF[(kind + "s", i)]], 1)

                attention("na", 0)
                act.wait_ge(caches_out, 48)
                for t in range(KT):
                    ps = await_job(act, ("vm", t))
                    nc.scalar.copy(vm[:, t, :], ps[:, 0:512]).then_inc(freed[PAIR_OF[("vm", t)]], 1)
                for h in range(NH):
                    ps = await_job(act, ("kn", h))
                    nc.scalar.copy(kT[0:HD, h, :], ps[0:HD, KMID:KMID + KEYS]).then_inc(freed[PAIR_OF[("kn", h)]], 1)
                attention("ml", len(units))

                split_high(N_WIN)
                act.wait_ge(pv_done, 2 * len(units))
                for n in (N_IN - 2, N_IN - 1):
                    await_mod_stored(act, n)
                split_high(N_WIN + 1)
                for g in range(NM):
                    ps = await_job(act, ("pool", g))
                    nc.scalar.mul(yT[0][:, g, :], ps[:, 1024 - T:1024], psc[:, g:g + 1]).then_inc(freed[PAIR_OF[("pool", g)]], 1)
                for g in range(2):
                    act.dma_start(gb1[:, g, :], mod_rows[g:g + 1, 2 * D:3 * D].partition_broadcast(P)).then_inc(gb_in, 16)
                for i, (m, n) in enumerate(MERGE):
                    ps = await_job(act, ("gate", m, n))
                    if i >= 2:
                        await_read(act, ("branch", *MERGE[i - 2]))
                    nc.scalar.activation(sig[:, i % 2, :], ps[:, MID:MID + T], ACT.Sigmoid)\
                        .then_inc(freed[PAIR_OF[("gate", m, n)]], 1)
                    if i % 2 and N_WIN + 2 + i // 2 < len(HALVES):
                        split_high(N_WIN + 2 + i // 2)
                await_job(act, ("gate", KD - 1, 2))
                act.dma_start(x2, x_res.rearrange("(t p) d -> p t d", p=P)).then_inc(x2_in, 16)
                for g in range(2):
                    act.dma_start(bc2[:, 2 * g, :], mod_rows[g:g + 1, 4 * D:5 * D].partition_broadcast(P)).then_inc(bc2_in, 16)
                    act.dma_start(bc2[:, 2 * g + 1, :], mod_rows[g:g + 1, 3 * D:4 * D].partition_broadcast(P)).then_inc(bc2_in, 16)
                def tail_transposed(t):
                    ps = await_job(act, ("ht", t))
                    if t >= 2:
                        await_job(act, ("lg", t - 2))
                    nc.scalar.copy(h2T[:, t % 2, :], ps[:, :]).then_inc(freed[PAIR_OF[("ht", t)]], 1)

                def root(t, count):
                    act.wait_ge(ms3, count)
                    nc.scalar.activation(rs[:, t:t + 1], rs[:, t:t + 1], ACT.Sqrt).then_inc(root3, 1)

                for t in range(TT):
                    ps = await_job(act, ("y", t))
                    if t >= 2:
                        act.wait_ge(x2_new, t - 1)
                    nc.scalar.activation(yb[:, t % 2, :], ps[:, :], ACT.Square, accum_out=ss[:, t:t + 1]).then_inc(sq3, 1)
                    root(t, 2 * t + 1)
                    act.wait_ge(x2_new, t + 1)
                    if t >= 1:
                        act.wait_ge(sq3, 2 * t)
                    nc.scalar.activation(squares, x2[:, t, :], ACT.Square,
                                         accum_out=ss[:, t:t + 1]).then_inc(sq3, 1)
                    root(t, 2 * t + 2)
                    if t:
                        tail_transposed(t - 1)
                tail_transposed(TT - 1)
                act.wait_ge(routed_a, 1)
                nc.scalar.activation(e4, e4, ACT.Exp).then_inc(routed_b, 1)
                act.wait_ge(routed_a, 2)
                nc.scalar.activation(m2, m2, ACT.Exp).then_inc(routed_b, 1)

                await_mod_stored(act, N_IN)
                await_mod_stored(act, N_IN + 1)
                for g in range(2):
                    act.dma_start(gb2[:, g, :], mod_rows[g:g + 1, 5 * D:6 * D].partition_broadcast(P)).then_inc(gb_in, 16)
                act.wait_ge(rows_zeroed, 16 * (NB - 2 * T // BLOCK))
                act.sem_inc(sil_ready, 1)
                act.sem_inc(y_read, 3)
                for s in range(2):
                    act.sem_inc(yo_stored[s], 16)
                out_blocks = expert_out.rearrange("(b p) d -> b p d", p=P)
                act.wait_ge(blocks_ready, 1)
                n_pairs = act.value_load(pair_count[0:1], min_val=1, max_val=NB // 2)
                with act.Fori(0, n_pairs) as it:
                    for s in range(2):
                        act.wait_ge(h_filled, it * 2 + (s + 3))
                        nc.scalar.activation(sil[:, s, :], pair[1][:, s * 512:s * 512 + FF], ACT.Silu).then_inc(sil_ready, 1)
                        act.wait_ge(y_filled, it * 2 + (s + 3))
                        act.wait_ge(yo_stored[s], it * 16 + 16)
                        nc.scalar.copy(yo[:, s, :], (pair[2], opair)[s][:, :]).then_inc(y_read, 1)
                        act.wait_ge(y_read, it * 2 + (s + 4))
                        act.dma_start(out_blocks[ds(it * 2 + s, 1)].rearrange("a p d -> p (a d)"), yo[:, s, :]).then_inc(yo_stored[s], 16)
                for t in range(TT):
                    act.wait_ge(mixed, t + 1)
                    nc.scalar.activation(hT[:, (t % 2) * D:(t % 2 + 1) * D], picks[t][:, 0, :], ACT.Square,
                                         accum_out=ss[:, t:t + 1]).then_inc(sq3, 1)
                    root(t, 2 * TT + t + 1)
                    act.wait_ge(x2_new, TT + t + 1)
                    act.dma_start(x_res[t * P:(t + 1) * P, :], x2[:, t, :]).then_inc(x_stored, 16)
                act.wait_ge(x_stored, 16 * TT)
                act.wait_ge(root3, 3 * TT)
                act.sem_inc(layer_done, 1)
                act.wait_ge(go["act"], 1)
                act.sem_clear(go["act"])

        @block.vector
        def _(dve):
            V = nc.vector
            dve.wait_ge(consts_in, 16)
            V.tensor_copy(tok_ids, const("tok"))
            dve.wait_ge(pro_aux_in, 16)
            for i in range(4):
                dve.wait_ge(pro_filled, i + 1)
                V.scalar_tensor_tensor(out=pro_st[0:2, i, :], in0=pair[i // 2][0:2, (i % 2) * 512:(i % 2 + 1) * 512],
                                       scalar=float(i // 2), in1=pro_aux[0:2, i, 0:512],
                                       op0=ALU.add, op1=ALU.add).then_inc(pro_step, 1)
                dve.wait_ge(pro_step, i + 1)
                V.tensor_tensor(pro_st[0:2, i, :], pro_st[0:2, i, :], pro_aux[0:2, i, 512:1024], ALU.mult).then_inc(pro_rows, 1)
            with dve.Fori(0, DEPTH) as L:
                steps = [0]

                def link(ins):
                    ins.then_inc(dve_step, 1)
                    steps[0] += 1
                    dve.wait_ge(dve_step, steps[0])

                def mod_rows_of(n):
                    ps = await_job(dve, ("mod", n))
                    dve.wait_ge(aux_in[n % 2], 16 * (n // 2 + 1))
                    if mod_before(n) is not None:
                        await_mod_stored(dve, mod_before(n))
                    one = 1.0 if MODS[n][0] // 2 in (1, 4) else 0.0
                    V.scalar_tensor_tensor(out=modst[n][0:2], in0=ps[0:2, 0:512], scalar=one, in1=aux[n][0:2, 0:512],
                                           op0=ALU.add, op1=ALU.add).then_inc(freed[PAIR_OF[("mod", n)]], 1)
                    await_read(dve, ("mod", n))
                    V.tensor_tensor(modst[n][0:2], modst[n][0:2], aux[n][0:2, 512:1024], ALU.mult).then_inc(mod_row, 1)

                def split_low(i):
                    dve.wait_ge(high_ready, i + 1)
                    w = half_source(dve, i)
                    V.tensor_tensor(w_low[i % 2], w, w_high[i % 2], ALU.subtract).then_inc(parts_ready, 1)

                for t in range(TT):
                    dve.wait_ge(sq_ready, t + 1)
                    V.tensor_scalar(rs[:, t:t + 1], ss[:, t:t + 1], 1.0 / D, EPS, ALU.mult, ALU.add).then_inc(ms_ready, 1)
                    dve.wait_ge(root_ready, t + 1)
                    link(V.reciprocal(rstd[:, t:t + 1], rs[:, t:t + 1]))
                    if t == 0:
                        dve.wait_ge(bc_in, 64)
                    dve.wait_ge(x_in[t], 16)
                    rows = bc1[min(t, 1)]
                    if t >= 2:
                        await_job(dve, ("xt", t - 2))
                    link(V.scalar_tensor_tensor(out=hb[:, t % 2, :], in0=xt[:, t, :], scalar=rstd[:, t:t + 1],
                                                in1=rows[:, 0, :], op0=ALU.mult, op1=ALU.mult))
                    V.tensor_tensor(hb[:, t % 2, :], hb[:, t % 2, :], rows[:, 1, :], ALU.add).then_inc(h_ready, 1)
                for i in range(4):
                    split_low(i)
                for a in range(2):
                    for t in range(TT):
                        ps = await_job(dve, ("nv", a, t))
                        V.tensor_copy(nv[:, t, a * 256:(a + 1) * 256], ps[:, 0:256]).then_inc(freed[PAIR_OF[("nv", a, t)]], 1)
                    split_low(4 + a)
                for i in range(6, N_WIN):
                    split_low(i)
                for a, b in ((0, C_AT), (C_AT + N_CTX, L_AT), (L_AT + N_LAT, PADT)):
                    V.memset(u_pad[:, :, a:b], 0.0)
                for m in range(NM):
                    ps = await_job(dve, ("u", m))
                    V.tensor_copy(u_pad[:, m, C_AT:C_AT + N_CTX], ps[:, TMID:TMID + N_CTX])
                    V.tensor_copy(u_pad[:, m, L_AT:L_AT + N_LAT], ps[:, TMID + N_CTX:TMID + T])\
                        .then_inc(freed[PAIR_OF[("u", m)]], 1)

                def low_transposed(t):
                    ps = await_job(dve, ("lowt", t))
                    tok = slice(t * P, (t + 1) * P)
                    V.tensor_tensor(cqT[:, :, tok], ps[:, 0:QL].rearrange("p (k c) -> p k c", k=QT),
                                    lown[:, 0:QT].unsqueeze(2).to_broadcast([P, QT, P]), ALU.mult)
                    V.tensor_tensor(ckvT[:, :, tok], ps[:, QL:QL + KVL].rearrange("p (k c) -> p k c", k=KVT),
                                    lown[:, QT:QT + KVT].unsqueeze(2).to_broadcast([P, KVT, P]), ALU.mult)
                    V.tensor_copy(kpeT[HD:QKD, tok], ps[HD:QKD, QL + KVL:QL + KVL + P])\
                        .then_inc(freed[PAIR_OF[("lowt", t)]], 1)

                dve.wait_ge(small_in, 80)
                for t in range(TT):
                    dve.wait_ge(low_sq, t + 1)
                    V.tensor_scalar(rs2[:, 2 * t:2 * t + 1], ss2[:, 2 * t:2 * t + 1], 1.0 / QL, EPS, ALU.mult, ALU.add)
                    V.tensor_scalar(rs2[:, 2 * t + 1:2 * t + 2], ss2[:, 2 * t + 1:2 * t + 2], 1.0 / KVL, EPS,
                                    ALU.mult, ALU.add).then_inc(low_ms, 1)
                    dve.wait_ge(low_root, t + 1)
                    link(V.reciprocal(rstd2[:, 2 * t:2 * t + 2], rs2[:, 2 * t:2 * t + 2]))
                    await_read(dve, ("low", t))
                    tm = ltm[:, t % 2, :]
                    V.tensor_scalar(tm[:, 0:QL], tm[:, 0:QL], rstd2[:, 2 * t:2 * t + 1], None, ALU.mult)
                    last = V.tensor_scalar(tm[:, QL:QL + KVL], tm[:, QL:QL + KVL], rstd2[:, 2 * t + 1:2 * t + 2],
                                           None, ALU.mult)
                    if t:
                        kp = tm[:, QL + KVL:LOW]
                        k4 = kp.rearrange("p (a j f) -> p a j f", a=2, j=2)
                        s4 = const("sin")[:, (t - 1) * RD:t * RD].rearrange("p (a j f) -> p a j f", a=2, j=2)
                        r4 = rot.rearrange("p (a j f) -> p a j f", a=2, j=2)
                        V.tensor_tensor(r4[:, :, 0, :], k4[:, :, 1, :], s4[:, :, 0, :], ALU.mult)
                        link(V.tensor_tensor(r4[:, :, 1, :], k4[:, :, 0, :], s4[:, :, 1, :], ALU.mult))
                        link(V.tensor_tensor(kp, kp, const("cos")[:, (t - 1) * RD:t * RD], ALU.mult))
                        last = V.tensor_tensor(kp, kp, rot, ALU.add)
                    last.then_inc(low_scaled, 1)
                    if t:
                        low_transposed(t - 1)
                low_transposed(TT - 1)

                units = attention_steps()

                def attention(kind, base):
                    def maxima(i):
                        h, t = units[i]
                        ps = await_job(dve, (kind + "s", i))
                        if kind == "na" and t:
                            if i >= 3:
                                await_job(dve, (kind + "t", i - 3))
                            r0 = 6 - 2 * (t - 1)
                            V.tensor_tensor_reduce(probs[i % 3][:, 0:N_LAT], ps[:, MID:MID + N_LAT],
                                                   tb[:, h, r0 * GW:r0 * GW + N_LAT], 1.0, LEAST,
                                                   ALU.add, ALU.max, mxs[i % 2][:, 0:1])
                            V.tensor_scalar(probs[i % 3][:, N_LAT:T], ps[:, MID + N_LAT:MID + T], 1.0, LEAST,
                                            ALU.mult, ALU.max, accum_out=mxs[i % 2][:, 1:2])\
                                .then_inc(freed[PAIR_OF[(kind + "s", i)]], 1)
                            await_read(dve, (kind + "s", i))
                            V.tensor_scalar(negms[i % 3], mxs[i % 2][:, 0:1], mxs[i % 2][:, 1:2], -1.0,
                                            ALU.max, ALU.mult).then_inc(biased, 1)
                        else:
                            n = T if t else P
                            link(V.reduce_max(mxs[i % 2][:, 0:1], ps[:, MID:MID + n], AX_X))
                            V.tensor_scalar(negms[i % 3], mxs[i % 2][:, 0:1], -1.0 if kind == "na" else -QKD ** -0.5,
                                            None, ALU.mult).then_inc(biased, 1)

                    def normalise(i):
                        n = T if units[i][1] else P
                        h, t = units[i]
                        if kind == "na" and t:
                            dve.wait_ge(exped, h * (TT - 1) + t)
                        else:
                            await_read(dve, (kind + "s", i))
                        inv = rinv[:, i % 2:i % 2 + 1]
                        link(V.reciprocal(inv, rsums[i % 3]))
                        V.tensor_scalar(probs[i % 3][:, 0:n], probs[i % 3][:, 0:n], inv, None, ALU.mult)\
                            .then_inc(scaled, 1)

                    for i in range(len(units) + LAG_PV):
                        if i < len(units):
                            maxima(i)
                        if 0 <= i - 1 < len(units):
                            normalise(i - 1)
                        if i < len(units) and (kind, *units[i]) in MOD_AT:
                            mod_rows_of(MOD_AT[(kind, *units[i])])
                        done = i - LAG_PV
                        if done >= 0 and done % (2 * TT) == 2 * TT - 1:
                            m = done // (2 * TT)
                            n = 1 if kind == "na" else 2
                            dve.wait_ge(pv_done, base + done + 1)
                            if n == 2 and m == 0:
                                dve.wait_ge(pooled, NM)
                            V.tensor_copy(yT[n][:, m, :], opair[:, 0:T]).then_inc(o_freed, 1)

                dve.wait_ge(bias_masked, 1)
                attention("na", 0)
                for h in range(NH):
                    ps = await_job(dve, ("qm", h))
                    lat = slice(MID + N_CTX, MID + T)
                    V.tensor_copy(qT[0:QKD, h, 0:N_CTX], ps[0:QKD, MID:MID + N_CTX])
                    V.tensor_copy(qT[0:HD, h, N_CTX:T], ps[0:HD, lat])
                    V.tensor_tensor(qT[HD:QKD, h, N_CTX:T], ps[HD:QKD, lat], const("rope")[HD:QKD], ALU.mult)
                    V.tensor_tensor(swapped[HD:QKD], ps[QKD:P, lat], const("rope")[QKD:P], ALU.mult)\
                        .then_inc(freed[PAIR_OF[("qm", h)]], 1)
                    await_read(dve, ("qm", h))
                    V.tensor_tensor(qT[HD:QKD, h, N_CTX:T], qT[HD:QKD, h, N_CTX:T], swapped[HD:QKD], ALU.add)\
                        .then_inc(q_ready, 1)
                    dve.wait_ge(q_ready, h + 1)
                attention("ml", len(units))

                for i in range(N_WIN, N_WIN + 2):
                    split_low(i)
                dve.wait_ge(g_parts_ready, KD)
                for i, (m, n) in enumerate(MERGE):
                    ps = await_job(dve, ("branch", m, n))
                    await_read(dve, ("gate", m, n))
                    out = mergedT[:, m, :] if n == 0 else prod[:, i % 2, :]
                    V.tensor_tensor(out, ps[:, MID:MID + T], sig[:, i % 2, :], ALU.mult)\
                        .then_inc(freed[PAIR_OF[("branch", m, n)]], 1)
                    if n:
                        await_read(dve, ("branch", m, n))
                        ins = V.tensor_tensor(mergedT[:, m, :], mergedT[:, m, :], prod[:, i % 2, :], ALU.add)
                        if n == 2:
                            ins.then_inc(merged, 1)
                    if i % 2 and N_WIN + 2 + i // 2 < len(HALVES):
                        split_low(N_WIN + 2 + i // 2)

                def inverse_root(t, count):
                    dve.wait_ge(sq3, count)
                    V.tensor_scalar(rs[:, t:t + 1], ss[:, t:t + 1], 1.0 / D, EPS, ALU.mult, ALU.add).then_inc(ms3, 1)
                    dve.wait_ge(root3, count)
                    link(V.reciprocal(rstd[:, t:t + 1], rs[:, t:t + 1]))

                def logits(t):
                    ps = await_job(dve, ("lg", t))
                    V.tensor_copy(lg[:, t, :], ps[:, 0:LG]).then_inc(freed[PAIR_OF[("lg", t)]], 1)

                dve.wait_ge(gb_in, 32)
                dve.wait_ge(x2_in, 16)
                for t in range(TT):
                    g = min(t, 1)
                    inverse_root(t, 2 * t + 1)
                    V.scalar_tensor_tensor(out=yb[:, t % 2, :], in0=pair[PAIR_OF[("y", t)]][:, :], scalar=rstd[:, t:t + 1],
                                           in1=gb1[:, g, :], op0=ALU.mult, op1=ALU.mult)\
                        .then_inc(freed[PAIR_OF[("y", t)]], 1)
                    await_read(dve, ("y", t))
                    V.tensor_tensor(x2[:, t, :], x2[:, t, :], yb[:, t % 2, :], ALU.add).then_inc(x2_new, 1)
                    inverse_root(t, 2 * t + 2)
                    if t == 0:
                        dve.wait_ge(bc2_in, 64)
                    link(V.scalar_tensor_tensor(out=h2[:, t, :], in0=x2[:, t, :], scalar=rstd[:, t:t + 1],
                                                in1=bc2[:, 2 * g, :], op0=ALU.mult, op1=ALU.mult))
                    V.tensor_tensor(h2[:, t, :], h2[:, t, :], bc2[:, 2 * g + 1, :], ALU.add).then_inc(h2_ready, 1)
                    if t >= 2:
                        logits(t - 2)
                mod_rows_of(N_IN)
                logits(TT - 2)
                mod_rows_of(N_IN + 1)
                logits(TT - 1)
                await_read(dve, ("lg", TT - 1))

                def wide(v, n=EG):
                    return v.to_broadcast([P, TT, n])

                rev = const("rev").rearrange("p (t n) -> p t n", t=TT)

                def first_max(values, mark, top):
                    link(V.tensor_tensor(mark, values, wide(top), ALU.is_equal))
                    link(V.tensor_tensor(w4, mark, rev, ALU.mult))
                    link(V.reduce_max(big, w4, AX_X))
                    link(V.tensor_tensor(mark, w4, wide(big), ALU.is_equal))

                lgg = lg[:, :, 0:NG]
                link(V.reduce_max(gmax, lgg, AX_X))
                V.tensor_tensor(e4, lgg, wide(gmax), ALU.subtract).then_inc(routed_a, 1)
                first_max(lgg, oh_g, gmax)
                g16 = [P, TT, NG, EG]
                v4 = "p t (g e) -> p t g e"
                link(V.tensor_tensor(ch1.rearrange(v4, g=NG), lg[:, :, NG:LG].rearrange(v4, g=NG),
                                     oh_g.unsqueeze(3).to_broadcast(g16), ALU.mult))
                link(V.tensor_reduce(el, ch1.rearrange("p t (g e) -> p t e g", g=NG), AX_X, ALU.add))
                link(V.reduce_max(m1, el, AX_X))
                first_max(el, oh1, m1)
                link(V.scalar_tensor_tensor(out=elm, in0=oh1, scalar=NEG, in1=el, op0=ALU.mult, op1=ALU.add))
                link(V.reduce_max(m2, elm, AX_X))
                first_max(elm, oh2, m2)
                V.tensor_tensor(m2, m2, m1, ALU.subtract).then_inc(routed_a, 1)
                V.tensor_tensor(ch1.rearrange(v4, g=NG), oh_g.unsqueeze(3).to_broadcast(g16),
                                oh1.unsqueeze(2).to_broadcast(g16), ALU.mult)
                link(V.tensor_tensor(ch2.rearrange(v4, g=NG), oh_g.unsqueeze(3).to_broadcast(g16),
                                     oh2.unsqueeze(2).to_broadcast(g16), ALU.mult))
                V.tensor_tensor(chs, ch1, ch2, ALU.add).then_inc(chosen, 1)
                mod_rows_of(N_IN + 2)
                mod_rows_of(N_IN + 3)
                dve.wait_ge(routed_b, 2)
                V.tensor_reduce(gsum, e4, AX_X, ALU.add)
                link(V.tensor_scalar(m1, m2, 1.0, None, ALU.add))
                link(V.tensor_tensor(gsum, gsum, m1, ALU.mult))
                link(V.reciprocal(gate1, gsum))
                link(V.tensor_tensor(gate2, gate1, m2, ALU.mult))
                ps = await_job(dve, ("cnt", 0))
                pos = ps[:, 0:TT * NE].rearrange("p (t n) -> p t n", t=TT)
                tot = ps[:, 128:128 + TT * NE].rearrange("p (t n) -> p t n", t=TT)
                V.tensor_copy(slots[:, 0, :], pos[:, 0, :])
                link(V.tensor_copy(n_e, tot[:, 0, :]))
                for t in range(1, TT):
                    link(V.tensor_tensor(slots[:, t, :], pos[:, t, :], n_e, ALU.add))
                    link(V.tensor_tensor(n_e, tot[:, t, :], n_e, ALU.add))
                link(V.tensor_scalar(blocks, n_e, 0.0, None, ALU.is_gt))
                for j in range(1, TT):
                    link(V.scalar_tensor_tensor(out=blocks, in0=n_e, scalar=float(j * BLOCK), in1=blocks,
                                                op0=ALU.is_gt, op1=ALU.add))
                link(V.tensor_tensor_scan(blk_end, ones[:, 0:NE], blocks, 0.0, ALU.mult, ALU.add))
                link(V.tensor_tensor(blk_start, blk_end, blocks, ALU.subtract))
                for t in range(TT):
                    last = V.scalar_tensor_tensor(out=slots[:, t, :], in0=blk_start, scalar=float(BLOCK),
                                                  in1=slots[:, t, :], op0=ALU.mult, op1=ALU.add)
                link(last)
                V.tensor_tensor(ch1, ch1, slots, ALU.mult)
                link(V.tensor_tensor(ch2, ch2, slots, ALU.mult))
                V.tensor_reduce(slot1, ch1, AX_X, ALU.add)
                link(V.tensor_reduce(slot2, ch2, AX_X, ALU.add))
                V.tensor_copy(slot_ids[:, 0:TT].unsqueeze(2), slot1)
                V.tensor_copy(slot_ids[:, TT:2 * TT].unsqueeze(2), slot2).then_inc(slots_ready, 1)
                link(V.tensor_tensor(bcmp, blk_end.unsqueeze(1).to_broadcast([P, NB, NE]),
                                     const("blk").unsqueeze(2).to_broadcast([P, NB, NE]), ALU.is_le))
                link(V.tensor_reduce(bexp, bcmp, AX_X, ALU.add))
                link(V.tensor_scalar(bexp, bexp, float(NE - 1), None, ALU.min))
                V.tensor_copy(blk_ids, bexp)
                link(V.tensor_scalar(halves, const("blk")[:, 0:NB:2], blk_end[:, NE - 1:NE], None, ALU.is_lt))
                link(V.tensor_reduce(npair_f, halves, AX_X, ALU.add))
                V.tensor_copy(pair_count, npair_f).then_inc(blocks_ready, 1)
                mod_rows_of(N_IN + 4)
                mod_rows_of(N_IN + 5)

                dve.sem_inc(t_freed, 1)
                dve.sem_inc(hid_ready, 3)

                def transposed(b, s):
                    dve.wait_ge(t_filled, b + 3)
                    V.tensor_copy(xgT[:, s, :], pair[0][:, :]).then_inc(t_freed, 1)

                def hidden(b, s):
                    dve.wait_ge(sil_ready, b + 2)
                    V.tensor_tensor(hid[:, s, :], sil[:, s, :], pair[1][:, s * 512 + FF:s * 512 + 2 * FF], ALU.mult)\
                        .then_inc(hid_ready, 1)

                dve.wait_ge(blocks_ready, 1)
                n_pairs = dve.value_load(pair_count[0:1], min_val=2, max_val=NB // 2)
                transposed(0, 0)
                with dve.Fori(0, n_pairs - 1) as it:
                    hidden(it * 2, 0)
                    transposed(it * 2 + 1, 1)
                    hidden(it * 2 + 1, 1)
                    transposed(it * 2 + 2, 0)
                hidden(n_pairs * 2 - 2, 0)
                transposed(n_pairs * 2 - 1, 1)
                hidden(n_pairs * 2 - 1, 1)

                dve.wait_ge(gb_in, 64)
                def mix(t):
                    a, b = picks[t][:, 0, :], picks[t][:, 1, :]
                    dve.wait_ge(picked[t], 32)
                    link(V.tensor_scalar(a, a, gate1[:, t, :], None, ALU.mult))
                    V.scalar_tensor_tensor(out=a, in0=b, scalar=gate2[:, t, :], in1=a, op0=ALU.mult, op1=ALU.add)\
                        .then_inc(mixed, 1)

                mix(0)
                for t in range(TT):
                    if t + 1 < TT:
                        mix(t + 1)
                    a = picks[t][:, 0, :]
                    inverse_root(t, 2 * TT + t + 1)
                    link(V.scalar_tensor_tensor(out=a, in0=a, scalar=rstd[:, t:t + 1], in1=gb2[:, min(t, 1), :],
                                                op0=ALU.mult, op1=ALU.mult))
                    V.tensor_tensor(x2[:, t, :], x2[:, t, :], a, ALU.add).then_inc(x2_new, 1)
                dve.wait_ge(x2_new, 2 * TT)
                dve.sem_inc(layer_done, 1)
                dve.wait_ge(go["dve"], 1)
                dve.sem_clear(go["dve"])

        @block.gpsimd
        def _(pool):
            G = nc.gpsimd
            G.memset(src_ids, 0).then_inc(ids_zeroed, 1)
            pool.wait_ge(ids_zeroed, 1)
            with nc.allow_non_contiguous_dma(reason="four-byte rows"):
                pool.dma_start(slot_token.rearrange("(b p) o -> p (b o)", p=P), src_ids).then_inc(list_zeroed, 16)
            pool.wait_ge(list_zeroed, 16)
            await_job(pool, ("xt", 0))
            full = expert_out.rearrange("(b p) d -> b p d", p=P)
            least = 2 * T // BLOCK
            for b in range(least, NB):
                pool.dma_start(full[b], zeros).then_inc(rows_zeroed, 16)
            pool.wait_ge(consts_in, 16)
            with pool.Fori(0, DEPTH) as L:
                steps = [0]

                def link(ins):
                    ins.then_inc(pool_step, 1)
                    steps[0] += 1
                    pool.wait_ge(pool_step, steps[0])

                for t in range(TT):
                    pool.wait_ge(h_high_ready, t + 1)
                    await_read(pool, ("xt", t))
                    G.tensor_tensor(h_low[:, t, :].rearrange("p (k c) -> p k c", k=KD), h_t[:, :, t * P:(t + 1) * P],
                                    h_high[:, t, :].rearrange("p (k c) -> p k c", k=KD), ALU.subtract)\
                        .then_inc(h_parts_ready, 1)

                pool.wait_ge(bias_in, 32)
                tbr = r1[:, NQ_W:NQ_W + T_W].rearrange("p (r c) -> p r c", c=GW)
                G.tensor_tensor(tbr, tbr, const("mask").unsqueeze(1).to_broadcast([P, NH * DR, GW]), ALU.add)\
                    .then_inc(bias_masked, 1)

                await_read(pool, ("u", NM - 1))
                edge = const("edge").rearrange("p (g a b) -> p g a b", g=NM, a=2)
                for g, w in enumerate(POOL_W):
                    u = u_pad[:, g, :]
                    link(G.tensor_tensor(sum_a[:, 1:PADT], u[:, 0:PADT - 1], u[:, 1:PADT], ALU.add))
                    cur, nxt, lo, hi = sum_a, sum_b, 1, PADT
                    for d in (1, 2, 4)[:g]:
                        link(G.tensor_tensor(nxt[:, lo + d:hi - d], cur[:, lo:hi - 2 * d], cur[:, lo + 2 * d:hi], ALU.add))
                        cur, nxt, lo, hi = nxt, cur, lo + d, hi - d
                    link(G.tensor_scalar(nxt[:, C_AT:L_AT + N_LAT], cur[:, C_AT:L_AT + N_LAT], 1.0 / w, None, ALU.mult))
                    for i, (a, b) in enumerate(((C_AT, L_AT), (C_AT + N_CTX - 8, L_AT + N_LAT - 8))):
                        for c in (a, b):
                            ins = G.tensor_tensor(nxt[:, c:c + 8], nxt[:, c:c + 8], edge[:, g, i, :], ALU.mult)
                    link(ins)
                    G.tensor_tensor(u[:, C_AT:L_AT + N_LAT], nxt[:, C_AT:L_AT + N_LAT], u[:, C_AT:L_AT + N_LAT],
                                    ALU.subtract).then_inc(pooled, 1)
                    pool.wait_ge(pooled, g + 1)

                await_job(pool, ("vm", 0))
                await_read(pool, ("lowt", TT - 1))
                pool.wait_ge(caches_in, 64)
                for h in range(NH):
                    G.tensor_copy(kT[HD:QKD, h, :], kpeT[HD:QKD, :]).then_inc(kpe_copied, 1)

                await_job(pool, ("mls", len(attention_steps()) - 1))
                for k in range(KD):
                    G.tensor_copy(g_high[:, k, :], h_t[:, k, :]).then_inc(g_high_ready, 1)
                for k in range(KD):
                    pool.wait_ge(g_high_ready, k + 1)
                    G.tensor_tensor(g_low[:, k, :], h_t[:, k, :], g_high[:, k, :], ALU.subtract).then_inc(g_parts_ready, 1)

                pool.wait_ge(slots_ready, 1)
                for i in range(2 * TT):
                    pool.indirect_dma_start(slot_token, bass.IndirectOffsetOnAxis(ap=slot_ids[:, i:i + 1], axis=0),
                                            tok_ids[:, i % TT:i % TT + 1], None).then_inc(scattered, 16)
                pool.wait_ge(list_in, 16)
                pool.wait_ge(h2_stored, 16 * TT)
                pool.wait_ge(blocks_ready, 1)
                n_pairs = pool.value_load(pair_count[0:1], min_val=1, max_val=NB // 2)
                with pool.Fori(0, n_pairs) as it:
                    for s in range(2):
                        pool.wait_ge(t_filled, it * 2 + (s + 1))
                        pool.sem_inc(ran_on, 1)
                        G.tensor_copy(src_id[s], src_ids[:, ds(it * 2 + s, 1)]).then_inc(id_ready, 1)
                        pool.wait_ge(id_ready, it * 2 + (s + 1))
                        pool.sem_inc(ran_on, 1)
                        pool.indirect_dma_start(xg[:, s, :], None, h2_rows,
                                                bass.IndirectOffsetOnAxis(ap=src_id[s], axis=0)).then_inc(xg_in[s], 16)
                for s in range(2):
                    pool.wait_ge(yo_stored[s], n_pairs * 16 + 16)
                pool.sem_inc(ran_on, 1)
                for t in range(TT):
                    for k in range(2):
                        i = k * TT + t
                        pool.indirect_dma_start(picks[t][:, k, :], None, expert_out,
                                                bass.IndirectOffsetOnAxis(ap=slot_ids[:, i:i + 1], axis=0))\
                            .then_inc(picked[t], 16)
                for t in range(TT):
                    pool.wait_ge(picked[t], 32)
                pool.dma_reset()
                pool.sem_inc(layer_done, 1)
                pool.wait_ge(go["pool"], 1)
                pool.sem_clear(go["pool"])

        @block.tensor
        def _(pe):
            pe.wait_ge(cv_ready, 1)
            pe.wait_ge(consts_in, 16)
            for i in range(4):
                pe.wait_ge(pro_in[i], 16)
                for k in range(KD):
                    last = nc.tensor.matmul(pair[i // 2][0:2, (i % 2) * 512:(i % 2 + 1) * 512], cvec[:, k, :],
                                            pro_w[i][:, k, :], start=k == 0, stop=k == KD - 1)
                last.then_inc(pro_filled, 1)
            pe.wait_ge(pro_rows, 4)
            with pe.Fori(0, DEPTH) as L:
                def chunk(key, k, n):
                    pe.wait_ge(landed[SLOT_OF[key]], 16 * FILL_OF[key])
                    return view(ring, SLOT_OF[key] * SLOT, k * n, k=k)

                def mm(out, lhsT, rhs, first, last):
                    return nc.tensor.matmul(out, lhsT, rhs, start=first, stop=last, skip_group_check=True)

                def channels(key, w, c0, kt, rhs, width, at_, rows=P):
                    ps = pair_for(pe, key)
                    half = width // 2
                    for j in range(2):
                        for k in range(kt):
                            last = mm(ps[0:rows, at_ + j * half:at_ + (j + 1) * half], w[:, k, c0:c0 + rows],
                                      rhs[:, k, j * half:(j + 1) * half], k == 0, k == kt - 1)
                    last.then_inc(filled[PAIR_OF[key]], 1)

                def three_products(out, w_parts, x_parts, first, last):
                    for j, (a, b) in enumerate(((0, 0), (0, 1), (1, 0))):
                        ins = mm(out, w_parts[a], x_parts[b], first and j == 0, last and j == 2)
                    return ins

                by_tile = [(TMID + 128 * a, 128 * (b - a), lambda k, a=a, b=b: [x[:, a:b, k * P:(k + 1) * P] for x in (h_high, h_low)])
                           for a, b in ((0, 2), (2, TT))]
                by_channel = [(MID + a, T // 2, lambda k, a=a: [x[:, k, a:a + T // 2] for x in (g_high, g_low)])
                              for a in (0, T // 2)]

                def channels_split(key, i, c0, pieces):
                    pe.wait_ge(parts_ready, i + 1)
                    ps = pair_for(pe, key)
                    for a, n, parts_at in pieces:
                        for k in range(KD):
                            w = [x[i % 2][:, k, c0:c0 + P] for x in (w_high, w_low)]
                            last = three_products(ps[:, a:a + n], w, parts_at(k), k == 0, k == KD - 1)
                    last.then_inc(filled[PAIR_OF[key]], 1)

                def tokens(key, parts, kt, lhs, t):
                    ps = pair_for(pe, key)
                    for w, a, n in parts:
                        for k in range(kt):
                            last = mm(ps[:, a:a + n], lhs[:, k, t * P:(t + 1) * P], w[:, k, :], k == 0, k == kt - 1)
                    last.then_inc(filled[PAIR_OF[key]], 1)

                def turned(key, pieces):
                    ps = pair_for(pe, key)
                    for s, a in pieces:
                        last = nc.tensor.transpose(ps[0:s.shape[1], a:a + P], s, ident)
                    last.then_inc(filled[PAIR_OF[key]], 1)

                def modulate(n):
                    w = chunk(("mod", n), KD, 512)
                    ps = pair_for(pe, ("mod", n))
                    for k in range(KD):
                        last = mm(ps[0:2, 0:512], cvec[:, k, :], w[:, k, :], k == 0, k == KD - 1)
                    last.then_inc(filled[PAIR_OF[("mod", n)]], 1)

                for t in range(TT):
                    pe.wait_ge(h_ready, t + 1)
                    turned(("xt", t), [(hb[:, t % 2, k * P:(k + 1) * P], k * P) for k in range(KD)])
                pe.wait_ge(h_parts_ready, TT)
                for m in range(NM):
                    channels_split(("nk", m), m // 2, m % 2 * P, by_tile)
                for a in range(2):
                    pe.wait_ge(parts_ready, 3 + a)
                    for t in range(TT):
                        ps = pair_for(pe, ("nv", a, t))
                        for k in range(KD):
                            last = three_products(ps[:, 0:256], [x[:, t, k * P:(k + 1) * P] for x in (h_high, h_low)],
                                                  [x[a][:, k, :] for x in (w_high, w_low)], k == 0, k == KD - 1)
                        last.then_inc(filled[PAIR_OF[("nv", a, t)]], 1)
                for m in range(NM):
                    channels_split(("nq", m), 4 + m // 2, m % 2 * P, by_tile)
                for m in range(NM):
                    channels_split(("u", m), 6 + m // 2, m % 2 * P, by_tile)
                await_read(pe, ("xt", TT - 1))
                wa, wb = chunk(("low", 0), KD, LOW // 2), chunk(("low", 1), KD, LOW // 2)

                def low_transposes(t):
                    pe.wait_ge(low_scaled, t + 1)
                    tm = ltm[:, t % 2, :]
                    pieces = [(tm[:, k * P:(k + 1) * P], k * P) for k in range(QT + KVT)]
                    pieces.append((tm[:, QL + KVL - HD:LOW], QL + KVL))
                    turned(("lowt", t), pieces)

                for t in range(TT):
                    tokens(("low", t), [(wa, LMID, LOW // 2), (wb, 512, LOW // 2)], KD, h_t, t)
                    if t:
                        low_transposes(t - 1)
                low_transposes(TT - 1)

                units = attention_steps()

                def attention(kind, base):
                    n_pairs = NM * (kind == "ml")

                    def scores(i):
                        h, t = units[i]
                        ps = pair_for(pe, (kind + "s", i))
                        if kind == "na":
                            m, p0 = h // 2, HD * (h % 2)
                            q, k = nqT[p0:p0 + HD, m, t * P:(t + 1) * P], nkT[p0:p0 + HD, m, :]
                        else:
                            q, k = qT[0:QKD, h, t * P:(t + 1) * P], kT[0:QKD, h, :]
                        if t == 0:
                            last = mm(ps[:, MID:MID + P], q, k[:, 0:P], True, True)
                        else:
                            for j in range(2):
                                last = mm(ps[:, MID + j * (T // 2):MID + (j + 1) * (T // 2)], q,
                                          k[:, P + j * (T // 2):P + (j + 1) * (T // 2)], True, True)
                        last.then_inc(filled[PAIR_OF[(kind + "s", i)]], 1)

                    def transposes(i):
                        pe.wait_ge(scaled, base + i + 1)
                        n = TT if units[i][1] else 1
                        ps = pair_for(pe, (kind + "t", i))
                        for j in range(n):
                            last = nc.tensor.transpose(ps[:, j * P:(j + 1) * P], probs[i % 3][:, j * P:(j + 1) * P], ident)
                        last.then_inc(filled[PAIR_OF[(kind + "t", i)]], 1)

                    def values(i):
                        h, t = units[i]
                        await_read(pe, (kind + "t", i))
                        v = nv if kind == "na" else vm
                        p0, m = HD * (h % 2), n_pairs + h // 2
                        if i % (2 * TT) == 0 and m:
                            pe.wait_ge(o_freed, m)
                        keys = range(1, KT) if t else range(0, 1)
                        for j, kt in enumerate(keys):
                            last = mm(opair[p0:p0 + HD, t * P:(t + 1) * P], v[:, kt, h * HD:(h + 1) * HD],
                                      probT[i % 2][:, j * P:(j + 1) * P], j == 0, j == len(keys) - 1)
                        last.then_inc(pv_done, 1)

                    for i in range(len(units) + LAG_PV):
                        if i < len(units):
                            scores(i)
                            if (kind, *units[i]) in MOD_AT:
                                modulate(MOD_AT[(kind, *units[i])])
                        if 0 <= i - LAG_PT < len(units):
                            transposes(i - LAG_PT)
                        if 0 <= i - LAG_PV < len(units):
                            values(i - LAG_PV)

                pe.wait_ge(caches_in, 64)
                await_read(pe, ("u", NM - 1))
                attention("na", 0)
                await_read(pe, ("lowt", TT - 1))
                w = chunk(("ukv",), KVT, 1024)
                for t in range(KT):
                    tokens(("vm", t), [(w[:, :, 512:1024], 0, 512)], KVT, ckvT, t)
                for h in range(NH):
                    channels(("kn", h), w, h * HD, KVT, ckvT, KEYS, KMID, rows=HD)
                w = chunk(("uq",), QT, 1024)
                for h in range(NH):
                    channels(("qm", h), w, h * P, QT, cqT, T, MID)
                await_read(pe, ("kn", NH - 1))
                pe.wait_ge(q_ready, NH)
                pe.wait_ge(kpe_copied, NH)
                attention("ml", len(units))

                pe.wait_ge(small_in, 80)
                pe.wait_ge(pooled, NM)
                for g in range(NM):
                    ps = pair_for(pe, ("pool", g))
                    wg = wpool_sb[:, g * P:(g + 1) * P]
                    mm(ps[:, 1024 - T:512], wg, u_pad[:, g, C_AT:C_AT + N_CTX], True, True)
                    mm(ps[:, 512:1024], wg, u_pad[:, g, L_AT:L_AT + N_LAT], True, True)\
                        .then_inc(filled[PAIR_OF[("pool", g)]], 1)
                for m, n in MERGE:
                    if m % 4 == 0:
                        wb = chunk(("branch", m // 4, n), NM, 512)
                    if n == 0 and m == 0:
                        pe.wait_ge(g_parts_ready, KD)
                    channels_split(("gate", m, n), HALF_OF[(("gate", m // 4, n), m % 4 // 2)], m % 2 * P, by_channel)
                    if n == 0 and m == 0:
                        await_read(pe, ("pool", NM - 1))
                    if n == 2 and m == 0:
                        pe.wait_ge(o_freed, 2 * NM)
                    channels(("branch", m, n), wb, (m % 4) * P, NM, yT[n], T, MID)
                pe.wait_ge(merged, KD)
                wa, wb = chunk(("out", 0), KD, 512), chunk(("out", 1), KD, 512)
                def out_tile(t):
                    tokens(("y", t), [(wa, 0, 512), (wb, 512, 512)], KD, mergedT, t)

                def tail_turn(t):
                    pe.wait_ge(h2_ready, t + 1)
                    turned(("ht", t), [(h2[:, t, k * P:(k + 1) * P], k * P) for k in range(KD)])

                def tail_logits(t):
                    await_read(pe, ("ht", t))
                    ps = pair_for(pe, ("lg", t))
                    for k in range(KD):
                        last = mm(ps[:, 0:LG], h2T[:, t % 2, k * P:(k + 1) * P], router_sb[:, k * LG:(k + 1) * LG],
                                  k == 0, k == KD - 1)
                    last.then_inc(filled[PAIR_OF[("lg", t)]], 1)

                def count_chosen(_):
                    pe.wait_ge(chosen, 1)
                    ps = pair_for(pe, ("cnt", 0))
                    cf = chs.rearrange("p t n -> p (t n)")
                    mm(ps[:, 0:TT * NE], tri, cf, True, True)
                    mm(ps[:, 128:128 + TT * NE], ones, cf, True, True).then_inc(filled[PAIR_OF[("cnt", 0)]], 1)

                steps_of = {"y": out_tile, "ht": tail_turn, "lg": tail_logits, "mod": modulate, "cnt": count_chosen}
                for kind, n in TAIL:
                    steps_of[kind](n)

                pe.sem_inc(h_filled, 2)
                pe.sem_inc(y_filled, 2)
                pe.sem_inc(t_filled, 2)
                for n in range(NMOD - 3, NMOD):
                    if ("mod", n) in PAIR_OF:
                        await_read(pe, ("mod", n))
                pe.wait_ge(slots_ready, 1)
                pe.wait_ge(blocks_ready, 1)
                n_pairs = pe.value_load(pair_count[0:1], min_val=2, max_val=NB // 2)

                def gathered(b, s, rnd):
                    pe.wait_ge(xg_in[s], rnd * 16 + 16)
                    pe.wait_ge(t_freed, b + 1)
                    for k in range(KD):
                        last = nc.tensor.transpose(pair[0][:, k * P:(k + 1) * P], xg[:, s, k * P:(k + 1) * P], ident)
                    last.then_inc(t_filled, 1)

                def up(b, s, rnd):
                    pe.wait_ge(up_in[s], rnd * 32 + 32)
                    pe.wait_ge(t_freed, b + 2)
                    pe.wait_ge(hid_ready, b + 2)
                    for j in range(2 * FT):
                        w = w13[s][:, (j // FT) * 2048:(j // FT + 1) * 2048].rearrange("p (k f) -> p k f", k=KD)
                        for k in range(KD):
                            last = mm(pair[1][:, s * 512 + j * P:s * 512 + (j + 1) * P],
                                      w[:, k, (j % FT) * P:(j % FT + 1) * P], xgT[:, s, k * P:(k + 1) * P],
                                      k == 0, k == KD - 1)
                    last.then_inc(h_filled, 1)

                def down(b, s, rnd):
                    pe.wait_ge(down_in[s], rnd * 16 + 16)
                    pe.wait_ge(hid_ready, b + 4)
                    pe.wait_ge(y_read, b + 2)
                    out = (pair[2], opair)[s]
                    for j in range(2):
                        for k in range(FT):
                            last = mm(out[:, j * 512:(j + 1) * 512], hid[:, s, k * P:(k + 1) * P],
                                      w2s[s][:, k * D + j * 512:k * D + (j + 1) * 512], k == 0, k == FT - 1)
                    last.then_inc(y_filled, 1)

                gathered(0, 0, 0)
                with pe.Fori(0, n_pairs - 1) as it:
                    up(it * 2, 0, it)
                    gathered(it * 2 + 1, 1, it)
                    down(it * 2, 0, it)
                    up(it * 2 + 1, 1, it)
                    gathered(it * 2 + 2, 0, it + 1)
                    down(it * 2 + 1, 1, it)
                rnd = n_pairs - 1
                up(n_pairs * 2 - 2, 0, rnd)
                gathered(n_pairs * 2 - 1, 1, rnd)
                down(n_pairs * 2 - 2, 0, rnd)
                up(n_pairs * 2 - 1, 1, rnd)
                down(n_pairs * 2 - 1, 1, rnd)
                pe.wait_ge(y_filled, n_pairs * 2 + 2)
                pe.sem_inc(layer_done, 1)
                pe.wait_ge(go["pe"], 1)
                pe.sem_clear(go["pe"])


def kernel(**inputs):
    import numpy as np
    import concourse.bacc as bacc
    from concourse import mybir as mb
    from concourse.bass_utils import run_bass_kernel_spmd

    a = {k: np.asarray(v) for k, v in inputs.items()}
    f = np.float32
    ar = {}
    ar["x0"] = np.concatenate([a["x_prompt"][0], a["x_sample"][0]])
    ar["k_cache_t"] = a["cache_na_k"][0].reshape(DEPTH, N_CACHE, NH * HD).transpose(0, 2, 1)
    ar["v_cache"] = a["cache_na_v"][0].reshape(DEPTH, N_CACHE, NH * HD)
    ar["ckv_cache_t"] = a["cache_mla_ckv"][0].transpose(0, 2, 1)
    ar["kpe_cache_t"] = a["cache_mla_kpe"][0].transpose(0, 2, 1)
    ar["c_t"] = np.stack([a["c_ctx"], a["c"][0]]).reshape(2, KD, P).transpose(2, 1, 0).reshape(P, 2 * KD)
    ones = np.ones((DEPTH, D), f)
    gains = np.stack([ones, a["g_pre_mix"], a["g_post_mix"], ones, a["g_pre_ffn"], a["g_post_ffn"]], 1)
    aux = np.stack([a["b_mod"].reshape(DEPTH, NMOD, 512), gains.reshape(DEPTH, NMOD, 512)], 2).reshape(DEPTH, NMOD, 1, 1024)
    ar["mod_aux"] = np.concatenate([aux, aux], 2)
    ar["w_mod"], ar["w_in"], ar["w_pool"] = a["w_mod"], a["w_in"], a["w_pool"]
    ar["pool_scale"] = a["pool_scale"].reshape(DEPTH, NM, P).transpose(0, 2, 1)
    pad = GW - WIN
    wide = np.concatenate([np.zeros((DEPTH, NH, 15, pad), f), a["na_rpb"], np.zeros((DEPTH, NH, 15, pad), f)], -1)
    rows = np.stack([wide[..., GW - 1 - q:2 * GW - 1 - q] for q in range(GW)], 1)
    ar["rpb_rows"] = rows
    ar["q_norm"] = a["mla_q_norm"].reshape(DEPTH, QT, P).transpose(0, 2, 1)
    ar["kv_norm"] = a["mla_kv_norm"].reshape(DEPTH, KVT, P).transpose(0, 2, 1)
    uq = a["mla_w_uq"].reshape(DEPTH, QL, NH, QKD)
    rope = uq[..., HD:].reshape(DEPTH, QL, NH, 2, 2, RD // 4)
    ar["w_uq"] = np.concatenate([uq, rope[..., ::-1, :].reshape(DEPTH, QL, NH, RD)], -1).reshape(DEPTH, QL, NH * P)
    ukv = a["mla_w_ukv"].reshape(DEPTH, KVL, NH, 2, HD)
    ar["w_ukv"] = ukv.transpose(0, 1, 3, 2, 4).reshape(DEPTH, KVL, 2 * NH * HD)
    ar["w_branch"], ar["w_out"] = a["w_branch"], a["w_out"]
    ar["w_router"] = np.concatenate([a["w_group_router"], a["w_expert_router"]], -1)
    ar["w_gate"] = a["w_exp_gate"].reshape(DEPTH * NE, D, FF)
    ar["w_up"] = a["w_exp_up"].reshape(DEPTH * NE, D, FF)
    ar["w_down"] = a["w_exp_down"].reshape(DEPTH * NE, FF, D)

    p = np.arange(P)
    c0 = np.clip(np.arange(GW) - WIN // 2, 0, GW - WIN)
    kc = np.arange(GW)
    mask = np.where((kc[None] >= c0[:, None]) & (kc[None] < c0[:, None] + WIN), 0.0, NEG)
    nf = RD // 4
    inv = 10000.0 ** (-np.arange(nf, dtype=f) / nf)
    tok = np.arange(N_LAT)
    ang = np.stack([(tok // GW)[:, None] * inv, (tok % GW)[:, None] * inv], 1).astype(f)
    cos = np.stack([np.cos(ang)] * 2, 2).reshape(N_LAT, RD)
    sin = np.stack([-np.sin(ang), np.sin(ang)], 2).reshape(N_LAT, RD)
    ropes = np.zeros((P, N_LAT))
    ropes[HD:QKD], ropes[QKD:P] = cos.T, sin.T
    tiled = {
        "ident": np.eye(P), "tri": p[:, None] < p[None], "ones": np.ones((P, P)), "mask": np.concatenate([mask, mask]),
        "rope": ropes,
        "cos": cos.reshape(4, P, RD).transpose(1, 0, 2).reshape(P, 4 * RD),
        "sin": sin.reshape(4, P, RD).transpose(1, 0, 2).reshape(P, 4 * RD),
        "rev": np.tile(np.arange(EG, 0, -1), (P, TT)),
        "tok": np.arange(TT)[None] * P + p[:, None], "blk": np.tile(np.arange(NB), (P, 1)),
    }
    n = 64
    t = np.concatenate([np.arange(8), np.arange(n - 8, n)])
    tiled["edge"] = np.tile(np.concatenate([w / (np.clip(t + w - w // 2, 0, n) - np.clip(t - w // 2, 0, n)) for w in POOL_W]), (P, 1))
    ar["consts"] = np.concatenate([tiled[n].astype(f) for n, _ in CONST_COLS], 1)

    ar["zeros"] = np.zeros((BLOCK, D), f)

    outs = {"x_res": (T, D), "o_nk_t": (DEPTH, NH * HD, N_CTX), "o_nv": (DEPTH, N_CTX, NH * HD),
            "o_ckv_t": (DEPTH, KVL, N_CTX), "o_kpe": (DEPTH, N_CTX, RD)}
    nc = bacc.Bacc("TRN2", target_bir_lowering=False, num_devices=1)
    arrays, args = {}, {}
    for name, v in ar.items():
        v = np.ascontiguousarray(v)
        arrays["in_" + name] = v
        args[name] = nc.dram_tensor("in_" + name, v.shape, mb.dt.from_np(v.dtype), kind="ExternalInput").ap()
    for name, shape in outs.items():
        args[name] = nc.dram_tensor("out_" + name, shape, mb.dt.float32, kind="ExternalOutput").ap()
    bass_hybrid_step(nc, **args)
    r = run_bass_kernel_spmd(nc, [arrays], core_ids=[0]).results[0]
    x = r["out_x_res"]
    return (x[None, :N_CTX], x[None, N_CTX:],
            r["out_o_nk_t"].transpose(0, 2, 1).reshape(1, DEPTH, N_CTX, NH, HD),
            r["out_o_nv"].reshape(1, DEPTH, N_CTX, NH, HD),
            r["out_o_ckv_t"].transpose(0, 2, 1)[None], r["out_o_kpe"][None])
```

```python
import concourse.bass as bass
from concourse import mybir
from contextlib import ExitStack

F32 = mybir.dt.float32
F32R = mybir.dt.float32r
U32 = mybir.dt.uint32
ALU = mybir.AluOpType
ACT = mybir.ActivationFunctionType
AX_X = mybir.AxisListType.X
ds = bass.ds

P = 128
D = 1024
KD = D // P
N_CTX, N_LAT = 128, 512
T = N_CTX + N_LAT
TT = T // P
N_CACHE = 128
KEYS = T + N_CACHE
KT = KEYS // P
DEPTH = 2
GW = 64
ROWS = N_LAT // GW
WIN = 16
NH, HD = 8, 64
NM = NH * HD // P
RD = 32
QKD = HD + RD
QL, KVL = 384, 256
QT, KVT = QL // P, KVL // P
LOW = QL + KVL + RD
MOD = 6 * D
NMOD = MOD // 512
EPS = 1e-6
NG, EG = 4, 4
NE = NG * EG
FF = 256
FT = FF // P
DR = 14
POOL_W = (2, 4, 8, 16)
PADT = 8 + N_CTX + 16 + N_LAT + 8
C_AT, L_AT = 8, 8 + N_CTX + 16
BLOCK = P
NB = (2 * T + NE * (BLOCK - 1)) // BLOCK
NB += NB % 2
NEG = -1e30
LEAST = -3e38

U_AT, NQ_AT, NK_AT, NV_AT, LOW_AT, G_AT = 0, 512, 1024, 1536, 2048, 2048 + LOW

NPAIR = 3
NSLOT = 3
SLOT = 4096
LAG_PT, LAG_PV = 2, 3


def attention_steps():
    return [(h, t) for h in range(NH) for t in range(1, TT)]


MERGE = [(m, n) for c in range(2) for n in range(3) for m in range(4 * c, 4 * c + 4)]

CONST_COLS = [("ident", P), ("tri", P), ("ones", P), ("mask", GW), ("rope", N_LAT), ("cos", 4 * RD), ("sin", 4 * RD),
              ("rev", TT * EG), ("tok", TT), ("blk", NB), ("first", NB + 1), ("behind", P),
              ("edge", 4 * 16)]


MODS = [(j, 0) for j in range(4, NMOD)] + [(j, 1) for j in range(4)]
N_NA, N_ML, N_IN = 2, 4, 6
MOD_UNIT = 16
TAIL = [("y", 0), ("y", 1), ("ht", 0), ("y", 2), ("lg", 0), ("ht", 1), ("y", 3), ("lg", 1), ("ht", 2), ("y", 4),
        ("lg", 2), ("ht", 3), ("mod", 6), ("lg", 3), ("ht", 4), ("mod", 7), ("lg", 4), ("mod", 8), ("cnt", 0),
        ("mod", 9), ("mod", 10), ("list", 0), ("mod", 11)]


def mod_before(n):
    return n - 1 if n < N_IN else n - 2 if n >= N_IN + 2 else None


def plan_jobs():
    jobs = [("xt", t) for t in range(TT)]
    jobs += [("nk", m) for m in range(NM)] + [("nv", a, t) for a in range(2) for t in range(TT)]
    jobs += [("nq", m) for m in range(NM)] + [("u", m) for m in range(NM)]
    for t in range(TT):
        jobs.append(("low", t))
        if t:
            jobs.append(("lowt", t - 1))
    jobs.append(("lowt", TT - 1))

    def attention(kind, n_mod):
        jobs.extend([(kind + "c", 0), ("mod", n_mod), (kind + "c", 1), (kind + "s", 0), ("mod", n_mod + 1), (kind + "c", 2)])
        units = attention_steps()
        for i in range(len(units) + LAG_PV):
            if 0 < i < len(units):
                jobs.append((kind + "s", i))
            if kind == "ml" and i == MOD_UNIT:
                jobs.append(("mod", N_ML))
            if 0 <= i - LAG_PT < len(units):
                jobs.append((kind + "t", i - LAG_PT))

    attention("na", 0)
    jobs += [("vm", t) for t in range(KT)] + [("kn", m) for m in range(NM)] + [("qm", h) for h in range(NH)]
    attention("ml", N_NA)
    jobs.append(("mod", N_ML + 1))
    jobs += [("pool", g) for g in range(NM)]
    for m, n in MERGE:
        jobs += [("gate", m, n), ("branch", m, n)]
    return jobs + TAIL


HALVES = [(("nk",), a, ("nk", 2 * a + 1)) for a in range(2)] + [(("nv",), a, ("nv", a, TT - 1)) for a in range(2)]
HALVES += [((kind,), a, (kind, 2 * a + 1)) for kind in ("nq", "u") for a in range(2)]
N_WIN = len(HALVES)
HALVES += [(("gate", c, n), a, ("gate", 4 * c + 2 * a + 1, n)) for c in range(2) for n in range(3) for a in range(2)]
HALF_OF = {(key, a): i for i, (key, a, _) in enumerate(HALVES)}


def plan_chunks():
    def mods(a, b):
        return [(("mod", n), ("mod", n)) for n in range(a, b)]

    chunks = [((kind,), None) for kind in ("nk", "nv", "nq", "u")]
    chunks += [(("low", 0), ("low", TT - 1)), (("low", 1), ("low", TT - 1))]
    chunks += mods(0, N_NA) + [(("ukv",), ("kn", NM - 1)), (("uq",), ("qm", NH - 1))] + mods(N_NA, N_IN)
    for c in range(2):
        for n in range(3):
            chunks += [(("gate", c, n), None), (("branch", c, n), ("branch", 4 * c + 3, n))]
    chunks += [(("out", 0), ("y", TT - 1)), (("out", 1), ("y", TT - 1))] + mods(N_IN, NMOD)
    return chunks


def bass_hybrid_step(nc, x0, k_cache_t, v_cache, ckv_cache_t, kpe_cache_t, c_t, mod_aux, w_mod, w_in, w_pool,
                     pool_scale, rpb_rows, q_norm, kv_norm, w_uq, w_ukv, w_branch, w_out, w_router,
                     w_gate, w_up, w_down, consts, zeros,
                     x_res, o_nk_t, o_nv, o_ckv_t, o_kpe):
    jobs, chunks = plan_jobs(), plan_chunks()
    PAIR_OF = {key: i % NPAIR for i, key in enumerate(jobs)}
    USE_OF = {key: i // NPAIR + 1 for i, key in enumerate(jobs)}
    SLOT_OF = {key: i % NSLOT for i, (key, _) in enumerate(chunks)}
    FILL_OF = {key: i // NSLOT + 1 for i, (key, _) in enumerate(chunks)}

    with ExitStack() as ctx:
        sems = []

        def sem(name):
            s = ctx.enter_context(nc.semaphore(name))
            sems.append(s)
            return s

        def sb(name, shape, dt=F32):
            return ctx.enter_context(nc.sbuf_tensor(name, shape, dt))

        def twins(name, n):
            with nc.sbuf_tensor(name + "_r", [P, n], F32R) as as_r:
                pass
            return sb(name, [P, n]), as_r

        ring = sb("ring", [P, NSLOT * SLOT])
        hT = sb("hT", [P, KD * T])
        ysT, ysT_r = twins("ysT", 2 * NM * T)
        NQ_W, T_W, NK_W, NV_W = NM * T, NH * DR * GW, NM * KEYS, KT * 512
        R1_W = NQ_W + T_W + NK_W + NV_W
        r1, r1_r = twins("r1", R1_W)
        PART = KD * 256
        mid, mid_r = twins("mid", 4 * PART)
        LOW_W = QT * T + KVT * KEYS
        assert LOW_W + KEYS + 2 * LOW + 4 * T <= 4 * PART
        u_sb = sb("u_sb", [P, NM * PADT])
        cst = sb("cst", [P, consts.shape[1]])
        small = sb("small", [P, 1000])
        wpool_sb = sb("wpool_sb", [P, NM * P])
        router_sb = sb("router_sb", [P, KD * (NG + NE)])
        cols = sb("cols", [P, 2 * KD + NM + QT + KVT + 4])
        ids = sb("ids", [P, 64], U32)

        def view(buf, at, n, **kw):
            v = buf[:, at:at + n]
            if kw:
                (name, size), = kw.items()
                v = v.rearrange(f"p ({name} z) -> p {name} z", **{name: size})
            return v

        low_t = view(mid, 0, LOW_W)
        kpeT = view(mid, LOW_W, KEYS)
        low_tm = view(mid, LOW_W + KEYS, 2 * LOW)
        pp = view(mid, LOW_W + KEYS + 2 * LOW, 4 * T)
        w_high = [view(mid_r, 2 * i * PART, PART, k=KD) for i in range(2)]
        w_low = [view(mid_r, (2 * i + 1) * PART, PART, k=KD) for i in range(2)]
        h_high, h_low = view(ysT_r, 0, TT * D, t=TT), view(r1_r, NQ_W, TT * D, t=TT)
        g_high, g_low = view(r1_r, 0, KD * T, k=KD), view(r1_r, KD * T, KD * T, k=KD)

        xt = view(r1, KD * T, TT * D, t=TT)
        bc1 = [view(hT, 2 * D, 2 * D, a=2),
               view(r1, 13 * D, 2 * D, a=2)]
        assert 12 * D + 4 * FF <= 13 * D and 15 * D <= R1_W and KD * T == 5 * D
        hb = view(pp, 0, 2 * D, a=2)
        h_t = view(hT, 0, KD * T, k=KD)
        nqT = view(r1, 0, NQ_W, m=NM)
        tb = view(r1, NQ_W, T_W, h=NH)
        nkT = view(r1, NQ_W + T_W, NK_W, m=NM)
        nv = view(r1, NQ_W + T_W + NK_W, NV_W, t=KT)
        qT = view(r1, 0, NH * T, h=NH)
        kT = view(r1, NH * T, NH * KEYS, h=NH)
        vm = view(r1, NH * T + NH * KEYS, KT * 512, t=KT)
        assert NH * T + NH * KEYS + KT * 512 <= R1_W
        cqT = view(low_t, 0, QT * T, k=QT)
        ckvT = view(low_t, QT * T, KVT * KEYS, k=KVT)
        ltm = view(low_tm, 0, 2 * LOW, a=2)
        probs = [view(pp, 0, T), view(pp, T, T), view(low_tm, 0, T)]
        probT = [view(pp, 2 * T, T), view(pp, 3 * T, T)]
        c_probs, c_probT = view(pp, 0, NH * P, h=NH), view(pp, 2 * T, NH * P, h=NH)
        yT = [None, view(ysT, 0, NM * T, m=NM), view(ysT, NM * T, NM * T, m=NM)]
        u_pad = view(u_sb, 0, NM * PADT, m=NM)
        sum_a = view(ysT, NM * T, PADT)
        sum_b = view(ysT, NM * T + PADT, PADT)
        mergedT = view(hT, 0, KD * T, k=KD)
        yT[0] = view(r1, 2 * KD * T, NM * T, m=NM)
        sig = view(r1, (2 * KD + NM) * T, 2 * T, a=2)
        prod = view(r1, (2 * KD + NM + 2) * T, 2 * T, a=2)
        x2 = view(r1, KD * T, TT * D, t=TT)
        gb1 = view(u_sb, 0, 2 * D, a=2)
        bc2 = view(r1, 0, 4 * D, a=4)
        yb = view(pp, 0, 2 * D, a=2)
        h2 = view(ysT, 0, TT * D, t=TT)
        h2T = view(low_t, 0, 2 * D, a=2)
        squares = view(r1, 4 * D, D)
        tail = (2 * KD + NM + 4) * T
        st_ml = view(r1, NH * T + NH * KEYS + KT * 512, 512)
        assert NH * T + NH * KEYS + KT * 512 + 512 + 1024 <= R1_W and tail + 512 <= R1_W
        aux_na, aux_ml = view(ysT, NM * T + 2 * PADT, 1024), view(r1, R1_W - 1024, 1024)
        st_in = view(low_tm, T, 512)
        aux = [aux_na] * N_NA + [aux_ml] * (N_IN - N_NA) + [view(low_tm, 0, 1024), view(low_t, 2 * D, 1024)] * 3
        modst = [st_in] * N_NA + [st_ml] * (N_IN - N_NA) + [view(r1, tail, 512), view(pp, 2 * D, 512)] * 3
        w13 = [view(ring, (1 - s) * 6144, 4096) for s in range(2)]
        w2s = [view(ring, (1 - s) * 6144 + 4096, 2048) for s in range(2)]
        pro_w = [view(ring, i * SLOT, SLOT, k=KD) for i in range(3)] + [view(hT, 0, SLOT, k=KD)]
        pro_aux = view(ysT, 0, 4 * 1024, a=4)
        pro_st = view(mid, 0, 4 * 512, a=4)
        xg = view(r1, 0, 2 * D, a=2)
        xgT = view(r1, 2 * D, 2 * D, a=2)
        yo = view(r1, 10 * D, 2 * D, a=2)
        sil = view(r1, 12 * D, 2 * FF, a=2)
        hid = view(r1, 12 * D + 2 * FF, 2 * FF, a=2)
        gb2 = view(hT, 0, 2 * D, a=2)
        picks = [view(ysT, 2 * t * D, 2 * D, a=2) if t < 2 else view(r1, (0, 2, 10)[t - 2] * D, 2 * D, a=2) for t in range(TT)]
        assert 10 * D >= 2 * KD * T and 12 * D + 4 * FF <= R1_W

        at = 0
        where = {}
        for name, n in CONST_COLS:
            where[name] = (at, at + n)
            at += n

        def const(name):
            a, b = where[name]
            return cst[:, a:b]

        ident, tri, ones = const("ident"), const("tri"), const("ones")
        cvec = view(cols, 0, 2 * KD, k=KD)
        psc = cols[:, 2 * KD:2 * KD + NM]
        lown = cols[:, 2 * KD + NM:2 * KD + NM + QT + KVT]

        sm_at = [0]

        def sm(n):
            a = sm_at[0]
            sm_at[0] += n
            assert sm_at[0] <= 1000
            return small[:, a:a + n]

        ss, ssx, rs, rstd = sm(8), sm(8), sm(8), sm(8)
        ss2, rs2, rstd2 = sm(12), sm(12), sm(12)
        mx, negm, rsum, rinv = sm(2), sm(1), sm(3), sm(2)
        mxs = [mx, sm(2)]
        c_max, c_sum, c_inv = sm(NH), sm(NH), sm(NH)
        negms = [negm] + [sm(1) for _ in range(2)]
        rsums = [rsum[:, i:i + 1] for i in range(3)]
        cvraw = sm(2 * KD)
        LG = NG + NE
        lg = sm(TT * LG).rearrange("p (t n) -> p t n", t=TT)

        def smt(n):
            return sm(TT * n).rearrange("p (t n) -> p t n", t=TT)

        gmax, gsum, gate1, gate2, m1, m2 = smt(1), smt(1), smt(1), smt(1), smt(1), smt(1)
        e4, oh_g, el, oh1, oh2, w4 = smt(4), smt(4), smt(4), smt(4), smt(4), smt(4)
        ch1, ch2, chs = smt(NE), smt(NE), smt(NE)
        slots = smt(NE)
        both = sm(2 * TT).rearrange("p (i n) -> p i n", n=1)
        slot1, slot2 = both[:, 0:TT, :], both[:, TT:2 * TT, :]
        place = sm(2 * TT).rearrange("p (i n) -> p i n", n=1)
        reached = view(pp, 512, 2 * TT * (NB + 1), i=2 * TT)
        in_block = view(pp, 1024, 2 * TT * NB, i=2 * TT)
        at_place = view(low_t, 0, 2 * TT * P, i=2 * TT)
        elm, big = smt(4), smt(1)
        rot = sm(RD)
        swapped = view(low_tm, T, N_LAT)
        n_e, blocks, blk_end, blk_start = sm(NE), sm(NE), sm(NE), sm(NE)
        bexp, npair_f, halves = sm(NB), sm(1), sm(NB // 2)
        bcmp = view(pp, 0, NB * NE, a=NB)
        slot_ids = ids[:, 0:2 * TT]
        blk_ids = ids[:, 16:16 + NB]
        pair_count = ids[:, 16 + NB:17 + NB]
        src_id = [ids[:, 60:61], ids[:, 61:62]]
        src_ids = sb("src_ids", [P, NB], U32)[:, :]

        pair = [ctx.enter_context(nc.psum_tensor(f"pair{i}", [P, 1024], F32)) for i in range(NPAIR)]
        opair = ctx.enter_context(nc.psum_tensor("opair", [P, 1024], F32))
        MID = 512 - T // 2
        TMID = 512 - 2 * P
        KMID = 512 - KEYS // 2
        LMID = 512 - LOW // 2

        spare = 2 * T // BLOCK
        mod_rows = nc.dram_tensor("mod_rows", [2, MOD], F32).ap()
        h2_rows = nc.dram_tensor("h2_rows", [T, D], F32).ap()
        expert_out = nc.dram_tensor("expert_out", [NB * BLOCK, D], F32).ap()

        consts_in, x_loaded, x_stored, cv_in, cv_ready = (
            ctx.enter_context(nc.semaphore(n)) for n in ("consts_in", "x_loaded", "x_stored", "cv_in", "cv_ready"))
        pro_in = [ctx.enter_context(nc.semaphore(f"pro_in{i}")) for i in range(4)]
        pro_aux_in, pro_filled, pro_step, pro_rows, pro_stored, pro_bc_in, x_squared = (
            ctx.enter_context(nc.semaphore(n)) for n in ("pro_aux_in", "pro_filled", "pro_step", "pro_rows", "pro_stored", "pro_bc_in", "x_squared"))
        layer_done = ctx.enter_context(nc.semaphore("layer_done"))
        go = {e: ctx.enter_context(nc.semaphore("go_" + e)) for e in ("pe", "act", "dve", "pool")}
        filled = [sem(f"filled{i}") for i in range(NPAIR)]
        freed = [sem(f"freed{i}") for i in range(NPAIR)]
        landed = [sem(f"landed{i}") for i in range(NSLOT)]
        aux_in = [sem(f"aux_in{i}") for i in range(2)]
        mod_row, bc_in = sem("mod_row"), sem("bc_in")
        mod_stored = [sem(f"mod_stored{i}") for i in range(2)]
        bias_in, bias_masked, caches_in, small_in, kpe_in = (sem(n) for n in ("bias_in", "bias_masked", "caches_in", "small_in", "kpe_in"))
        pooled, pool_step, kpe_copied = (sem(n) for n in ("pooled", "pool_step", "kpe_copied"))
        dve_step, act_step = sem("dve_step"), sem("act_step")
        ms_ready, root_ready = sem("ms_ready"), sem("root_ready")
        h_ready = sem("h_ready")
        high_ready, parts_ready, h_high_ready, h_parts_ready, g_high_ready, g_parts_ready = (
            sem(n) for n in ("high_ready", "parts_ready", "h_high_ready", "h_parts_ready", "g_high_ready", "g_parts_ready"))
        low_sq, low_ms, low_root, low_scaled = sem("low_sq"), sem("low_ms"), sem("low_root"), sem("low_scaled")
        caches_out, kpe_out = sem("caches_out"), sem("kpe_out")
        q_ready = sem("q_ready")
        c_shifted, c_exped, c_scaled = sem("c_shifted"), sem("c_exped"), sem("c_scaled")
        biased, exped, scaled, pv_done, o_freed = (sem(n) for n in ("biased", "exped", "scaled", "pv_done", "o_freed"))
        merged, x2_in, gb_in, bc2_in = sem("merged"), sem("x2_in"), sem("gb_in"), sem("bc2_in")
        x2_new, h2_ready, h2_stored = sem("x2_new"), sem("h2_ready"), sem("h2_stored")
        routed_a, routed_b, chosen, slots_ready, marks_ready, blocks_ready = (
            sem(n) for n in ("routed_a", "routed_b", "chosen", "slots_ready", "marks_ready", "blocks_ready"))
        id_ready, ran_on = sem("id_ready"), sem("ran_on")
        xg_in = [sem(f"xg_in{i}") for i in range(2)]
        picked = [sem(f"picked{i}") for i in range(TT)]
        up_in = [sem(f"up_in{i}") for i in range(2)]
        down_in = [sem(f"down_in{i}") for i in range(2)]
        t_filled, t_freed, h_filled, sil_ready, hid_ready, y_filled, y_read = (
            sem(n) for n in ("t_filled", "t_freed", "h_filled", "sil_ready", "hid_ready", "y_filled", "y_read"))
        yo_stored = [sem(f"yo_stored{i}") for i in range(2)]
        rows_zeroed = sem("rows_zeroed")
        gated, normed, added = sem("gated"), sem("normed"), sem("added")
        mixed, sq3, ms3, root3 = (sem(n) for n in ("mixed", "sq3", "ms3", "root3"))

        assert [s.num for s in sems] == list(range(sems[0].num, sems[-1].num + 1))

        def pair_for(eng, key):
            if USE_OF[key] > 1:
                eng.wait_ge(freed[PAIR_OF[key]], USE_OF[key] - 1)
            return pair[PAIR_OF[key]]

        def await_job(eng, key):
            eng.wait_ge(filled[PAIR_OF[key]], USE_OF[key])
            return pair[PAIR_OF[key]]

        def await_read(eng, key):
            eng.wait_ge(freed[PAIR_OF[key]], USE_OF[key])

        def half_source(eng, i):
            key, a, _ = HALVES[i]
            eng.wait_ge(landed[SLOT_OF[key]], 16 * FILL_OF[key])
            return view(ring, SLOT_OF[key] * SLOT, SLOT, k=KD)[:, :, a * 256:(a + 1) * 256]

        def await_mod_stored(eng, n):
            eng.wait_ge(mod_stored[n % 2], 16 * (n // 2 + 1))

        block = ctx.enter_context(nc.Block())

        @block.sync
        def _(sp):
            sp.dma_start(cst[:, :], consts).then_inc(consts_in, 16)
            sp.dma_start(cvraw, c_t).then_inc(cv_in, 16)
            for i in range(4):
                sp.dma_start(pro_w[i], w_mod[0, :, i * 512:(i + 1) * 512].rearrange("(k p) n -> p k n", p=P)).then_inc(pro_in[i], 16)
            sp.dma_start(pro_aux[0:2], mod_aux[0, 0:4].rearrange("b r n -> r b n")).then_inc(pro_aux_in, 16)
            sp.dma_start(xt, x0.rearrange("(t p) d -> p t d", p=P)).then_inc(x_loaded, 16)
            sp.dma_start(x_res, x0).then_inc(x_stored, 16)
            sp.wait_ge(pro_rows, 4)
            sp.dma_start(mod_rows[:, 0:4 * 512].rearrange("r (b n) -> r b n", b=4), pro_st[0:2]).then_inc(pro_stored, 16)

            def load_rows(signal):
                for g in range(2):
                    for i, c0 in enumerate((D, 0)):
                        sp.dma_start(bc1[g][:, i, :], mod_rows[g:g + 1, c0:c0 + D].partition_broadcast(P)).then_inc(signal, 16)

            sp.wait_ge(pro_stored, 16)
            load_rows(pro_bc_in)
            with sp.Fori(0, DEPTH) as L:
                def src(key):
                    kind = key[0]
                    wl = w_in[ds(L, 1)].rearrange("a (k p) n -> p (a k) n", p=P)
                    if kind == "mod":
                        j, ahead = MODS[key[1]]
                        w = w_mod[ds((L + ahead) % DEPTH, 1)].rearrange("a (k p) n -> p (a k) n", p=P)
                        return w[:, :, j * 512:(j + 1) * 512]
                    if kind in ("u", "nq", "nk", "nv"):
                        c0 = {"u": U_AT, "nq": NQ_AT, "nk": NK_AT, "nv": NV_AT}[kind]
                        return wl[:, :, c0:c0 + 512]
                    if kind == "low":
                        c0 = LOW_AT + key[1] * (LOW // 2)
                        return wl[:, :, c0:c0 + LOW // 2]
                    if kind == "ukv":
                        return w_ukv[ds(L, 1)].rearrange("a (k p) n -> p (a k) n", p=P)
                    if kind == "uq":
                        return w_uq[ds(L, 1)].rearrange("a (k p) n -> p (a k) n", p=P)
                    if kind == "gate":
                        c0 = G_AT + key[2] * D + key[1] * 512
                        return wl[:, :, c0:c0 + 512]
                    if kind == "branch":
                        w = w_branch[ds(L, 1)].rearrange("a n (k p) d -> p (a n k) d", p=P)
                        return w[:, 4 * key[2]:4 * key[2] + 4, key[1] * 512:(key[1] + 1) * 512]
                    w = w_out[ds(L, 1)].rearrange("a (k p) n -> p (a k) n", p=P)
                    return w[:, :, key[1] * 512:(key[1] + 1) * 512]

                def zero_spare_blocks():
                    spare_blocks = expert_out.rearrange("(b p) d -> b p d", p=P)
                    n_zeroed = (NB - spare) - L * (NB - spare - 1)
                    with sp.Fori(0, n_zeroed) as b:
                        sp.dma_start(spare_blocks[ds(b + spare, 1)].rearrange("a p d -> p (a d)"), zeros).then_inc(rows_zeroed, 16)
                    with sp.Fori(0, L * (NB - spare - 1) + 1):
                        sp.sem_inc(rows_zeroed, 16)

                stored = [0]

                def store_mods(upto):
                    while stored[0] <= upto:
                        n = stored[0]
                        j = MODS[n][0]
                        sp.wait_ge(mod_row, n + 1)
                        sp.dma_start(mod_rows[:, j * 512:(j + 1) * 512], modst[n][0:2]).then_inc(mod_stored[n % 2], 16)
                        stored[0] += 1

                for i, (key, _) in enumerate(chunks):
                    if i >= NSLOT:
                        before, last_reader = chunks[i - NSLOT]
                        if last_reader is None:
                            sp.wait_ge(parts_ready, HALF_OF[(before, 1)] + 1)
                        else:
                            await_job(sp, last_reader)
                        if before[0] == "mod":
                            store_mods(before[1])
                    s = src(key)
                    k, n = s.shape[1], s.shape[2]
                    dst = view(ring, SLOT_OF[key] * SLOT, k * n, k=k)
                    sp.dma_start(dst, s).then_inc(landed[SLOT_OF[key]], 16)
                    if key[0] == "uq":
                        zero_spare_blocks()
                    if key[0] == "mod":
                        n = key[1]
                        j, ahead = MODS[n]
                        if mod_before(n) is not None:
                            store_mods(mod_before(n))
                        if n == 0:
                            await_job(sp, ("u", NM - 1))
                        if n == N_NA:
                            sp.wait_ge(o_freed, NM)
                        if n == N_IN:
                            store_mods(n - 1)
                            await_mod_stored(sp, n - 1)
                            await_job(sp, ("gate", KD - 1, 2))
                        sp.dma_start(aux[n][0:2], mod_aux[ds((L + ahead) % DEPTH, 1)][:, j:j + 1].rearrange("a b r n -> (a b r) n"))\
                            .then_inc(aux_in[n % 2], 16)

                sp.wait_ge(blocks_ready, 1)
                n_pairs = sp.value_load(pair_count[0:1], min_val=1, max_val=NB // 2)
                await_job(sp, ("mod", NMOD - 2))
                with sp.Fori(0, n_pairs) as it:
                    for s in range(2):
                        if s:
                            await_job(sp, ("mod", NMOD - 1))
                        e = sp.value_load(blk_ids[0:1, ds(it * 2 + s, 1)], min_val=0, max_val=NE - 1)
                        sp.wait_ge(h_filled, it * 2 + (s + 1))
                        for w, at_ in ((w_gate, 0), (w_up, 2048)):
                            sp.dma_start(w13[s][:, at_:at_ + 2048].rearrange("p (k f) -> p k f", k=KD),
                                         w[ds(L * NE + e, 1)].rearrange("a (k p) f -> p (a k) f", p=P)).then_inc(up_in[s], 16)
                        sp.wait_ge(y_filled, it * 2 + (s + 1))
                        sp.dma_start(w2s[s].rearrange("p (k f) -> p k f", k=FT),
                                     w_down[ds(L * NE + e, 1)].rearrange("a (k p) f -> p (a k) f", p=P)).then_inc(down_in[s], 16)
                store_mods(NMOD - 1)
                for n in (NMOD - 2, NMOD - 1):
                    await_mod_stored(sp, n)
                sp.wait_ge(picked[TT - 1], 32)
                load_rows(bc_in)
                for t in range(TT):
                    if t < TT - 1:
                        sp.wait_ge(added, t + 1)
                    else:
                        sp.wait_ge(x2_new, TT + 1)
                    sp.dma_start(x_res[t * P:(t + 1) * P, :], x2[:, t, :]).then_inc(x_stored, 16)
                sp.wait_ge(bc_in, 64)

                sp.wait_ge(layer_done, 4)
                sp.sem_clear(range(sems[0].num, sems[-1].num + 1))
                sp.sem_clear(layer_done)
                for e in ("pe", "act", "dve", "pool"):
                    sp.sem_inc(go[e], 1)
            sp.wait_ge(x_stored, 16 + DEPTH * 16 * TT)

        @block.scalar
        def _(act):
            def token_squares(t):
                nc.scalar.activation(mid[:, (3 + t) * D:(4 + t) * D], xt[:, t, :], ACT.Square, accum_out=ssx[:, t:t + 1])\
                    .then_inc(x_squared, 1)

            act.wait_ge(cv_in, 16)
            nc.scalar.activation(cols[:, 0:2 * KD], cvraw, ACT.Silu).then_inc(cv_ready, 1)
            act.wait_ge(x_loaded, 16)
            for t in range(TT):
                token_squares(t)
            act.wait_ge(x_squared, TT)
            with act.Fori(0, DEPTH) as L:
                def layer(t):
                    return t[ds(L, 1)]

                steps = [0]

                def chain(ins):
                    ins.then_inc(act_step, 1)
                    steps[0] += 1
                    act.wait_ge(act_step, steps[0])

                act.wait_ge(ms_ready, 1)
                nc.scalar.activation(rs[:, 0:TT], rs[:, 0:TT], ACT.Sqrt).then_inc(root_ready, 1)
                act.dma_start(cols[:, 2 * KD:2 * KD + NM], layer(pool_scale).rearrange("a p n -> p (a n)")).then_inc(small_in, 16)
                act.dma_start(lown[:, 0:QT], layer(q_norm).rearrange("a p n -> p (a n)")).then_inc(small_in, 16)
                act.dma_start(lown[:, QT:QT + KVT], layer(kv_norm).rearrange("a p n -> p (a n)")).then_inc(small_in, 16)
                act.dma_start(view(wpool_sb, 0, NM * P, g=NM), layer(w_pool).rearrange("a g c d -> c (a g) d")).then_inc(small_in, 16)
                act.dma_start(view(router_sb, 0, KD * LG, k=KD), layer(w_router).rearrange("a (k p) n -> p (a k) n", p=P)).then_inc(small_in, 16)
                def split_high(i):
                    if i >= 2:
                        await_job(act, HALVES[i - 2][2])
                    w = half_source(act, i)
                    nc.scalar.copy(w_high[i % 2], w).then_inc(high_ready, 1)

                act.wait_ge(pro_stored, 16)
                act.dma_start(nkT[:, :, T:KEYS], layer(k_cache_t).rearrange("a (m p) t -> p (a m) t", p=P)).then_inc(caches_in, 16)
                act.dma_start(nv[:, KT - 1, :], layer(v_cache).rearrange("a p n -> p (a n)")).then_inc(caches_in, 16)
                for t in range(TT):
                    ps = await_job(act, ("xt", t))
                    nc.scalar.copy(h_high[:, t, :], ps[:, :]).then_inc(h_high_ready, 1)
                    nc.scalar.copy(h_t[:, :, t * P:(t + 1) * P], ps[:, :].rearrange("p (k c) -> p k c", k=KD))\
                        .then_inc(freed[PAIR_OF[("xt", t)]], 1)
                    if t == 2:
                        split_high(0)
                split_high(1)
                for m in range(NM):
                    ps = await_job(act, ("nk", m))
                    nc.scalar.copy(nkT[:, m, 0:T], ps[:, TMID:TMID + T]).then_inc(freed[PAIR_OF[("nk", m)]], 1)
                    if m % 2:
                        split_high(2 + m // 2)
                await_read(act, ("nk", NM - 1))
                act.dma_start(layer(o_nk_t).rearrange("a (m p) t -> p (a m) t", p=P), nkT[:, :, 0:N_CTX]).then_inc(caches_out, 16)
                split_high(4)
                split_high(5)
                await_read(act, ("nv", 1, 0))
                act.dma_start(layer(o_nv).rearrange("a p n -> p (a n)"), nv[:, 0, :]).then_inc(caches_out, 16)
                for m in range(NM):
                    ps = await_job(act, ("nq", m))
                    nc.scalar.mul(nqT[:, m, :], ps[:, TMID:TMID + T], HD ** -0.5).then_inc(freed[PAIR_OF[("nq", m)]], 1)
                    if m % 2:
                        split_high(6 + m // 2)
                await_job(act, ("u", NM - 1))
                act.dma_start(ckvT[:, :, T:KEYS], layer(ckv_cache_t).rearrange("a (k p) t -> p (a k) t", p=P)).then_inc(caches_in, 16)
                act.dma_start(kpeT[HD:QKD, T:KEYS], layer(kpe_cache_t).rearrange("a p t -> p (a t)")).then_inc(caches_in, 16)
                tr = layer(rpb_rows).rearrange("a q h r c -> q (a h) r c")
                tb4 = tb.rearrange("p h (r c) -> p h r c", c=GW)
                act.dma_start(tb4[0:GW], tr[:, :, 1:1 + DR, :]).then_inc(bias_in, 16)
                act.dma_start(tb4[GW:P], tr[:, :, 0:DR, :]).then_inc(bias_in, 16)

                for t in range(TT):
                    ps = await_job(act, ("low", t))
                    nc.scalar.activation(pp[:, 0:QL], ps[:, LMID:LMID + QL], ACT.Square,
                                         accum_out=ss2[:, 2 * t:2 * t + 1])
                    nc.scalar.activation(pp[:, QL:QL + KVL], ps[:, LMID + QL:LMID + QL + KVL], ACT.Square,
                                         accum_out=ss2[:, 2 * t + 1:2 * t + 2]).then_inc(low_sq, 1)
                    if t >= 2:
                        await_job(act, ("lowt", t - 2))
                        if t == 2:
                            act.wait_ge(kpe_out, 16)
                    nc.scalar.copy(ltm[:, t % 2, :], ps[:, LMID:LMID + LOW]).then_inc(freed[PAIR_OF[("low", t)]], 1)
                    if t == 0:
                        await_read(act, ("low", 0))
                        act.dma_start(layer(o_kpe).rearrange("a p n -> p (a n)"), ltm[:, 0, QL + KVL:LOW]).then_inc(kpe_out, 16)
                    act.wait_ge(low_ms, t + 1)
                    nc.scalar.activation(rs2[:, 2 * t:2 * t + 2], rs2[:, 2 * t:2 * t + 2], ACT.Sqrt).then_inc(low_root, 1)
                await_read(act, ("lowt", 0))
                act.dma_start(layer(o_ckv_t).rearrange("a (k p) t -> p (a k) t", p=P), ckvT[:, :, 0:N_CTX]).then_inc(caches_out, 16)

                units = attention_steps()

                def attention(kind, base):
                    scale = 1.0 if kind == "na" else QKD ** -0.5
                    act.wait_ge(c_shifted, 1 + base // len(units))
                    nc.scalar.activation(c_probs, c_probs, ACT.Exp, scale=scale).then_inc(c_exped, 1)
                    ps = await_job(act, (kind + "c", 1))
                    nc.scalar.copy(c_probT, ps[:, :].rearrange("p (h c) -> p h c", h=NH)).then_inc(freed[PAIR_OF[(kind + "c", 1)]], 1)
                    for i in range(len(units) + LAG_PV):
                        j = i - LAG_PT
                        if 0 <= j < len(units):
                            ps = await_job(act, (kind + "t", j))
                            if j == 0:
                                await_job(act, (kind + "c", 2))
                            if j >= 2:
                                act.wait_ge(pv_done, base + j - 1)
                            nc.scalar.copy(probT[j % 2], ps[:, 0:T]).then_inc(freed[PAIR_OF[(kind + "t", j)]], 1)
                        if i < len(units):
                            act.wait_ge(biased, base + i + 1)
                            if kind == "na":
                                nc.scalar.activation(probs[i % 3], probs[i % 3], ACT.Exp,
                                                     bias=negms[i % 3], accum_out=rsums[i % 3]).then_inc(exped, 1)
                            else:
                                ps = pair[PAIR_OF[(kind + "s", i)]]
                                if i >= 3:
                                    await_job(act, (kind + "t", i - 3))
                                nc.scalar.activation(probs[i % 3], ps[:, MID:MID + T], ACT.Exp,
                                                     bias=negms[i % 3], scale=scale, accum_out=rsums[i % 3])\
                                    .then_inc(freed[PAIR_OF[(kind + "s", i)]], 1)

                attention("na", 0)
                act.wait_ge(caches_out, 48)
                for t in range(KT):
                    ps = await_job(act, ("vm", t))
                    nc.scalar.copy(vm[:, t, :], ps[:, 0:512]).then_inc(freed[PAIR_OF[("vm", t)]], 1)
                for m in range(NM):
                    ps = await_job(act, ("kn", m))
                    nc.scalar.copy(kT[0:HD, 2 * m, :], ps[0:HD, KMID:KMID + KEYS])
                    nc.scalar.copy(kT[0:HD, 2 * m + 1, :], ps[HD:P, KMID:KMID + KEYS]).then_inc(freed[PAIR_OF[("kn", m)]], 1)
                attention("ml", len(units))

                for k in range(KD):
                    nc.scalar.copy(g_high[:, k, :], h_t[:, k, :]).then_inc(g_high_ready, 1)
                split_high(N_WIN)
                act.wait_ge(pv_done, 2 * len(units))
                split_high(N_WIN + 1)
                for g in range(NM):
                    ps = await_job(act, ("pool", g))
                    nc.scalar.mul(yT[0][:, g, :], ps[:, 1024 - T:1024], psc[:, g:g + 1]).then_inc(freed[PAIR_OF[("pool", g)]], 1)
                await_mod_stored(act, 1)
                for g in range(2):
                    act.dma_start(gb1[:, g, :], mod_rows[g:g + 1, 2 * D:3 * D].partition_broadcast(P)).then_inc(gb_in, 16)
                for i, (m, n) in enumerate(MERGE):
                    ps = await_job(act, ("gate", m, n))
                    if i >= 2:
                        await_read(act, ("branch", *MERGE[i - 2]))
                    nc.scalar.activation(sig[:, i % 2, :], ps[:, MID:MID + T], ACT.Sigmoid)\
                        .then_inc(freed[PAIR_OF[("gate", m, n)]], 1)
                    if i % 2 and N_WIN + 2 + i // 2 < len(HALVES):
                        split_high(N_WIN + 2 + i // 2)
                await_job(act, ("gate", KD - 1, 2))
                act.wait_ge(x_stored, L * (16 * TT) + 16)
                act.dma_start(x2, x_res.rearrange("(t p) d -> p t d", p=P)).then_inc(x2_in, 16)
                for n in (N_IN - 2, N_IN - 1):
                    await_mod_stored(act, n)
                for g in range(2):
                    act.dma_start(bc2[:, 2 * g, :], mod_rows[g:g + 1, 4 * D:5 * D].partition_broadcast(P)).then_inc(bc2_in, 16)
                    act.dma_start(bc2[:, 2 * g + 1, :], mod_rows[g:g + 1, 3 * D:4 * D].partition_broadcast(P)).then_inc(bc2_in, 16)
                def tail_transposed(t):
                    act.wait_ge(h2_ready, t + 1)
                    act.dma_start(h2_rows[t * P:(t + 1) * P, :], h2[:, t, :]).then_inc(h2_stored, 16)
                    ps = await_job(act, ("ht", t))
                    if t >= 2:
                        await_job(act, ("lg", t - 2))
                    nc.scalar.copy(h2T[:, t % 2, :], ps[:, :]).then_inc(freed[PAIR_OF[("ht", t)]], 1)

                def root(t, count):
                    act.wait_ge(ms3, count)
                    nc.scalar.activation(rs[:, t:t + 1], rs[:, t:t + 1], ACT.Sqrt).then_inc(root3, 1)

                for t in range(TT):
                    ps = await_job(act, ("y", t))
                    if t >= 2:
                        act.wait_ge(x2_new, t - 1)
                    nc.scalar.activation(yb[:, t % 2, :], ps[:, :], ACT.Square, accum_out=ss[:, t:t + 1]).then_inc(sq3, 1)
                    root(t, 2 * t + 1)
                    act.wait_ge(x2_new, t + 1)
                    if t >= 1:
                        act.wait_ge(sq3, 2 * t)
                    nc.scalar.activation(squares, x2[:, t, :], ACT.Square,
                                         accum_out=ss[:, t:t + 1]).then_inc(sq3, 1)
                    root(t, 2 * t + 2)
                    if t:
                        tail_transposed(t - 1)
                tail_transposed(TT - 1)
                await_mod_stored(act, N_IN)
                await_mod_stored(act, N_IN + 1)
                for g in range(2):
                    act.dma_start(gb2[:, g, :], mod_rows[g:g + 1, 5 * D:6 * D].partition_broadcast(P)).then_inc(gb_in, 16)
                act.wait_ge(routed_a, 1)
                nc.scalar.activation(e4, e4, ACT.Exp).then_inc(routed_b, 1)
                act.wait_ge(routed_a, 2)
                nc.scalar.activation(m2, m2, ACT.Exp).then_inc(routed_b, 1)

                act.wait_ge(rows_zeroed, 16 * (NB - spare + 1))
                act.sem_inc(sil_ready, 1)
                act.sem_inc(y_read, 3)
                for s in range(2):
                    act.sem_inc(yo_stored[s], 16)
                out_blocks = expert_out.rearrange("(b p) d -> b p d", p=P)
                act.wait_ge(blocks_ready, 1)
                n_pairs = act.value_load(pair_count[0:1], min_val=1, max_val=NB // 2)
                with act.Fori(0, n_pairs) as it:
                    for s in range(2):
                        act.wait_ge(h_filled, it * 2 + (s + 3))
                        nc.scalar.activation(sil[:, s, :], pair[1][:, s * 512:s * 512 + FF], ACT.Silu).then_inc(sil_ready, 1)
                        act.wait_ge(y_filled, it * 2 + (s + 3))
                        act.wait_ge(yo_stored[s], it * 16 + 16)
                        nc.scalar.copy(yo[:, s, :], (pair[2], opair)[s][:, :]).then_inc(y_read, 1)
                        act.wait_ge(y_read, it * 2 + (s + 4))
                        act.dma_start(out_blocks[ds(it * 2 + s, 1)].rearrange("a p d -> p (a d)"), yo[:, s, :]).then_inc(yo_stored[s], 16)

                def first_gated(t):
                    act.wait_ge(picked[t], 32)
                    nc.scalar.mul(picks[t][:, 0, :], picks[t][:, 0, :], gate1[:, t, :]).then_inc(gated, 1)

                first_gated(0)
                for t in range(TT):
                    if t + 1 < TT:
                        first_gated(t + 1)
                    act.wait_ge(mixed, t + 1)
                    nc.scalar.activation((hT, ysT)[t % 2][:, 4 * D:5 * D], picks[t][:, 0, :], ACT.Square,
                                         accum_out=ss[:, t:t + 1]).then_inc(sq3, 1)
                    root(t, 2 * TT + t + 1)
                    if t >= 2:
                        act.wait_ge(added, t - 1)
                        token_squares(t - 2)
                act.wait_ge(added, TT - 1)
                token_squares(TT - 2)
                act.wait_ge(x2_new, TT + 1)
                await_mod_stored(act, NMOD - 1)
                token_squares(TT - 1)
                act.wait_ge(root3, 3 * TT)
                act.wait_ge(x_squared, L * TT + 2 * TT)
                act.sem_inc(layer_done, 1)
                act.wait_ge(go["act"], 1)
                act.sem_clear(go["act"])

        @block.vector
        def _(dve):
            V = nc.vector
            dve.wait_ge(consts_in, 16)
            dve.wait_ge(pro_aux_in, 16)
            for i in range(4):
                dve.wait_ge(pro_filled, i + 1)
                V.scalar_tensor_tensor(out=pro_st[0:2, i, :], in0=pair[i // 2][0:2, (i % 2) * 512:(i % 2 + 1) * 512],
                                       scalar=float(i // 2), in1=pro_aux[0:2, i, 0:512],
                                       op0=ALU.add, op1=ALU.add).then_inc(pro_step, 1)
                dve.wait_ge(pro_step, i + 1)
                V.tensor_tensor(pro_st[0:2, i, :], pro_st[0:2, i, :], pro_aux[0:2, i, 512:1024], ALU.mult).then_inc(pro_rows, 1)
            dve.wait_ge(x_squared, TT)
            dve.wait_ge(pro_bc_in, 64)
            with dve.Fori(0, DEPTH) as L:
                steps = [0]

                def link(ins):
                    ins.then_inc(dve_step, 1)
                    steps[0] += 1
                    dve.wait_ge(dve_step, steps[0])

                def mod_rows_of(n):
                    ps = await_job(dve, ("mod", n))
                    dve.wait_ge(aux_in[n % 2], 16 * (n // 2 + 1))
                    if mod_before(n) is not None:
                        await_mod_stored(dve, mod_before(n))
                    one = 1.0 if MODS[n][0] // 2 in (1, 4) else 0.0
                    V.scalar_tensor_tensor(out=modst[n][0:2], in0=ps[0:2, 0:512], scalar=one, in1=aux[n][0:2, 0:512],
                                           op0=ALU.add, op1=ALU.add).then_inc(freed[PAIR_OF[("mod", n)]], 1)
                    await_read(dve, ("mod", n))
                    V.tensor_tensor(modst[n][0:2], modst[n][0:2], aux[n][0:2, 512:1024], ALU.mult).then_inc(mod_row, 1)

                def split_low(i):
                    dve.wait_ge(high_ready, i + 1)
                    w = half_source(dve, i)
                    V.tensor_tensor(w_low[i % 2], w, w_high[i % 2], ALU.subtract).then_inc(parts_ready, 1)

                V.tensor_scalar(rs[:, 0:TT], ssx[:, 0:TT], 1.0 / D, EPS, ALU.mult, ALU.add).then_inc(ms_ready, 1)
                dve.wait_ge(root_ready, 1)
                link(V.reciprocal(rstd[:, 0:TT], rs[:, 0:TT]))
                for t in range(TT):
                    rows = bc1[min(t, 1)]
                    if t >= 2:
                        await_job(dve, ("xt", t - 2))
                    link(V.scalar_tensor_tensor(out=hb[:, t % 2, :], in0=xt[:, t, :], scalar=rstd[:, t:t + 1],
                                                in1=rows[:, 0, :], op0=ALU.mult, op1=ALU.mult))
                    V.tensor_tensor(hb[:, t % 2, :], hb[:, t % 2, :], rows[:, 1, :], ALU.add).then_inc(h_ready, 1)
                dve.wait_ge(x_stored, L * (16 * TT) + 16)
                for t in range(TT - 2, TT):
                    dve.wait_ge(h_high_ready, t + 1)
                    await_read(dve, ("xt", t))
                    V.tensor_tensor(h_low[:, t, :].rearrange("p (k c) -> p k c", k=KD), h_t[:, :, t * P:(t + 1) * P],
                                    h_high[:, t, :].rearrange("p (k c) -> p k c", k=KD), ALU.subtract)\
                        .then_inc(h_parts_ready, 1)
                for i in range(4):
                    split_low(i)
                for a in range(2):
                    for t in range(TT):
                        ps = await_job(dve, ("nv", a, t))
                        V.tensor_copy(nv[:, t, a * 256:(a + 1) * 256], ps[:, 0:256]).then_inc(freed[PAIR_OF[("nv", a, t)]], 1)
                    split_low(4 + a)
                for i in range(6, N_WIN):
                    split_low(i)
                for a, b in ((0, C_AT), (C_AT + N_CTX, L_AT), (L_AT + N_LAT, PADT)):
                    V.memset(u_pad[:, :, a:b], 0.0)
                for m in range(NM):
                    ps = await_job(dve, ("u", m))
                    V.tensor_copy(u_pad[:, m, C_AT:C_AT + N_CTX], ps[:, TMID:TMID + N_CTX])
                    V.tensor_copy(u_pad[:, m, L_AT:L_AT + N_LAT], ps[:, TMID + N_CTX:TMID + T])\
                        .then_inc(freed[PAIR_OF[("u", m)]], 1)

                def low_transposed(t):
                    ps = await_job(dve, ("lowt", t))
                    tok = slice(t * P, (t + 1) * P)
                    V.tensor_tensor(cqT[:, :, tok], ps[:, 0:QL].rearrange("p (k c) -> p k c", k=QT),
                                    lown[:, 0:QT].unsqueeze(2).to_broadcast([P, QT, P]), ALU.mult)
                    V.tensor_tensor(ckvT[:, :, tok], ps[:, QL:QL + KVL].rearrange("p (k c) -> p k c", k=KVT),
                                    lown[:, QT:QT + KVT].unsqueeze(2).to_broadcast([P, KVT, P]), ALU.mult)
                    V.tensor_copy(kpeT[HD:QKD, tok], ps[HD:QKD, QL + KVL:QL + KVL + P])\
                        .then_inc(freed[PAIR_OF[("lowt", t)]], 1)

                dve.wait_ge(small_in, 80)
                for t in range(TT):
                    dve.wait_ge(low_sq, t + 1)
                    V.tensor_scalar(rs2[:, 2 * t:2 * t + 1], ss2[:, 2 * t:2 * t + 1], 1.0 / QL, EPS, ALU.mult, ALU.add)
                    V.tensor_scalar(rs2[:, 2 * t + 1:2 * t + 2], ss2[:, 2 * t + 1:2 * t + 2], 1.0 / KVL, EPS,
                                    ALU.mult, ALU.add).then_inc(low_ms, 1)
                    dve.wait_ge(low_root, t + 1)
                    link(V.reciprocal(rstd2[:, 2 * t:2 * t + 2], rs2[:, 2 * t:2 * t + 2]))
                    await_read(dve, ("low", t))
                    tm = ltm[:, t % 2, :]
                    V.tensor_scalar(tm[:, 0:QL], tm[:, 0:QL], rstd2[:, 2 * t:2 * t + 1], None, ALU.mult)
                    last = V.tensor_scalar(tm[:, QL:QL + KVL], tm[:, QL:QL + KVL], rstd2[:, 2 * t + 1:2 * t + 2],
                                           None, ALU.mult)
                    if t:
                        kp = tm[:, QL + KVL:LOW]
                        k4 = kp.rearrange("p (a j f) -> p a j f", a=2, j=2)
                        s4 = const("sin")[:, (t - 1) * RD:t * RD].rearrange("p (a j f) -> p a j f", a=2, j=2)
                        r4 = rot.rearrange("p (a j f) -> p a j f", a=2, j=2)
                        V.tensor_tensor(r4[:, :, 0, :], k4[:, :, 1, :], s4[:, :, 0, :], ALU.mult)
                        link(V.tensor_tensor(r4[:, :, 1, :], k4[:, :, 0, :], s4[:, :, 1, :], ALU.mult))
                        link(V.tensor_tensor(kp, kp, const("cos")[:, (t - 1) * RD:t * RD], ALU.mult))
                        last = V.tensor_tensor(kp, kp, rot, ALU.add)
                    last.then_inc(low_scaled, 1)
                    if t:
                        low_transposed(t - 1)
                low_transposed(TT - 1)

                units = attention_steps()

                def attention(kind, base, n_mod):
                    n = 1 if kind == "na" else 2

                    def maxima(i):
                        h, t = units[i]
                        ps = await_job(dve, (kind + "s", i))
                        if kind == "na":
                            if i >= 3:
                                await_job(dve, (kind + "t", i - 3))
                            r0 = 6 - 2 * (t - 1)
                            V.tensor_tensor_reduce(probs[i % 3][:, 0:N_LAT], ps[:, MID:MID + N_LAT],
                                                   tb[:, h, r0 * GW:r0 * GW + N_LAT], 1.0, LEAST,
                                                   ALU.add, ALU.max, mxs[i % 2][:, 0:1])
                            V.tensor_scalar(probs[i % 3][:, N_LAT:T], ps[:, MID + N_LAT:MID + T], 1.0, LEAST,
                                            ALU.mult, ALU.max, accum_out=mxs[i % 2][:, 1:2])\
                                .then_inc(freed[PAIR_OF[(kind + "s", i)]], 1)
                            await_read(dve, (kind + "s", i))
                            V.tensor_scalar(negms[i % 3], mxs[i % 2][:, 0:1], mxs[i % 2][:, 1:2], -1.0,
                                            ALU.max, ALU.mult).then_inc(biased, 1)
                        else:
                            link(V.reduce_max(mxs[i % 2][:, 0:1], ps[:, MID:MID + T], AX_X))
                            V.tensor_scalar(negms[i % 3], mxs[i % 2][:, 0:1], -QKD ** -0.5,
                                            None, ALU.mult).then_inc(biased, 1)

                    def normalise(i):
                        if kind == "na":
                            dve.wait_ge(exped, i + 1)
                        else:
                            await_read(dve, (kind + "s", i))
                        inv = rinv[:, i % 2:i % 2 + 1]
                        link(V.reciprocal(inv, rsums[i % 3]))
                        V.tensor_scalar(probs[i % 3], probs[i % 3], inv, None, ALU.mult).then_inc(scaled, 1)

                    def by_head(v):
                        return v.unsqueeze(2).to_broadcast([P, NH, P])

                    ps = await_job(dve, (kind + "c", 0))[:, :].rearrange("p (h c) -> p h c", h=NH)
                    link(V.reduce_max(c_max, ps, AX_X))
                    V.tensor_tensor(c_probs, ps, by_head(c_max), ALU.subtract).then_inc(freed[PAIR_OF[(kind + "c", 0)]], 1)
                    await_read(dve, (kind + "c", 0))
                    dve.sem_inc(c_shifted, 1)
                    dve.wait_ge(c_exped, n)
                    link(V.tensor_reduce(c_sum, c_probs, AX_X, ALU.add))
                    link(V.reciprocal(c_inv, c_sum))
                    V.tensor_tensor(c_probs, c_probs, by_head(c_inv), ALU.mult).then_inc(c_scaled, 1)
                    mod_rows_of(n_mod)
                    await_job(dve, (kind + "c", 1))
                    for i in range(len(units) + LAG_PV):
                        if i < len(units):
                            maxima(i)
                        if i == 0:
                            mod_rows_of(n_mod + 1)
                            ps = await_job(dve, (kind + "c", 2))
                            if n == 2:
                                dve.wait_ge(pooled, NM)
                            V.tensor_copy(yT[n][:, :, 0:P], ps[:, 0:NM * P].rearrange("p (m c) -> p m c", m=NM))\
                                .then_inc(freed[PAIR_OF[(kind + "c", 2)]], 1)
                        if 0 <= i - 1 < len(units):
                            normalise(i - 1)
                        if kind == "ml" and i == MOD_UNIT:
                            mod_rows_of(N_ML)
                        done = i - LAG_PV
                        if done >= 0 and done % 8 == 7:
                            m = done // 8
                            dve.wait_ge(pv_done, base + done + 1)
                            V.tensor_copy(yT[n][:, m, P:T], opair[:, m % 2 * 512:(m % 2 + 1) * 512]).then_inc(o_freed, 1)

                dve.wait_ge(bias_masked, 1)
                attention("na", 0, 0)
                for h in range(NH):
                    ps = await_job(dve, ("qm", h))
                    lat = slice(MID + N_CTX, MID + T)
                    V.tensor_copy(qT[0:QKD, h, 0:N_CTX], ps[0:QKD, MID:MID + N_CTX])
                    V.tensor_copy(qT[0:HD, h, N_CTX:T], ps[0:HD, lat])
                    V.tensor_tensor(qT[HD:QKD, h, N_CTX:T], ps[HD:QKD, lat], const("rope")[HD:QKD], ALU.mult)
                    V.tensor_tensor(swapped[HD:QKD], ps[QKD:P, lat], const("rope")[QKD:P], ALU.mult)\
                        .then_inc(freed[PAIR_OF[("qm", h)]], 1)
                    await_read(dve, ("qm", h))
                    V.tensor_tensor(qT[HD:QKD, h, N_CTX:T], qT[HD:QKD, h, N_CTX:T], swapped[HD:QKD], ALU.add)\
                        .then_inc(q_ready, 1)
                    dve.wait_ge(q_ready, h + 1)
                attention("ml", len(units), N_NA)
                for k in range(0, KD, 2):
                    dve.wait_ge(g_high_ready, k + 1)
                    V.tensor_tensor(g_low[:, k, :], h_t[:, k, :], g_high[:, k, :], ALU.subtract).then_inc(g_parts_ready, 1)
                split_low(N_WIN)
                mod_rows_of(N_ML + 1)
                await_mod_stored(dve, N_IN - 1)

                split_low(N_WIN + 1)
                dve.wait_ge(g_parts_ready, KD)
                for i, (m, n) in enumerate(MERGE):
                    ps = await_job(dve, ("branch", m, n))
                    await_read(dve, ("gate", m, n))
                    out = mergedT[:, m, :] if n == 0 else prod[:, i % 2, :]
                    V.tensor_tensor(out, ps[:, MID:MID + T], sig[:, i % 2, :], ALU.mult)\
                        .then_inc(freed[PAIR_OF[("branch", m, n)]], 1)
                    if n:
                        await_read(dve, ("branch", m, n))
                        ins = V.tensor_tensor(mergedT[:, m, :], mergedT[:, m, :], prod[:, i % 2, :], ALU.add)
                        if n == 2:
                            ins.then_inc(merged, 1)
                    if i % 2 and N_WIN + 2 + i // 2 < len(HALVES):
                        split_low(N_WIN + 2 + i // 2)

                def inverse_root(t, count):
                    dve.wait_ge(sq3, count)
                    V.tensor_scalar(rs[:, t:t + 1], ss[:, t:t + 1], 1.0 / D, EPS, ALU.mult, ALU.add).then_inc(ms3, 1)
                    dve.wait_ge(root3, count)
                    link(V.reciprocal(rstd[:, t:t + 1], rs[:, t:t + 1]))

                def logits(t):
                    ps = await_job(dve, ("lg", t))
                    V.tensor_copy(lg[:, t, :], ps[:, 0:LG]).then_inc(freed[PAIR_OF[("lg", t)]], 1)

                dve.wait_ge(gb_in, 32)
                dve.wait_ge(x2_in, 16)
                for t in range(TT):
                    g = min(t, 1)
                    inverse_root(t, 2 * t + 1)
                    V.scalar_tensor_tensor(out=yb[:, t % 2, :], in0=pair[PAIR_OF[("y", t)]][:, :], scalar=rstd[:, t:t + 1],
                                           in1=gb1[:, g, :], op0=ALU.mult, op1=ALU.mult)\
                        .then_inc(freed[PAIR_OF[("y", t)]], 1)
                    await_read(dve, ("y", t))
                    V.tensor_tensor(x2[:, t, :], x2[:, t, :], yb[:, t % 2, :], ALU.add).then_inc(x2_new, 1)
                    inverse_root(t, 2 * t + 2)
                    if t == 0:
                        dve.wait_ge(bc2_in, 64)
                    link(V.scalar_tensor_tensor(out=h2[:, t, :], in0=x2[:, t, :], scalar=rstd[:, t:t + 1],
                                                in1=bc2[:, 2 * g, :], op0=ALU.mult, op1=ALU.mult))
                    V.tensor_tensor(h2[:, t, :], h2[:, t, :], bc2[:, 2 * g + 1, :], ALU.add).then_inc(h2_ready, 1)
                    if t >= 2:
                        logits(t - 2)
                mod_rows_of(N_IN)
                logits(TT - 2)
                mod_rows_of(N_IN + 1)
                logits(TT - 1)
                await_read(dve, ("lg", TT - 1))

                def wide(v, n=EG):
                    return v.to_broadcast([P, TT, n])

                rev = const("rev").rearrange("p (t n) -> p t n", t=TT)

                def first_max(values, mark, top):
                    link(V.tensor_tensor(mark, values, wide(top), ALU.is_equal))
                    link(V.tensor_tensor(w4, mark, rev, ALU.mult))
                    link(V.reduce_max(big, w4, AX_X))
                    link(V.tensor_tensor(mark, w4, wide(big), ALU.is_equal))

                lgg = lg[:, :, 0:NG]
                link(V.reduce_max(gmax, lgg, AX_X))
                V.tensor_tensor(e4, lgg, wide(gmax), ALU.subtract).then_inc(routed_a, 1)
                first_max(lgg, oh_g, gmax)
                g16 = [P, TT, NG, EG]
                v4 = "p t (g e) -> p t g e"
                link(V.tensor_tensor(ch1.rearrange(v4, g=NG), lg[:, :, NG:LG].rearrange(v4, g=NG),
                                     oh_g.unsqueeze(3).to_broadcast(g16), ALU.mult))
                link(V.tensor_reduce(el, ch1.rearrange("p t (g e) -> p t e g", g=NG), AX_X, ALU.add))
                link(V.reduce_max(m1, el, AX_X))
                first_max(el, oh1, m1)
                link(V.scalar_tensor_tensor(out=elm, in0=oh1, scalar=NEG, in1=el, op0=ALU.mult, op1=ALU.add))
                link(V.reduce_max(m2, elm, AX_X))
                first_max(elm, oh2, m2)
                V.tensor_tensor(m2, m2, m1, ALU.subtract).then_inc(routed_a, 1)
                V.tensor_tensor(ch1.rearrange(v4, g=NG), oh_g.unsqueeze(3).to_broadcast(g16),
                                oh1.unsqueeze(2).to_broadcast(g16), ALU.mult)
                link(V.tensor_tensor(ch2.rearrange(v4, g=NG), oh_g.unsqueeze(3).to_broadcast(g16),
                                     oh2.unsqueeze(2).to_broadcast(g16), ALU.mult))
                V.tensor_tensor(chs, ch1, ch2, ALU.add).then_inc(chosen, 1)
                mod_rows_of(N_IN + 2)
                dve.wait_ge(routed_b, 2)
                V.tensor_reduce(gsum, e4, AX_X, ALU.add)
                link(V.tensor_scalar(m1, m2, 1.0, None, ALU.add))
                link(V.tensor_tensor(gsum, gsum, m1, ALU.mult))
                link(V.reciprocal(gate1, gsum))
                link(V.tensor_tensor(gate2, gate1, m2, ALU.mult))
                ps = await_job(dve, ("cnt", 0))
                pos = ps[:, 0:TT * NE].rearrange("p (t n) -> p t n", t=TT)
                tot = ps[:, 128:128 + TT * NE].rearrange("p (t n) -> p t n", t=TT)
                V.tensor_copy(slots[:, 0, :], pos[:, 0, :])
                link(V.tensor_copy(n_e, tot[:, 0, :]))
                for t in range(1, TT):
                    link(V.tensor_tensor(slots[:, t, :], pos[:, t, :], n_e, ALU.add))
                    link(V.tensor_tensor(n_e, tot[:, t, :], n_e, ALU.add))
                dve.sem_inc(freed[PAIR_OF[("cnt", 0)]], 1)
                link(V.tensor_scalar(blocks, n_e, 0.0, None, ALU.is_gt))
                for j in range(1, TT):
                    link(V.scalar_tensor_tensor(out=blocks, in0=n_e, scalar=float(j * BLOCK), in1=blocks,
                                                op0=ALU.is_gt, op1=ALU.add))
                link(V.tensor_tensor_scan(blk_end, ones[:, 0:NE], blocks, 0.0, ALU.mult, ALU.add))
                link(V.tensor_tensor(blk_start, blk_end, blocks, ALU.subtract))
                for t in range(TT):
                    last = V.scalar_tensor_tensor(out=slots[:, t, :], in0=blk_start, scalar=float(BLOCK),
                                                  in1=slots[:, t, :], op0=ALU.mult, op1=ALU.add)
                link(last)
                V.tensor_tensor(ch1, ch1, slots, ALU.mult)
                link(V.tensor_tensor(ch2, ch2, slots, ALU.mult))
                V.tensor_reduce(slot1, ch1, AX_X, ALU.add)
                link(V.tensor_reduce(slot2, ch2, AX_X, ALU.add))
                n2 = [P, 2 * TT, NB + 1]
                link(V.tensor_tensor(reached, both.to_broadcast(n2), const("first").unsqueeze(1).to_broadcast(n2), ALU.is_ge))
                link(V.tensor_reduce(place, reached, AX_X, ALU.add))
                link(V.scalar_tensor_tensor(out=place, in0=place, scalar=-float(BLOCK), in1=both, op0=ALU.mult, op1=ALU.add))
                V.tensor_tensor(at_place, place.to_broadcast([P, 2 * TT, P]),
                                const("behind").unsqueeze(1).to_broadcast([P, 2 * TT, P]), ALU.is_equal)
                link(V.tensor_tensor(in_block, reached[:, :, 0:NB], reached[:, :, 1:NB + 1], ALU.subtract))
                for k in range(2):
                    half = in_block[:, k * TT:(k + 1) * TT, :]
                    ins = V.tensor_tensor(half, half, const("tok").unsqueeze(2).to_broadcast([P, TT, NB]), ALU.mult)
                ins.then_inc(marks_ready, 1)
                V.tensor_copy(slot_ids.unsqueeze(2), both).then_inc(slots_ready, 1)
                link(V.tensor_tensor(bcmp, blk_end.unsqueeze(1).to_broadcast([P, NB, NE]),
                                     const("blk").unsqueeze(2).to_broadcast([P, NB, NE]), ALU.is_le))
                link(V.tensor_reduce(bexp, bcmp, AX_X, ALU.add))
                link(V.tensor_scalar(bexp, bexp, float(NE - 1), None, ALU.min))
                V.tensor_copy(blk_ids, bexp)
                link(V.tensor_scalar(halves, const("blk")[:, 0:NB:2], blk_end[:, NE - 1:NE], None, ALU.is_lt))
                link(V.tensor_reduce(npair_f, halves, AX_X, ALU.add))
                V.tensor_copy(pair_count, npair_f).then_inc(blocks_ready, 1)
                mod_rows_of(N_IN + 3)
                mod_rows_of(N_IN + 4)
                ps = await_job(dve, ("list", 0))
                V.tensor_copy(src_ids, ps[:, 0:NB]).then_inc(freed[PAIR_OF[("list", 0)]], 1)
                dve.sem_inc(t_filled, 2)
                dve.sem_inc(h_filled, 2)
                dve.sem_inc(y_filled, 2)
                mod_rows_of(N_IN + 5)

                dve.sem_inc(t_freed, 1)
                dve.sem_inc(hid_ready, 3)

                def transposed(b, s):
                    dve.wait_ge(t_filled, b + 3)
                    V.tensor_copy(xgT[:, s, :], pair[0][:, :]).then_inc(t_freed, 1)

                def hidden(b, s):
                    dve.wait_ge(sil_ready, b + 2)
                    V.tensor_tensor(hid[:, s, :], sil[:, s, :], pair[1][:, s * 512 + FF:s * 512 + 2 * FF], ALU.mult)\
                        .then_inc(hid_ready, 1)

                dve.wait_ge(blocks_ready, 1)
                n_pairs = dve.value_load(pair_count[0:1], min_val=2, max_val=NB // 2)
                transposed(0, 0)
                with dve.Fori(0, n_pairs - 1) as it:
                    hidden(it * 2, 0)
                    transposed(it * 2 + 1, 1)
                    hidden(it * 2 + 1, 1)
                    transposed(it * 2 + 2, 0)
                hidden(n_pairs * 2 - 2, 0)
                transposed(n_pairs * 2 - 1, 1)
                hidden(n_pairs * 2 - 1, 1)

                dve.wait_ge(gb_in, 64)
                def mix(t):
                    a, b = picks[t][:, 0, :], picks[t][:, 1, :]
                    dve.wait_ge(gated, t + 1)
                    dve.wait_ge(picked[t], 32)
                    V.scalar_tensor_tensor(out=a, in0=b, scalar=gate2[:, t, :], in1=a, op0=ALU.mult, op1=ALU.add)\
                        .then_inc(mixed, 1)

                mix(0)
                for t in range(TT):
                    a = picks[t][:, 0, :]
                    if t + 1 < TT:
                        mix(t + 1)
                    inverse_root(t, 2 * TT + t + 1)
                    V.scalar_tensor_tensor(out=a, in0=a, scalar=rstd[:, t:t + 1], in1=gb2[:, min(t, 1), :],
                                           op0=ALU.mult, op1=ALU.mult).then_inc(normed, 1)
                dve.wait_ge(normed, TT)
                V.tensor_tensor(x2[:, TT - 1, :], x2[:, TT - 1, :], a, ALU.add).then_inc(x2_new, 1)
                dve.wait_ge(x2_new, TT + 1)
                dve.sem_inc(layer_done, 1)
                dve.wait_ge(go["dve"], 1)
                dve.sem_clear(go["dve"])

        @block.gpsimd
        def _(pool):
            G = nc.gpsimd
            pool.wait_ge(consts_in, 16)
            with pool.Fori(0, DEPTH) as L:
                steps = [0]

                def link(ins):
                    ins.then_inc(pool_step, 1)
                    steps[0] += 1
                    pool.wait_ge(pool_step, steps[0])

                for t in range(TT - 2):
                    if t == 2:
                        pool.wait_ge(x_stored, L * (16 * TT) + 16)
                        pool.sem_inc(ran_on, 1)
                    pool.wait_ge(h_high_ready, t + 1)
                    await_read(pool, ("xt", t))
                    G.tensor_tensor(h_low[:, t, :].rearrange("p (k c) -> p k c", k=KD), h_t[:, :, t * P:(t + 1) * P],
                                    h_high[:, t, :].rearrange("p (k c) -> p k c", k=KD), ALU.subtract)\
                        .then_inc(h_parts_ready, 1)

                pool.wait_ge(bias_in, 32)
                tbr = r1[:, NQ_W:NQ_W + T_W].rearrange("p (r c) -> p r c", c=GW)
                G.tensor_tensor(tbr, tbr, const("mask").unsqueeze(1).to_broadcast([P, NH * DR, GW]), ALU.add)\
                    .then_inc(bias_masked, 1)

                await_read(pool, ("u", NM - 1))
                edge = const("edge").rearrange("p (g a b) -> p g a b", g=NM, a=2)
                for g, w in enumerate(POOL_W):
                    u = u_pad[:, g, :]
                    link(G.tensor_tensor(sum_a[:, 1:PADT], u[:, 0:PADT - 1], u[:, 1:PADT], ALU.add))
                    cur, nxt, lo, hi = sum_a, sum_b, 1, PADT
                    for d in (1, 2, 4)[:g]:
                        link(G.tensor_tensor(nxt[:, lo + d:hi - d], cur[:, lo:hi - 2 * d], cur[:, lo + 2 * d:hi], ALU.add))
                        cur, nxt, lo, hi = nxt, cur, lo + d, hi - d
                    link(G.tensor_scalar(nxt[:, C_AT:L_AT + N_LAT], cur[:, C_AT:L_AT + N_LAT], 1.0 / w, None, ALU.mult))
                    for i, (a, b) in enumerate(((C_AT, L_AT), (C_AT + N_CTX - 8, L_AT + N_LAT - 8))):
                        for c in (a, b):
                            ins = G.tensor_tensor(nxt[:, c:c + 8], nxt[:, c:c + 8], edge[:, g, i, :], ALU.mult)
                    link(ins)
                    G.tensor_tensor(u[:, C_AT:L_AT + N_LAT], nxt[:, C_AT:L_AT + N_LAT], u[:, C_AT:L_AT + N_LAT],
                                    ALU.subtract).then_inc(pooled, 1)
                    pool.wait_ge(pooled, g + 1)

                await_job(pool, ("vm", 0))
                await_read(pool, ("lowt", TT - 1))
                pool.wait_ge(caches_in, 64)
                for h in range(NH):
                    G.tensor_copy(kT[HD:QKD, h, :], kpeT[HD:QKD, :]).then_inc(kpe_copied, 1)

                for k in range(1, KD, 2):
                    pool.wait_ge(g_high_ready, k + 1)
                    G.tensor_tensor(g_low[:, k, :], h_t[:, k, :], g_high[:, k, :], ALU.subtract).then_inc(g_parts_ready, 1)

                await_read(pool, ("list", 0))
                pool.wait_ge(h2_stored, 16 * TT)
                pool.wait_ge(blocks_ready, 1)
                n_pairs = pool.value_load(pair_count[0:1], min_val=1, max_val=NB // 2)
                with pool.Fori(0, n_pairs) as it:
                    for s in range(2):
                        pool.wait_ge(t_filled, it * 2 + (s + 1))
                        pool.sem_inc(ran_on, 1)
                        G.tensor_copy(src_id[s], src_ids[:, ds(it * 2 + s, 1)]).then_inc(id_ready, 1)
                        pool.wait_ge(id_ready, it * 2 + (s + 1))
                        pool.sem_inc(ran_on, 1)
                        pool.indirect_dma_start(xg[:, s, :], None, h2_rows,
                                                bass.IndirectOffsetOnAxis(ap=src_id[s], axis=0)).then_inc(xg_in[s], 16)
                for s in range(2):
                    pool.wait_ge(yo_stored[s], n_pairs * 16 + 16)
                pool.sem_inc(ran_on, 1)
                for t in range(TT):
                    for k in range(2):
                        i = k * TT + t
                        pool.indirect_dma_start(picks[t][:, k, :], None, expert_out,
                                                bass.IndirectOffsetOnAxis(ap=slot_ids[:, i:i + 1], axis=0))\
                            .then_inc(picked[t], 16)
                for t in range(TT - 1):
                    pool.wait_ge(picked[t], 32)
                    pool.wait_ge(normed, t + 1)
                    G.tensor_tensor(x2[:, t, :], x2[:, t, :], picks[t][:, 0, :], ALU.add).then_inc(added, 1)
                pool.wait_ge(added, TT - 1)
                pool.wait_ge(picked[TT - 1], 32)
                pool.dma_reset()
                pool.sem_inc(layer_done, 1)
                pool.wait_ge(go["pool"], 1)
                pool.sem_clear(go["pool"])

        @block.tensor
        def _(pe):
            pe.wait_ge(cv_ready, 1)
            pe.wait_ge(consts_in, 16)
            for i in range(4):
                pe.wait_ge(pro_in[i], 16)
                for k in range(KD):
                    last = nc.tensor.matmul(pair[i // 2][0:2, (i % 2) * 512:(i % 2 + 1) * 512], cvec[:, k, :],
                                            pro_w[i][:, k, :], start=k == 0, stop=k == KD - 1)
                last.then_inc(pro_filled, 1)
            pe.wait_ge(pro_rows, 4)
            with pe.Fori(0, DEPTH) as L:
                def chunk(key, k, n):
                    pe.wait_ge(landed[SLOT_OF[key]], 16 * FILL_OF[key])
                    return view(ring, SLOT_OF[key] * SLOT, k * n, k=k)

                def mm(out, lhsT, rhs, first, last):
                    return nc.tensor.matmul(out, lhsT, rhs, start=first, stop=last, skip_group_check=True)

                def channels(key, w, c0, kt, rhs, width, at_):
                    ps = pair_for(pe, key)
                    half = width // 2
                    for j in range(2):
                        for k in range(kt):
                            last = mm(ps[:, at_ + j * half:at_ + (j + 1) * half], w[:, k, c0:c0 + P],
                                      rhs[:, k, j * half:(j + 1) * half], k == 0, k == kt - 1)
                    last.then_inc(filled[PAIR_OF[key]], 1)

                def three_products(out, w_parts, x_parts, first, last):
                    for j, (a, b) in enumerate(((0, 0), (0, 1), (1, 0))):
                        ins = mm(out, w_parts[a], x_parts[b], first and j == 0, last and j == 2)
                    return ins

                by_tile = [(TMID + 128 * a, 128 * (b - a), lambda k, a=a, b=b: [x[:, a:b, k * P:(k + 1) * P] for x in (h_high, h_low)])
                           for a, b in ((0, 2), (2, TT))]
                by_channel = [(MID + a, T // 2, lambda k, a=a: [x[:, k, a:a + T // 2] for x in (g_high, g_low)])
                              for a in (0, T // 2)]

                def channels_split(key, i, c0, pieces):
                    pe.wait_ge(parts_ready, i + 1)
                    ps = pair_for(pe, key)
                    for a, n, parts_at in pieces:
                        for k in range(KD):
                            w = [x[i % 2][:, k, c0:c0 + P] for x in (w_high, w_low)]
                            last = three_products(ps[:, a:a + n], w, parts_at(k), k == 0, k == KD - 1)
                    last.then_inc(filled[PAIR_OF[key]], 1)

                def tokens(key, parts, kt, lhs, t):
                    ps = pair_for(pe, key)
                    for w, a, n in parts:
                        for k in range(kt):
                            last = mm(ps[:, a:a + n], lhs[:, k, t * P:(t + 1) * P], w[:, k, :], k == 0, k == kt - 1)
                    last.then_inc(filled[PAIR_OF[key]], 1)

                def turned(key, pieces):
                    ps = pair_for(pe, key)
                    for s, a in pieces:
                        last = nc.tensor.transpose(ps[0:s.shape[1], a:a + P], s, ident)
                    last.then_inc(filled[PAIR_OF[key]], 1)

                def modulate(n):
                    w = chunk(("mod", n), KD, 512)
                    ps = pair_for(pe, ("mod", n))
                    for k in range(KD):
                        last = mm(ps[0:2, 0:512], cvec[:, k, :], w[:, k, :], k == 0, k == KD - 1)
                    last.then_inc(filled[PAIR_OF[("mod", n)]], 1)

                for t in range(TT):
                    pe.wait_ge(h_ready, t + 1)
                    turned(("xt", t), [(hb[:, t % 2, k * P:(k + 1) * P], k * P) for k in range(KD)])
                pe.wait_ge(h_parts_ready, TT)
                for m in range(NM):
                    channels_split(("nk", m), m // 2, m % 2 * P, by_tile)
                for a in range(2):
                    pe.wait_ge(parts_ready, 3 + a)
                    for t in range(TT):
                        ps = pair_for(pe, ("nv", a, t))
                        for k in range(KD):
                            last = three_products(ps[:, 0:256], [x[:, t, k * P:(k + 1) * P] for x in (h_high, h_low)],
                                                  [x[a][:, k, :] for x in (w_high, w_low)], k == 0, k == KD - 1)
                        last.then_inc(filled[PAIR_OF[("nv", a, t)]], 1)
                for m in range(NM):
                    channels_split(("nq", m), 4 + m // 2, m % 2 * P, by_tile)
                for m in range(NM):
                    channels_split(("u", m), 6 + m // 2, m % 2 * P, by_tile)
                await_read(pe, ("xt", TT - 1))
                wa, wb = chunk(("low", 0), KD, LOW // 2), chunk(("low", 1), KD, LOW // 2)

                def low_transposes(t):
                    pe.wait_ge(low_scaled, t + 1)
                    tm = ltm[:, t % 2, :]
                    pieces = [(tm[:, k * P:(k + 1) * P], k * P) for k in range(QT + KVT)]
                    pieces.append((tm[:, QL + KVL - HD:LOW], QL + KVL))
                    turned(("lowt", t), pieces)

                for t in range(TT):
                    tokens(("low", t), [(wa, LMID, LOW // 2), (wb, 512, LOW // 2)], KD, h_t, t)
                    if t:
                        low_transposes(t - 1)
                low_transposes(TT - 1)

                units = attention_steps()

                def attention(kind, base, n_mod):
                    v = nv if kind == "na" else vm

                    def operands(h, queries):
                        if kind == "na":
                            m, p0 = h // 2, HD * (h % 2)
                            return nqT[p0:p0 + HD, m, queries], nkT[p0:p0 + HD, m, :]
                        return qT[0:QKD, h, queries], kT[0:QKD, h, :]

                    def scores(i):
                        h, t = units[i]
                        ps = pair_for(pe, (kind + "s", i))
                        q, k = operands(h, slice(t * P, (t + 1) * P))
                        for j in range(2):
                            last = mm(ps[:, MID + j * (T // 2):MID + (j + 1) * (T // 2)], q,
                                      k[:, P + j * (T // 2):P + (j + 1) * (T // 2)], True, True)
                        last.then_inc(filled[PAIR_OF[(kind + "s", i)]], 1)

                    def transposes(i):
                        pe.wait_ge(scaled, base + i + 1)
                        turned((kind + "t", i), [(probs[i % 3][:, j * P:(j + 1) * P], j * P) for j in range(TT)])

                    def values(i):
                        h, t = units[i]
                        await_read(pe, (kind + "t", i))
                        p0, m = HD * (h % 2), base // 8 + h // 2
                        if i % 8 == 0 and m >= 2:
                            pe.wait_ge(o_freed, m - 1)
                        for j in range(TT):
                            last = mm(opair[p0:p0 + HD, m % 2 * 512 + (t - 1) * P:m % 2 * 512 + t * P],
                                      v[:, j + 1, h * HD:(h + 1) * HD], probT[i % 2][:, j * P:(j + 1) * P], j == 0, j == TT - 1)
                        last.then_inc(pv_done, 1)

                    def c_at(h):
                        return h % 2 * NM + h // 2

                    ps = pair_for(pe, (kind + "c", 0))
                    for h in range(NH):
                        q, k = operands(h, slice(0, P))
                        last = mm(ps[:, c_at(h) * P:(c_at(h) + 1) * P], q, k[:, 0:P], True, True)
                    last.then_inc(filled[PAIR_OF[(kind + "c", 0)]], 1)
                    modulate(n_mod)
                    pe.wait_ge(c_scaled, 1 + base // len(units))
                    turned((kind + "c", 1), [(c_probs[:, h, :], h * P) for h in range(NH)])
                    scores(0)
                    modulate(n_mod + 1)
                    await_read(pe, (kind + "c", 1))
                    ps = pair_for(pe, (kind + "c", 2))
                    for h in range(NH):
                        p0, m = HD * (h % 2), h // 2
                        last = mm(ps[p0:p0 + HD, m * P:(m + 1) * P], v[:, 0, h * HD:(h + 1) * HD],
                                  c_probT[:, c_at(h), :], True, True)
                    last.then_inc(filled[PAIR_OF[(kind + "c", 2)]], 1)
                    for i in range(len(units) + LAG_PV):
                        if 0 < i < len(units):
                            scores(i)
                        if kind == "ml" and i == MOD_UNIT:
                            modulate(N_ML)
                        if 0 <= i - LAG_PT < len(units):
                            transposes(i - LAG_PT)
                        if 0 <= i - LAG_PV < len(units):
                            values(i - LAG_PV)

                pe.wait_ge(caches_in, 64)
                await_read(pe, ("u", NM - 1))
                attention("na", 0, 0)
                await_read(pe, ("lowt", TT - 1))
                w = chunk(("ukv",), KVT, 1024)
                for t in range(KT):
                    tokens(("vm", t), [(w[:, :, 512:1024], 0, 512)], KVT, ckvT, t)
                for m in range(NM):
                    channels(("kn", m), w, m * P, KVT, ckvT, KEYS, KMID)
                w = chunk(("uq",), QT, 1024)
                for h in range(NH):
                    channels(("qm", h), w, h * P, QT, cqT, T, MID)
                await_read(pe, ("kn", NM - 1))
                pe.wait_ge(q_ready, NH)
                pe.wait_ge(kpe_copied, NH)
                attention("ml", len(units), N_NA)
                modulate(N_ML + 1)

                pe.wait_ge(small_in, 80)
                pe.wait_ge(pooled, NM)
                for g in range(NM):
                    ps = pair_for(pe, ("pool", g))
                    wg = wpool_sb[:, g * P:(g + 1) * P]
                    mm(ps[:, 1024 - T:512], wg, u_pad[:, g, C_AT:C_AT + N_CTX], True, True)
                    mm(ps[:, 512:1024], wg, u_pad[:, g, L_AT:L_AT + N_LAT], True, True)\
                        .then_inc(filled[PAIR_OF[("pool", g)]], 1)
                for m, n in MERGE:
                    if m % 4 == 0:
                        wb = chunk(("branch", m // 4, n), NM, 512)
                    if n == 0 and m == 0:
                        pe.wait_ge(g_parts_ready, KD)
                    channels_split(("gate", m, n), HALF_OF[(("gate", m // 4, n), m % 4 // 2)], m % 2 * P, by_channel)
                    if n == 0 and m == 0:
                        await_read(pe, ("pool", NM - 1))
                    if n == 2 and m == 0:
                        pe.wait_ge(o_freed, 2 * NM)
                    channels(("branch", m, n), wb, (m % 4) * P, NM, yT[n], T, MID)
                pe.wait_ge(merged, KD)
                wa, wb = chunk(("out", 0), KD, 512), chunk(("out", 1), KD, 512)
                def out_tile(t):
                    tokens(("y", t), [(wa, 0, 512), (wb, 512, 512)], KD, mergedT, t)

                def tail_turn(t):
                    pe.wait_ge(h2_ready, t + 1)
                    turned(("ht", t), [(h2[:, t, k * P:(k + 1) * P], k * P) for k in range(KD)])

                def tail_logits(t):
                    await_read(pe, ("ht", t))
                    ps = pair_for(pe, ("lg", t))
                    for k in range(KD):
                        last = mm(ps[:, 0:LG], h2T[:, t % 2, k * P:(k + 1) * P], router_sb[:, k * LG:(k + 1) * LG],
                                  k == 0, k == KD - 1)
                    last.then_inc(filled[PAIR_OF[("lg", t)]], 1)

                def count_chosen(_):
                    pe.wait_ge(chosen, 1)
                    ps = pair_for(pe, ("cnt", 0))
                    cf = chs.rearrange("p t n -> p (t n)")
                    mm(ps[:, 0:TT * NE], tri, cf, True, True)
                    mm(ps[:, 128:128 + TT * NE], ones, cf, True, True).then_inc(filled[PAIR_OF[("cnt", 0)]], 1)

                def list_tokens(_):
                    pe.wait_ge(marks_ready, 1)
                    ps = pair_for(pe, ("list", 0))
                    for i in range(2 * TT):
                        last = mm(ps[:, 0:NB], at_place[:, i, :], in_block[:, i, :], i == 0, i == 2 * TT - 1)
                    last.then_inc(filled[PAIR_OF[("list", 0)]], 1)

                steps_of = {"list": list_tokens, "y": out_tile, "ht": tail_turn, "lg": tail_logits, "mod": modulate, "cnt": count_chosen}
                for kind, n in TAIL:
                    steps_of[kind](n)

                for n in range(NMOD - 3, NMOD):
                    if ("mod", n) in PAIR_OF:
                        await_read(pe, ("mod", n))
                pe.wait_ge(slots_ready, 1)
                pe.wait_ge(blocks_ready, 1)
                n_pairs = pe.value_load(pair_count[0:1], min_val=2, max_val=NB // 2)

                def gathered(b, s, rnd):
                    pe.wait_ge(xg_in[s], rnd * 16 + 16)
                    pe.wait_ge(t_freed, b + 1)
                    for k in range(KD):
                        last = nc.tensor.transpose(pair[0][:, k * P:(k + 1) * P], xg[:, s, k * P:(k + 1) * P], ident)
                    last.then_inc(t_filled, 1)

                def up(b, s, rnd):
                    pe.wait_ge(up_in[s], rnd * 32 + 32)
                    pe.wait_ge(t_freed, b + 2)
                    pe.wait_ge(hid_ready, b + 2)
                    for j in range(2 * FT):
                        w = w13[s][:, (j // FT) * 2048:(j // FT + 1) * 2048].rearrange("p (k f) -> p k f", k=KD)
                        for k in range(KD):
                            last = mm(pair[1][:, s * 512 + j * P:s * 512 + (j + 1) * P],
                                      w[:, k, (j % FT) * P:(j % FT + 1) * P], xgT[:, s, k * P:(k + 1) * P],
                                      k == 0, k == KD - 1)
                    last.then_inc(h_filled, 1)

                def down(b, s, rnd):
                    pe.wait_ge(down_in[s], rnd * 16 + 16)
                    pe.wait_ge(hid_ready, b + 4)
                    pe.wait_ge(y_read, b + 2)
                    out = (pair[2], opair)[s]
                    for j in range(2):
                        for k in range(FT):
                            last = mm(out[:, j * 512:(j + 1) * 512], hid[:, s, k * P:(k + 1) * P],
                                      w2s[s][:, k * D + j * 512:k * D + (j + 1) * 512], k == 0, k == FT - 1)
                    last.then_inc(y_filled, 1)

                gathered(0, 0, 0)
                with pe.Fori(0, n_pairs - 1) as it:
                    up(it * 2, 0, it)
                    gathered(it * 2 + 1, 1, it)
                    down(it * 2, 0, it)
                    up(it * 2 + 1, 1, it)
                    gathered(it * 2 + 2, 0, it + 1)
                    down(it * 2 + 1, 1, it)
                rnd = n_pairs - 1
                up(n_pairs * 2 - 2, 0, rnd)
                gathered(n_pairs * 2 - 1, 1, rnd)
                down(n_pairs * 2 - 2, 0, rnd)
                up(n_pairs * 2 - 1, 1, rnd)
                down(n_pairs * 2 - 1, 1, rnd)
                pe.wait_ge(y_filled, n_pairs * 2 + 2)
                pe.sem_inc(layer_done, 1)
                pe.wait_ge(go["pe"], 1)
                pe.sem_clear(go["pe"])


def kernel(**inputs):
    import numpy as np
    import concourse.bacc as bacc
    from concourse import mybir as mb
    from concourse.bass_utils import run_bass_kernel_spmd

    a = {k: np.asarray(v) for k, v in inputs.items()}
    f = np.float32
    ar = {}
    ar["x0"] = np.concatenate([a["x_prompt"][0], a["x_sample"][0]])
    ar["k_cache_t"] = a["cache_na_k"][0].reshape(DEPTH, N_CACHE, NH * HD).transpose(0, 2, 1)
    ar["v_cache"] = a["cache_na_v"][0].reshape(DEPTH, N_CACHE, NH * HD)
    ar["ckv_cache_t"] = a["cache_mla_ckv"][0].transpose(0, 2, 1)
    ar["kpe_cache_t"] = a["cache_mla_kpe"][0].transpose(0, 2, 1)
    ar["c_t"] = np.stack([a["c_ctx"], a["c"][0]]).reshape(2, KD, P).transpose(2, 1, 0).reshape(P, 2 * KD)
    ones = np.ones((DEPTH, D), f)
    gains = np.stack([ones, a["g_pre_mix"], a["g_post_mix"], ones, a["g_pre_ffn"], a["g_post_ffn"]], 1)
    aux = np.stack([a["b_mod"].reshape(DEPTH, NMOD, 512), gains.reshape(DEPTH, NMOD, 512)], 2).reshape(DEPTH, NMOD, 1, 1024)
    ar["mod_aux"] = np.concatenate([aux, aux], 2)
    ar["w_mod"], ar["w_in"], ar["w_pool"] = a["w_mod"], a["w_in"], a["w_pool"]
    ar["pool_scale"] = a["pool_scale"].reshape(DEPTH, NM, P).transpose(0, 2, 1)
    pad = GW - WIN
    wide = np.concatenate([np.zeros((DEPTH, NH, 15, pad), f), a["na_rpb"], np.zeros((DEPTH, NH, 15, pad), f)], -1)
    rows = np.stack([wide[..., GW - 1 - q:2 * GW - 1 - q] for q in range(GW)], 1)
    ar["rpb_rows"] = rows
    ar["q_norm"] = a["mla_q_norm"].reshape(DEPTH, QT, P).transpose(0, 2, 1)
    ar["kv_norm"] = a["mla_kv_norm"].reshape(DEPTH, KVT, P).transpose(0, 2, 1)
    uq = a["mla_w_uq"].reshape(DEPTH, QL, NH, QKD)
    rope = uq[..., HD:].reshape(DEPTH, QL, NH, 2, 2, RD // 4)
    ar["w_uq"] = np.concatenate([uq, rope[..., ::-1, :].reshape(DEPTH, QL, NH, RD)], -1).reshape(DEPTH, QL, NH * P)
    ukv = a["mla_w_ukv"].reshape(DEPTH, KVL, NH, 2, HD)
    ar["w_ukv"] = ukv.transpose(0, 1, 3, 2, 4).reshape(DEPTH, KVL, 2 * NH * HD)
    ar["w_branch"], ar["w_out"] = a["w_branch"], a["w_out"]
    ar["w_router"] = np.concatenate([a["w_group_router"], a["w_expert_router"]], -1)
    ar["w_gate"] = a["w_exp_gate"].reshape(DEPTH * NE, D, FF)
    ar["w_up"] = a["w_exp_up"].reshape(DEPTH * NE, D, FF)
    ar["w_down"] = a["w_exp_down"].reshape(DEPTH * NE, FF, D)

    p = np.arange(P)
    c0 = np.clip(np.arange(GW) - WIN // 2, 0, GW - WIN)
    kc = np.arange(GW)
    mask = np.where((kc[None] >= c0[:, None]) & (kc[None] < c0[:, None] + WIN), 0.0, NEG)
    nf = RD // 4
    inv = 10000.0 ** (-np.arange(nf, dtype=f) / nf)
    tok = np.arange(N_LAT)
    ang = np.stack([(tok // GW)[:, None] * inv, (tok % GW)[:, None] * inv], 1).astype(f)
    cos = np.stack([np.cos(ang)] * 2, 2).reshape(N_LAT, RD)
    sin = np.stack([-np.sin(ang), np.sin(ang)], 2).reshape(N_LAT, RD)
    ropes = np.zeros((P, N_LAT))
    ropes[HD:QKD], ropes[QKD:P] = cos.T, sin.T
    tiled = {
        "ident": np.eye(P), "tri": p[:, None] < p[None], "ones": np.ones((P, P)), "mask": np.concatenate([mask, mask]),
        "rope": ropes,
        "cos": cos.reshape(4, P, RD).transpose(1, 0, 2).reshape(P, 4 * RD),
        "sin": sin.reshape(4, P, RD).transpose(1, 0, 2).reshape(P, 4 * RD),
        "rev": np.tile(np.arange(EG, 0, -1), (P, TT)),
        "tok": np.arange(TT)[None] * P + p[:, None], "blk": np.tile(np.arange(NB), (P, 1)),
        "first": np.tile(np.arange(NB + 1) * BLOCK, (P, 1)), "behind": np.tile(np.arange(P) - BLOCK, (P, 1)),
    }
    n = 64
    t = np.concatenate([np.arange(8), np.arange(n - 8, n)])
    tiled["edge"] = np.tile(np.concatenate([w / (np.clip(t + w - w // 2, 0, n) - np.clip(t - w // 2, 0, n)) for w in POOL_W]), (P, 1))
    ar["consts"] = np.concatenate([tiled[n].astype(f) for n, _ in CONST_COLS], 1)

    ar["zeros"] = np.zeros((BLOCK, D), f)

    outs = {"x_res": (T, D), "o_nk_t": (DEPTH, NH * HD, N_CTX), "o_nv": (DEPTH, N_CTX, NH * HD),
            "o_ckv_t": (DEPTH, KVL, N_CTX), "o_kpe": (DEPTH, N_CTX, RD)}
    nc = bacc.Bacc("TRN2", target_bir_lowering=False, num_devices=1)
    arrays, args = {}, {}
    for name, v in ar.items():
        v = np.ascontiguousarray(v)
        arrays["in_" + name] = v
        args[name] = nc.dram_tensor("in_" + name, v.shape, mb.dt.from_np(v.dtype), kind="ExternalInput").ap()
    for name, shape in outs.items():
        args[name] = nc.dram_tensor("out_" + name, shape, mb.dt.float32, kind="ExternalOutput").ap()
    bass_hybrid_step(nc, **args)
    r = run_bass_kernel_spmd(nc, [arrays], core_ids=[0]).results[0]
    x = r["out_x_res"]
    return (x[None, :N_CTX], x[None, N_CTX:],
            r["out_o_nk_t"].transpose(0, 2, 1).reshape(1, DEPTH, N_CTX, NH, HD),
            r["out_o_nv"].reshape(1, DEPTH, N_CTX, NH, HD),
            r["out_o_ckv_t"].transpose(0, 2, 1)[None], r["out_o_kpe"][None])
```
